# Optimizing a Trainium2 kernel written in Bass

```python
import jax, jax.numpy as jnp
from jax import lax
import numpy as np

D_MODEL = 1024
BATCH = 1
SEQ = 256
DEPTH = 2
DEC_BATCH = 8
DEC_SEQ = 1
PAST_LEN = 1024
PAGE_SIZE = 128

N_A_LAYERS = DEPTH // 2
N_B_LAYERS = DEPTH - N_A_LAYERS
CHUNK = 128
GATE_WIDTH = 2 * D_MODEL
N_GATE_GROUPS = 8
GROUP_WIDTH = GATE_WIDTH // N_GATE_GROUPS
HEAD_DIM = 128
N_HEADS = D_MODEL // HEAD_DIM
ROT_DIM = HEAD_DIM // 4
ROPE_THETA = 500000.0
MOBA_BLOCK = 256
MOBA_TOPK = 3
Q_BLOCK = 64
N_EXPERT_GROUPS = 4
EXPERTS_PER_GROUP = 4
N_EXPERTS = N_EXPERT_GROUPS * EXPERTS_PER_GROUP
EXPERT_TOPK = 2
EXPERT_FF = D_MODEL // 2
EPS = 1e-6

kernel_name = 'hybrid_gmlp_moba_hmoe_step'

def rms_norm(x, g):
    xf = x.astype(jnp.float32)
    y = xf * lax.rsqrt(jnp.mean(xf * xf, axis=-1, keepdims=True) + EPS)
    return (y * g.astype(jnp.float32)).astype(x.dtype)

def layer_norm(x, g, b):
    xf = x.astype(jnp.float32)
    xc = xf - jnp.mean(xf, axis=-1, keepdims=True)
    y = xc * lax.rsqrt(jnp.mean(xc * xc, axis=-1, keepdims=True) + EPS)
    return (y * g.astype(jnp.float32) + b.astype(jnp.float32)).astype(x.dtype)

def partial_rope(x, pos):
    half = ROT_DIM // 2
    inv_freq = ROPE_THETA ** (-jnp.arange(half, dtype=jnp.float32) / half)
    ang = pos.astype(jnp.float32)[:, None] * inv_freq[None, :]
    cos = jnp.cos(ang)[None, :, None, :]
    sin = jnp.sin(ang)[None, :, None, :]
    xr = x[..., :ROT_DIM].astype(jnp.float32)
    x1, x2 = xr[..., :half], xr[..., half:]
    rot = jnp.concatenate([x1 * cos - x2 * sin, x2 * cos + x1 * sin], axis=-1)
    return jnp.concatenate([rot.astype(x.dtype), x[..., ROT_DIM:]], axis=-1)

def chunk_gmlp(x, norm_g, w_in, ln_g, ln_b, w_s, b_s, w_out):
    bsz, t_len, _ = x.shape
    z = jax.nn.gelu(rms_norm(x, norm_g) @ w_in)
    u, v = z[..., :GATE_WIDTH], z[..., GATE_WIDTH:]
    v = layer_norm(v, ln_g, ln_b)
    n_chunks = -(-t_len // CHUNK)
    vp = jnp.pad(v, ((0, 0), (0, n_chunks * CHUNK - t_len), (0, 0)))
    vp = vp.reshape(bsz, n_chunks, CHUNK, N_GATE_GROUPS, GROUP_WIDTH)
    causal = jnp.tril(jnp.ones((CHUNK, CHUNK), dtype=bool))
    ws = jnp.where(causal[None], w_s, jnp.zeros((), w_s.dtype))
    mixed = jnp.einsum('gts,bnsgc->bntgc', ws, vp) + b_s.T[None, None, :, :, None]
    mixed = mixed.reshape(bsz, n_chunks * CHUNK, GATE_WIDTH)[:, :t_len]
    return (u * mixed) @ w_out, v

def hier_moe(x, norm_g, w_rg, b_rg, w_re, b_re, w_gate, w_up, w_down):
    h = rms_norm(x, norm_g)
    lg = (h @ w_rg + b_rg).astype(jnp.float32)
    g_sel = jnp.argmax(lg, axis=-1)
    p_grp = jnp.max(jax.nn.softmax(lg, axis=-1), axis=-1)
    le = (h @ w_re + b_re).astype(jnp.float32)
    le = le.reshape(le.shape[:-1] + (N_EXPERT_GROUPS, EXPERTS_PER_GROUP))
    idx = jnp.broadcast_to(g_sel[..., None, None], le.shape[:-2] + (1, EXPERTS_PER_GROUP))
    le_g = jnp.take_along_axis(le, idx, axis=-2)[..., 0, :]
    top_v, top_i = lax.top_k(le_g, EXPERT_TOPK)
    w_top = jax.nn.softmax(top_v, axis=-1) * p_grp[..., None]
    e_ids = g_sel[..., None] * EXPERTS_PER_GROUP + top_i
    gates = jnp.sum(jax.nn.one_hot(e_ids, N_EXPERTS, dtype=jnp.float32) * w_top[..., None], axis=-2).astype(x.dtype)
    y = jnp.zeros_like(x)
    for e in range(N_EXPERTS):
        he = jax.nn.silu(h @ w_gate[e]) * (h @ w_up[e])
        y = y + gates[..., e:e + 1] * (he @ w_down[e])
    return y

def shared_kv(x, pos, norm_g, w_kv, k_g):
    bsz, t_len, _ = x.shape
    kv = rms_norm(x, norm_g) @ w_kv
    hd = N_HEADS * HEAD_DIM
    k = kv[..., :hd].reshape(bsz, t_len, N_HEADS, HEAD_DIM)
    v = kv[..., hd:].reshape(bsz, t_len, N_HEADS, HEAD_DIM)
    return partial_rope(rms_norm(k, k_g), pos), v

def moba_attend(q, q_start, k_all, v_all):
    bsz, t_q = q.shape[:2]
    l_kv = k_all.shape[1]
    n_blk = -(-l_kv // MOBA_BLOCK)
    k_sel_n = min(MOBA_TOPK, n_blk)
    kpad = n_blk * MOBA_BLOCK - l_kv
    kb = jnp.pad(k_all, ((0, 0), (0, kpad), (0, 0), (0, 0))).reshape(bsz, n_blk, MOBA_BLOCK, N_HEADS, HEAD_DIM)
    vb = jnp.pad(v_all, ((0, 0), (0, kpad), (0, 0), (0, 0))).reshape(bsz, n_blk, MOBA_BLOCK, N_HEADS, HEAD_DIM)
    k_mean = jnp.mean(kb.astype(jnp.float32), axis=2)
    qb = min(Q_BLOCK, t_q)
    n_qb = -(-t_q // qb)
    qq = jnp.pad(q, ((0, 0), (0, n_qb * qb - t_q), (0, 0), (0, 0))).reshape(bsz, n_qb, qb, N_HEADS, HEAD_DIM)
    scale = HEAD_DIM ** -0.5
    n_sel = k_sel_n * MOBA_BLOCK
    blk_ids = jnp.arange(n_blk)
    slot_ids = jnp.arange(k_sel_n)
    head_ids = jnp.arange(N_HEADS)[:, None, None]
    own_offsets = jnp.arange(MOBA_BLOCK)

    def one_sequence(seq_args):
        q_s, kb_s, vb_s, km_s = seq_args

        def one_query_block(blk_args):
            qi, q_blk = blk_args
            start = q_start + qi * qb
            q_pos = start + jnp.arange(qb)
            cur = start // MOBA_BLOCK
            qh = q_blk.transpose(1, 0, 2)
            gate = jnp.einsum('hqd,nhd->hqn', qh.astype(jnp.float32), km_s)
            gate = jnp.where(blk_ids < cur, gate, -jnp.inf)
            _, sel = lax.top_k(gate, k_sel_n)
            k_g = kb_s[sel, :, head_ids]
            v_g = vb_s[sel, :, head_ids]
            s_sel = jnp.einsum('hqd,hqjkd->hqjk', qh, k_g, preferred_element_type=jnp.float32) * scale
            s_sel = jnp.where((slot_ids < cur)[None, None, :, None], s_sel, -jnp.inf)
            k_own = lax.dynamic_index_in_dim(kb_s, cur, axis=0, keepdims=False)
            v_own = lax.dynamic_index_in_dim(vb_s, cur, axis=0, keepdims=False)
            s_own = jnp.einsum('hqd,khd->hqk', qh, k_own, preferred_element_type=jnp.float32) * scale
            k_pos = cur * MOBA_BLOCK + own_offsets
            s_own = jnp.where(k_pos[None, None, :] <= q_pos[None, :, None], s_own, -jnp.inf)
            logits = jnp.concatenate([s_sel.reshape(N_HEADS, qb, n_sel), s_own], axis=-1)
            p = jax.nn.softmax(logits, axis=-1).astype(v_g.dtype)
            o = (jnp.einsum('hqjk,hqjkd->hqd', p[..., :n_sel].reshape(N_HEADS, qb, k_sel_n, MOBA_BLOCK), v_g)
                 + jnp.einsum('hqk,khd->hqd', p[..., n_sel:], v_own))
            return o.transpose(1, 0, 2)

        return lax.map(one_query_block, (jnp.arange(n_qb, dtype=jnp.int32), q_s))

    out = lax.map(one_sequence, (qq, kb, vb, k_mean))
    return out.reshape(bsz, n_qb * qb, N_HEADS, HEAD_DIM)[:, :t_q]

def moba_mixer(x, pos0, k_all, v_all, norm_g, w_q, q_g, w_o):
    bsz, t_len, _ = x.shape
    q = (rms_norm(x, norm_g) @ w_q).reshape(bsz, t_len, N_HEADS, HEAD_DIM)
    q = partial_rope(rms_norm(q, q_g), pos0 + jnp.arange(t_len, dtype=jnp.int32))
    o = moba_attend(q, pos0, k_all, v_all)
    return o.reshape(bsz, t_len, N_HEADS * HEAD_DIM) @ w_o

def gather_pages(pool, page_table):
    rows = pool[page_table]
    return rows.reshape((page_table.shape[0], -1) + pool.shape[2:])

def setup_inputs(seed: int = 0) -> dict:
    key = jax.random.key(seed)
    ks = jax.random.split(key, 32)
    n_pages = PAST_LEN // PAGE_SIZE
    n_used = DEC_BATCH * n_pages
    n_pool = n_used + -(-n_used // 4)
    hd = N_HEADS * HEAD_DIM

    def nrm(k, shape, scale):
        return jax.random.normal(k, shape, jnp.float32) * scale

    def gain(k, shape):
        return 1.0 + 0.02 * jax.random.normal(k, shape, jnp.float32)

    page_table = jax.random.permutation(ks[0], n_pool)[:n_used].reshape(DEC_BATCH, n_pages).astype(jnp.int32)
    return {
        'x_prompt': nrm(ks[1], (BATCH, SEQ, D_MODEL), 1.0),
        'x_sample': nrm(ks[2], (DEC_BATCH, DEC_SEQ, D_MODEL), 1.0),
        'cache_k': nrm(ks[3], (n_pool, PAGE_SIZE, N_HEADS, HEAD_DIM), 1.0),
        'cache_v': nrm(ks[4], (n_pool, PAGE_SIZE, N_HEADS, HEAD_DIM), 1.0),
        'page_table': page_table,
        'a_norm_g': gain(ks[5], (N_A_LAYERS, D_MODEL)),
        'a_w_in': nrm(ks[6], (N_A_LAYERS, D_MODEL, 2 * GATE_WIDTH), D_MODEL ** -0.5),
        'a_ln_g': gain(ks[7], (N_A_LAYERS, GATE_WIDTH)),
        'a_ln_b': nrm(ks[8], (N_A_LAYERS, GATE_WIDTH), 0.02),
        'a_w_s': nrm(ks[9], (N_A_LAYERS, N_GATE_GROUPS, CHUNK, CHUNK), CHUNK ** -0.5),
        'a_b_s': gain(ks[10], (N_A_LAYERS, N_GATE_GROUPS, CHUNK)),
        'a_w_out': nrm(ks[11], (N_A_LAYERS, GATE_WIDTH, D_MODEL), GATE_WIDTH ** -0.5),
        'kv_norm_g': gain(ks[12], (D_MODEL,)),
        'w_kv': nrm(ks[13], (D_MODEL, 2 * hd), D_MODEL ** -0.5),
        'k_norm_g': gain(ks[14], (HEAD_DIM,)),
        'b_norm_g': gain(ks[15], (N_B_LAYERS, D_MODEL)),
        'b_w_q': nrm(ks[16], (N_B_LAYERS, D_MODEL, hd), D_MODEL ** -0.5),
        'q_norm_g': gain(ks[17], (N_B_LAYERS, HEAD_DIM)),
        'b_w_o': nrm(ks[18], (N_B_LAYERS, hd, D_MODEL), hd ** -0.5),
        'moe_norm_g': gain(ks[19], (DEPTH, D_MODEL)),
        'moe_w_rg': nrm(ks[20], (DEPTH, D_MODEL, N_EXPERT_GROUPS), D_MODEL ** -0.5),
        'moe_b_rg': nrm(ks[21], (DEPTH, N_EXPERT_GROUPS), 0.01),
        'moe_w_re': nrm(ks[22], (DEPTH, D_MODEL, N_EXPERTS), D_MODEL ** -0.5),
        'moe_b_re': nrm(ks[23], (DEPTH, N_EXPERTS), 0.01),
        'moe_w_gate': nrm(ks[24], (DEPTH, N_EXPERTS, D_MODEL, EXPERT_FF), D_MODEL ** -0.5),
        'moe_w_up': nrm(ks[25], (DEPTH, N_EXPERTS, D_MODEL, EXPERT_FF), D_MODEL ** -0.5),
        'moe_w_down': nrm(ks[26], (DEPTH, N_EXPERTS, EXPERT_FF, D_MODEL), EXPERT_FF ** -0.5),
    }

def reference(x_prompt, x_sample, cache_k, cache_v, page_table,
              a_norm_g, a_w_in, a_ln_g, a_ln_b, a_w_s, a_b_s, a_w_out,
              kv_norm_g, w_kv, k_norm_g,
              b_norm_g, b_w_q, q_norm_g, b_w_o,
              moe_norm_g, moe_w_rg, moe_b_rg, moe_w_re, moe_b_re, moe_w_gate, moe_w_up, moe_w_down):
    seq = x_prompt.shape[1]
    dec_seq = x_sample.shape[1]
    past = page_table.shape[1] * cache_k.shape[1]
    pos_p = jnp.arange(seq, dtype=jnp.int32)
    pos_s = past + jnp.arange(dec_seq, dtype=jnp.int32)
    last_chunk_start = ((seq - 1) // CHUNK) * CHUNK
    xp, xs = x_prompt, x_sample
    v_rows_p, v_rows_s = [], []
    for i in range(DEPTH):
        if i < N_A_LAYERS:
            a_args = (a_norm_g[i], a_w_in[i], a_ln_g[i], a_ln_b[i], a_w_s[i], a_b_s[i], a_w_out[i])
            mp, rows_p = chunk_gmlp(xp, *a_args)
            ms, rows_s = chunk_gmlp(xs, *a_args)
            xp, xs = xp + mp, xs + ms
            v_rows_p.append(rows_p[:, last_chunk_start:])
            v_rows_s.append(rows_s)
        else:
            j = i - N_A_LAYERS
            b_args = (b_norm_g[j], b_w_q[j], q_norm_g[j], b_w_o[j])
            xp = xp + moba_mixer(xp, 0, k_p, v_p, *b_args)
            xs = xs + moba_mixer(xs, past, k_all_s, v_all_s, *b_args)
        m_args = (moe_norm_g[i], moe_w_rg[i], moe_b_rg[i], moe_w_re[i], moe_b_re[i],
                  moe_w_gate[i], moe_w_up[i], moe_w_down[i])
        xp = xp + hier_moe(xp, *m_args)
        xs = xs + hier_moe(xs, *m_args)
        if i == N_A_LAYERS - 1:
            k_p, v_p = shared_kv(xp, pos_p, kv_norm_g, w_kv, k_norm_g)
            k_s, v_s = shared_kv(xs, pos_s, kv_norm_g, w_kv, k_norm_g)
            k_all_s = jnp.concatenate([gather_pages(cache_k, page_table), k_s], axis=1)
            v_all_s = jnp.concatenate([gather_pages(cache_v, page_table), v_s], axis=1)
    return (xp, xs, jnp.stack(v_rows_p), jnp.stack(v_rows_s), k_p, v_p, k_s, v_s)


_drawn_inputs = setup_inputs


def setup_inputs(seed=0):
    import zlib

    import numpy as np

    out = dict(_drawn_inputs(seed))
    spreads = {}
    factors = {'a_ln_g': 2.831,
     'a_ln_b': 2.858,
     'kv_norm_g': 2.829,
     'k_norm_g': 2.854,
     'b_norm_g': 8.0,
     'q_norm_g': 7.054,
     'moe_b_rg': 8.0,
     'moe_b_re': 4.079}
    for name, (base, spread) in spreads.items():
        noise = np.random.default_rng([zlib.crc32(name.encode()), seed]).standard_normal(out[name].shape)
        drawn = base * np.exp(spread * noise) if base else spread * noise
        out[name] = __import__('jax').numpy.asarray(drawn.astype(out[name].dtype))
    for name, factor in factors.items():
        out[name] = (out[name] * factor).astype(out[name].dtype)
    return out
```

```python
from contextlib import ExitStack

import concourse.bass as bass
from concourse import mybir

F32, I32 = mybir.dt.float32, mybir.dt.int32
ACT, ALU, AX = mybir.ActivationFunctionType, mybir.AluOpType, mybir.AxisListType

P = 128
D = 1024
KT = D // P
NP_TOK, NS = 256, 8
T = NP_TOK + NS
TILES = [(0, P), (P, P), (2 * P, NS)]
GW = 2 * D
CT = GW // P
NG = 8
H, HD = 8, 128
ROT = HD // 4
NE, NPAIR, EF = 16, 8, 512
FT = EF // P
NGRP, EPG = 4, 4
NPAGE, PAGE, NBLK = 8, 128, 4
CAP = 64
LIMIT = CAP
EPS = 1e-6
SCALE = HD ** -0.5
NEG = -1e30
SLOT = 4096


def const_layout():
    at, off = {}, 0
    for name, n in [("ident", P), ("ones", P), ("earlier", P), ("causal", 3 * P), ("iota", CAP), ("rot", ROT),
                    ("cos", T), ("sin", T), ("pick", 2 * NBLK), ("first", EPG), ("blk", NBLK), ("valid", 3)]:
        at[name] = (off, n)
        off += n
    return at, off


def constants():
    import numpy as np
    at, n = const_layout()
    c = np.zeros((P, n), np.float32)

    def put(name, value):
        o, w = at[name]
        c[:value.shape[0], o:o + w] = value.reshape(value.shape[0], w)
    i = np.arange(P)
    put("ident", np.eye(P))
    put("ones", np.ones((P, P)))
    put("earlier", i[:, None] < i[None, :])
    m = np.where(i[:, None] >= i[None, :], 0.0, NEG)
    put("causal", np.concatenate([m, np.zeros((P, P)), m], 1))
    put("iota", np.tile(np.arange(CAP), (P, 1)))
    r = np.zeros((P, ROT))
    half = ROT // 2
    for j in range(half):
        r[j + half, j], r[j, j + half] = -1.0, 1.0
    put("rot", r)
    freq = (500000.0 ** (-np.arange(half, dtype=np.float32) / half)).astype(np.float32)
    pos = np.concatenate([np.arange(NP_TOK), np.full(NS, NPAGE * PAGE)]).astype(np.float32)
    ang = (np.tile(freq, 2)[:, None] * pos[None]).astype(np.float32).astype(np.float64)
    put("cos", np.cos(ang))
    put("sin", np.sin(ang))
    s = np.zeros((P, NBLK, 2))
    for h in range(H):
        for parity in range(2):
            s[32 * (2 * parity + h // 4) + h, h % 4, h // 4] = 1.0
    put("pick", s)
    put("first", np.tile(np.arange(EPG) - 9.0, (P, 1)))
    put("blk", np.tile(np.arange(NBLK) + 1.0, (P, 1)))
    v = np.ones((P, 3))
    v[NS:, 2] = 0.0
    put("valid", v)
    return c


class Chain:

    def __init__(self, eng, sem):
        self.eng, self.sem, self.base, self.n = eng, sem, 0, 0

    def ran(self, ins):
        self.n += 1
        return ins.then_inc(self.sem, 1)

    def wait(self):
        self.eng.wait_ge(self.sem, self.base + self.n)

    def link(self, ins):
        self.ran(ins)
        self.wait()


def wait_for(eng, sem, n):
    if not isinstance(n, int) or n > 0:
        eng.wait_ge(sem, n)


def bc(ap, shape):
    return ap.to_broadcast(list(shape))


def program(nc, a, o):
    ctx = ExitStack()
    with ctx:
        def sb(name, shape, dt=F32):
            return ctx.enter_context(nc.sbuf_tensor(name, list(shape), dt))

        def sem(name):
            return ctx.enter_context(nc.semaphore(name))

        W = sb("ring", [P, 8, SLOT])
        xT = sb("xT", [P, KT, T])
        CL, CN = const_layout()
        C = sb("consts", [P, CN])

        def const(name):
            off, n = CL[name]
            return C[:, off:off + n]
        ident, ones, earlier = const("ident"), const("ones"), const("earlier")
        gains = sb("gains", [P, 5, KT])
        G_A, G_M, G_KV, G_B = 0, 1, 3, 4
        hgain = sb("hgain", [P, 2])
        wr = sb("wr", [P, 2, KT, NGRP + NE])
        rbias = sb("rbias", [NGRP + NE, 2])
        eps = sb("eps", [P, 1])
        rms = sb("rms", [P, T])
        rstd = sb("rstd", [P, T])
        pages = sb("pages", [1, NS * NPAGE], I32)
        many = sb("many", [1, 1], I32)

        ARENA = 15920
        A = sb("arena", [P, ARENA])

        def region(off, *shape):
            n = 1
            for s in shape:
                n *= s
            assert off + n <= ARENA, (off, n)
            v = A[:, off:off + n]
            if len(shape) == 1:
                return v
            names = "abc"[:len(shape)]
            return v.rearrange(f"p ({' '.join(names)}) -> p {' '.join(names)}", **dict(zip(names, shape)))
        hT = region(0, KT, T)
        vT = region(2112, CT, T)
        vr = region(6336, 3, GW)
        lng = region(12480, 2, 512)
        wsT = region(13504, NG, P)
        bs = region(14528, NG, P)
        xr = region(6336, 3, D)
        wsr = region(6336 + 3 * D, NG, P)
        sqA = region(2112, KT, T)
        raw_g = [region(10432 + l * KT * NGRP, KT, NGRP) for l in range(2)]
        raw_e = [region(10496 + l * KT * NE, KT, NE) for l in range(2)]
        b00 = region(15552, NG, NS)
        d8 = region(15616, NG, NS)
        stats = region(15680, 3, 4 * 6)
        mv = region(15752, 3, 2)
        vrstd = region(15758, 3)
        hr = region(2112, 3, D)
        sqM = region(5184, KT, T)
        hot = region(7296, 3, 2, CAP)
        ghot = region(7680, 3, 2, CAP)
        sT = region(8064, T)
        hg = region(8328, KT, P)
        sg = region(9352, EF)
        he = region(9864, EF)
        heT = region(10376, FT, P)
        dr = region(10888, D)
        lgT = region(11912, T)
        lg = region(12176, 3, NGRP + NE)
        ro = 12236

        def small(*shape):
            nonlocal ro
            n = 1
            for s in shape:
                n *= s
            ro += n
            return region(ro - n, *shape)
        gm, pg, mn, m1, m2, e2, w1, w2 = (small(3) for _ in range(8))
        ohg, oh1, oh2, leg, le2, cand, ex = (small(3, 4) for _ in range(7))
        prod = small(3, 16)
        gates = small(3, 16)
        chose = small(3, 16)
        rank = small(3, 16)
        cmax = small(1)
        sgD = region(2112, T)
        heD = region(2376, FT, T)
        gb = region(3432, 3, P)
        gcol = region(3816, T)
        hk, hq = region(0, KT, T), region(2112, KT, T)
        kq = region(4224, 2 * H, T)
        krows = region(8448, 3, D)
        vrows = region(11520, 3, D)
        sqB = region(8448, KT, T)
        sqh = region(14592, 2, T)
        rmh = region(15120, T)
        rsh = region(15384, T)
        turned = region(15648, T)
        vTh = region(2112, 2, T)
        vTs = region(2640, H, NS)
        aT = region(0, H, T)
        own = region(2704, H, NS)
        ownp = region(2768, H, NS)
        s3 = region(8448, 3 * P)
        p3 = region(8832, 3 * P)
        pT3 = region(9216, 3 * P)
        mx3, rs3, ri3 = region(9600, 2), region(9602, 2), region(9604, 2)
        sc = region(9608, 2, NPAGE + 1, H)
        pe4 = region(9752, 2, NPAGE + 1, 32)
        ov = region(10328, 512)
        gsum, eqb, drop = region(10840, NBLK, H), region(10872, NBLK, H), region(10904, NBLK, H)
        mnb, vmb, pmx, mall, rsum, den, rden, tmp8 = (region(10936 + 8 * i, H) for i in range(8))
        dg = region(11000, H)
        hm = region(11008, 1)
        yr = region(2112, 3, D)

        PB = [ctx.enter_context(nc.psum_tensor(f"bank{i}", [P, 512], F32)) for i in range(8)]

        filled, before = [0] * 8, {}

        def stage(name, slots, each, times=1):
            before[name] = list(filled)
            for s in slots:
                filled[s] += each * times
        stage("v", range(0, 4), 16)
        stage("u", range(4, 8), 16)
        stage("wout", range(0, 4), 16)
        stage("moe0", [4, 5, 6, 7, 0, 1], 16, NPAIR)
        stage("kv", range(4, 8), 16)
        stage("q", [2, 3], 16)
        stage("seqs", range(8), 16 * 4, NS // 2)
        stage("wo", [2, 3], 16)
        stage("moe1", [4, 5, 6, 7, 0, 1], 16, NPAIR)

        full = [sem(f"full{s}") for s in range(8)]

        def arrived(eng, name, slot, nth=1, each=16):
            eng.wait_ge(full[slot], before[name][slot] + each * nth)

        c_load, x_load, g_load, page_load = sem("c_load"), sem("x_load"), sem("g_load"), sem("page_load")
        wr_raw, ws_load, bs_load = sem("wr_raw"), sem("ws_load"), sem("bs_load")
        eps_set, wr_made, ws_masked = sem("eps_set"), sem("wr_made"), sem("ws_masked")
        ws_turned, ws_kept, w00_out, d8_made = sem("ws_turned"), sem("ws_kept"), sem("w00_out"), sem("d8_made")
        x_turned, x_kept = sem("x_turned"), sem("x_kept")
        sq_made, ss_out, rms_made, rstd_made, h_made = (sem(n) for n in
                                                        ["sq_made", "ss_out", "rms_made", "rstd_made", "h_made"])
        v_out, v_gelu, v_turned, v_kept = sem("v_out"), sem("v_gelu"), sem("v_turned"), sem("v_kept")
        mv_made, vsd_made, ln_load, ln_used, ln_done = (sem(n) for n in
                                                        ["mv_made", "vsd_made", "ln_load", "ln_used", "ln_done"])
        u_out, u_gelu, mix_out, um_made = sem("u_out"), sem("u_gelu"), sem("mix_out"), sem("um_made")
        a_out, a_added = sem("a_out"), sem("a_added")
        vec, v_rows_out = sem("vector_steps"), sem("v_rows_out")
        stored = sem("stored")
        L2 = range(2)

        def pair_of(name):
            return [sem(f"{name}{l}") for l in L2]
        lgT_out, lgT_made, lg_out, hr_out, hr_kept = (sem(n) for n in ["lgT_out", "lgT_made", "lg_out", "hr_out", "hr_kept"])
        soft_in, soft_out, chose_made, rank_out, many_set, moe_done = (sem(n) for n in [
            "soft_in", "soft_out", "chose_made", "rank_out", "many_set", "moe_done"])
        gate_out, up_out, down_out = (pair_of(n) for n in ["gate_out", "up_out", "down_out"])
        hot_made, ghot_made, gather_out, hg_lo, hg_hi = (pair_of(n) for n in [
            "hot_made", "ghot_made", "gather_out", "hg_lo", "hg_hi"])
        silu_made, he_made, heT_out, heT_made = (pair_of(n) for n in ["silu_made", "he_made", "heT_out", "heT_made"])
        dr_lo, dr_hi, sT_out, sT_made, y_out, y_added = (pair_of(n) for n in [
            "dr_lo", "dr_hi", "sT_out", "sT_made", "y_out", "y_added"])
        gb_made, gcol_out, gcol_made, gD_out, sD_made, hD_made, yD_out, yD_added = (pair_of(n) for n in [
            "gb_made", "gcol_out", "gcol_made", "gD_out", "sD_made", "hD_made", "yD_out", "yD_added"])
        vecD = pair_of("vector_steps_all")
        kq_out, kq_sq, kq_ss, kq_rms, kq_normed, kq_rot, kq_made = (sem(n) for n in [
            "kq_out", "kq_sq", "kq_ss", "kq_rms", "kq_normed", "kq_rot", "kq_made"])
        vp_out, vp_kept, rows_out, rows_kept = (sem(n) for n in ["vp_out", "vp_kept", "rows_out", "rows_kept"])
        own_in, own_out, own_made, k_stored, pad_set = (sem(n) for n in ["own_in", "own_out", "own_made", "k_stored", "pad_set"])
        ps_out, ps_max, ps_exp, ps_norm, pT_out, pT_made, po_out, po_kept = (sem(n) for n in [
            "ps_out", "ps_max", "ps_exp", "ps_norm", "pT_out", "pT_made", "po_out", "po_kept"])
        qb_out, k_used, s_made, gs_out, pm_made, pm_turned, dg_made, mb_out, sc_made, se_made, rs_made, den_out = (
            sem(n) for n in ["qb_out", "k_used", "s_made", "gs_out", "pm_made", "pm_turned", "dg_made", "mb_out",
                             "sc_made", "se_made", "rs_made", "den_out"])
        pv_out, ov_made, o_out, att_made = sem("pv_out"), sem("ov_made"), sem("o_out"), sem("att_made")
        wo_out, wo_added = sem("wo_out"), sem("wo_added")
        y_turned, yr_made = sem("y_turned"), sem("yr_made")

        block = ctx.enter_context(nc.Block())

        def w_rows(ap, k):
            return ap.rearrange("(p k) n -> p k n", k=k)

        def slot(s, k):
            return W[:, s, :].rearrange("p (k n) -> p k n", k=k)

        @block.sync
        def _(sp):
            sp.dma_start(xr[:, 0:2, :], a["x_prompt"][0].rearrange("(t p) d -> p t d", p=P)).then_inc(x_load, 16)
            sp.dma_start(xr[0:NS, 2, :], a["x_sample"].rearrange("b s d -> (b s) d")).then_inc(x_load, 16)
            w_in = w_rows(a["a_w_in"][0], KT)
            for q in range(4):
                sp.dma_start(slot(q, 2), w_in[:, 2 * q:2 * q + 2, GW:2 * GW]).then_inc(full[q], 16)
            for q in range(4):
                sp.dma_start(slot(4 + q, 2), w_in[:, 2 * q:2 * q + 2, 0:GW]).then_inc(full[4 + q], 16)
            w_out = a["a_w_out"][0].rearrange("(c p) n -> p c n", p=P)
            sp.wait_ge(v_out, CT)
            for q in range(4):
                sp.dma_start(slot(q, 4), w_out[:, 4 * q:4 * q + 4, :]).then_inc(full[q], 16)

            def experts(layer):
                gate = a["moe_w_gate"][layer].rearrange("e (p k) n -> e p (k n)", k=KT)
                up = a["moe_w_up"][layer].rearrange("e (p k) n -> e p (k n)", k=KT)
                down = a["moe_w_down"][layer].rearrange("e (f p) n -> e p f n", p=P)

                def load(i):
                    for e in range(2):
                        sp.dma_start(W[:, 4 + e, :], gate[bass.ds(2 * i + e, 1)].rearrange("e p n -> (e p) n"))\
                            .then_inc(full[4 + e], 16)
                    if not isinstance(i, int):
                        sp.wait_ge(up_out[layer], i)
                    elif layer == 0:
                        pass
                    for e in range(2):
                        sp.dma_start(W[:, 6 + e, :], up[bass.ds(2 * i + e, 1)].rearrange("e p n -> (e p) n"))\
                            .then_inc(full[6 + e], 16)
                    if not isinstance(i, int):
                        sp.wait_ge(down_out[layer], i)
                    elif layer == 0:
                        sp.wait_ge(a_out, KT)
                    for e in range(2):
                        sp.dma_start(slot(e, FT), down[bass.ds(2 * i + e, 1)].rearrange("e p f n -> (e p) f n"))\
                            .then_inc(full[e], 16)
                load(0)
                with sp.Fori(1, NPAIR) as i:
                    sp.wait_ge(gate_out[layer], i)
                    load(i)

            sp.wait_ge(u_out, CT)
            experts(0)
            w_kv = w_rows(a["w_kv"], KT)
            for q in range(4):
                if q == 0:
                    sp.wait_ge(gate_out[0], NPAIR)
                if q == 2:
                    sp.wait_ge(up_out[0], NPAIR)
                sp.dma_start(slot(4 + q, 2), w_kv[:, 2 * q:2 * q + 2, :]).then_inc(full[4 + q], 16)
            w_q = w_rows(a["b_w_q"][0], KT)
            for q in range(2):
                sp.dma_start(slot(2 + q, 4), w_q[:, 4 * q:4 * q + 4, :]).then_inc(full[2 + q], 16)

            sp.wait_ge(page_load, 16)

            def load_pages(pool, s, first_slot, c):
                for g in range(4):
                    page = sp.value_load(pages[0:1, s * NPAGE + 4 * c + g:s * NPAGE + 4 * c + g + 1],
                                         min_val=0, max_val=pool.shape[0] - 1)
                    sp.dma_start(W[:, first_slot + c, g * D:(g + 1) * D],
                                 pool[bass.ds(page, 1)].rearrange("a p h d -> (a p) (h d)"))\
                        .then_inc(full[first_slot + c], 16)
            for s in range(NS):
                k_slot, v_slot = 4 * (s % 2), 4 * (s % 2) + 2
                if s == 0:
                    sp.wait_ge(down_out[0], NPAIR)
                if s == 1:
                    sp.wait_ge(vp_out, H)
                for c in range(2):
                    if s >= 2:
                        sp.wait_ge(k_used, 2 * (s - 2) + c + 1)
                    load_pages(a["cache_k"], s, k_slot, c)
                if s == 0:
                    sp.wait_ge(kq_out, 2 * H)
                if s >= 2:
                    sp.wait_ge(pv_out, s - 1)
                for c in range(2):
                    load_pages(a["cache_v"], s, v_slot, c)
            w_o = a["b_w_o"][0].rearrange("(h p) n -> p h n", p=P)
            sp.wait_ge(pv_out, NS - 1)
            for q in range(2):
                sp.dma_start(slot(2 + q, 4), w_o[:, 4 * q:4 * q + 4, :]).then_inc(full[2 + q], 16)
            sp.wait_ge(k_used, 2 * NS)
            sp.wait_ge(pv_out, NS)
            experts(1)
            sp.wait_ge(stored, 16 * 7)
            sp.wait_ge(k_stored, 16 * 2)

        @block.gpsimd
        def _(pool):
            pool.wait_ge(ws_load, 16)
            nc.gpsimd.affine_select(out=wsr, in_=wsr, compare_op=ALU.is_ge, fill=0.0, base=0,
                                    pattern=[[0, NG], [-1, P]], channel_multiplier=1).then_inc(ws_masked, 1)
            pool.wait_ge(wr_raw, 64)
            for l in L2:
                for src, lo, n in ((raw_g[l], 0, NGRP), (raw_e[l], NGRP, NE)):
                    nc.gpsimd.tensor_copy(wr[:, l, :, lo:lo + n], src).then_inc(wr_made, 1)
            for c in range(4):
                if c:
                    pool.wait_ge(ln_used, c)
                for i, name in enumerate(("a_ln_g", "a_ln_b")):
                    pool.dma_start(lng[:, i, :], a[name][0:1, 512 * c:512 * (c + 1)].partition_broadcast(P))\
                        .then_inc(ln_load, 16)
            pool.wait_ge(ln_done, 1)
            pool.dma_start(o["v_rows_prompt"][0, 0], vr[:, 1, :]).then_inc(stored, 16)
            pool.dma_start(o["v_rows_sample"][0].rearrange("b s n -> (b s) n"), vr[0:NS, 2, :]).then_inc(stored, 16)

            def moe(l):
                pool.wait_ge(many_set, l + 1)
                flag = pool.value_load(many[0:1, 0:1], min_val=0, max_val=T)
                with pool.If(flag > LIMIT):
                    pool.nop()
                with pool.Else():
                    def weigh(i):
                        pool.wait_ge(hot_made[l], i + 1)
                        if not isinstance(i, int):
                            pool.wait_ge(sT_out[l], i)
                        elif i:
                            pool.wait_ge(sT_out[l], i)
                        nc.gpsimd.tensor_tensor(ghot, hot, bc(gates[:, :, bass.ds(2 * i, 2)].unsqueeze(3),
                                                              [P, 3, 2, CAP]), ALU.mult).then_inc(ghot_made[l], 1)
                    weigh(0)
                    with pool.Fori(1, NPAIR) as i:
                        weigh(i)
                pool.nop()
            moe(0)
            nc.gpsimd.wait_ge(rows_kept, 6)
            for rows, kname in ((krows, "k"), (vrows, "v")):
                if kname == "v":
                    pool.wait_ge(rows_kept, 12)
                s_ = k_stored if kname == "k" else stored
                pool.dma_start(o[kname + "_prompt"][0].rearrange("(t p) h d -> p t (h d)", p=P),
                               rows[:, 0:2, :]).then_inc(s_, 16)
                pool.dma_start(o[kname + "_sample"].rearrange("b s h d -> (b s) (h d)"),
                               rows[0:NS, 2, :]).then_inc(s_, 16)
                if kname == "k":
                    pool.wait_ge(k_stored, 32)
                    nc.gpsimd.memset(pe4, 0.0).then_inc(pad_set, 1)
            moe(1)
            for t, (t0, n) in enumerate(TILES):
                pool.wait_ge(yr_made, 2 * (t + 1))
                dst = o["y_prompt"][0, t0:t0 + n, :] if t < 2 else o["y_sample"].rearrange("b s d -> (b s) d")
                pool.dma_start(dst, yr[0:n, t, :]).then_inc(stored, 16)

        @block.scalar
        def _(act):
            act.dma_start(C[:, :], a["consts"]).then_inc(c_load, 16)
            act.dma_start(wsr, a["a_w_s"][0].rearrange("g t s -> t g s")).then_inc(ws_load, 16)
            act.dma_start(bs[0:1], a["a_b_s"]).then_inc(bs_load, 16)
            for i, g in enumerate((a["a_norm_g"][0], a["moe_norm_g"][0], a["moe_norm_g"][1], a["kv_norm_g"],
                                   a["b_norm_g"][0])):
                act.dma_start(gains[:, i, :], g.rearrange("(p k) -> p k", k=KT)).then_inc(g_load, 16)
            act.dma_start(hgain[:, 0:1], a["k_norm_g"].rearrange("(p k) -> p k", k=1)).then_inc(g_load, 16)
            act.dma_start(hgain[:, 1:2], a["q_norm_g"][0].rearrange("(p k) -> p k", k=1)).then_inc(g_load, 16)
            for l in L2:
                act.dma_start(rbias[0:NGRP, l:l + 1], a["moe_b_rg"][l].rearrange("(p k) -> p k", k=1)).then_inc(g_load, 16)
                act.dma_start(rbias[NGRP:NGRP + NE, l:l + 1], a["moe_b_re"][l].rearrange("(p k) -> p k", k=1))\
                    .then_inc(g_load, 16)
                act.dma_start(raw_g[l], a["moe_w_rg"][l].rearrange("(p k) n -> p k n", k=KT)).then_inc(wr_raw, 16)
                act.dma_start(raw_e[l], a["moe_w_re"][l].rearrange("(p k) n -> p k n", k=KT)).then_inc(wr_raw, 16)
            act.dma_start(pages[:, :], a["page_table"].rearrange("b n -> (b n)").rearrange("(a n) -> a n", a=1))\
                .then_inc(page_load, 16)
            act.wait_ge(eps_set, 1)

            def square_and_root(n, sq, ready, count):
                act.wait_ge(ready, count)
                for half in range(2):
                    nc.scalar.activation(sq[:, 4 * half:4 * half + 4, :], xT[:, 4 * half:4 * half + 4, :], ACT.Square)\
                        .then_inc(sq_made, 1)
                act.wait_ge(ss_out, n + 1)
                nc.scalar.activation(rms[:, :], PB[2][:, 0:T], ACT.Sqrt, bias=eps[:, 0:1], scale=1.0 / D)\
                    .then_inc(rms_made, 1)
            square_and_root(0, sqA, x_kept, KT)

            for j in range(CT):
                act.wait_ge(v_out, j + 1)
                nc.scalar.activation(vT[:, j, :], PB[j % 2][:, 0:T], ACT.Gelu_apprx_tanh).then_inc(v_gelu, 1)
            act.wait_ge(mv_made, 1)
            nc.scalar.activation(vrstd, mv[:, :, 1], ACT.Sqrt, bias=eps[:, 0:1]).then_inc(vsd_made, 1)
            for j in range(CT):
                act.wait_ge(u_out, j + 1)
                nc.scalar.activation(vT[:, j, :], PB[j % 2][:, 0:T], ACT.Gelu_apprx_tanh).then_inc(u_gelu, 1)

            def moe(l):
                act.wait_ge(lgT_out, l + 1)
                act.wait_ge(g_load, 16 * 11)
                nc.scalar.activation(lgT[0:NGRP + NE, :], PB[3][0:NGRP + NE, 0:T], ACT.Identity,
                                     bias=rbias[:, l:l + 1]).then_inc(lgT_made, 1)
                for i in range(6):
                    t, half = divmod(i, 2)
                    n = TILES[t][1]
                    act.wait_ge(hr_out, 6 * l + i + 1)
                    nc.scalar.activation(hr[0:n, t, 512 * half:512 * (half + 1)], PB[4 + i % 4][0:n, :], ACT.Copy)\
                        .then_inc(hr_kept, 1)
                act.wait_ge(soft_in, 2 * l + 1)
                nc.scalar.activation(ex, ex, ACT.Exp).then_inc(soft_out, 1)
                act.wait_ge(soft_in, 2 * l + 2)
                nc.scalar.activation(e2, e2, ACT.Exp).then_inc(soft_out, 1)
                act.wait_ge(many_set, l + 1)
                flag = act.value_load(many[0:1, 0:1], min_val=0, max_val=T)
                with act.If(flag > LIMIT):
                    def all_tokens(i):
                        for c in range(2 * FT):
                            act.wait_ge(gD_out[l], i * (2 * FT) + c + 1)
                            wait_for(act, hD_made[l], i * (2 * FT) + c)
                            nc.scalar.activation(sgD, PB[c % 2][:, 0:T], ACT.Silu).then_inc(sD_made[l], 1)
                    all_tokens(0)
                    with act.Fori(1, NPAIR) as i:
                        all_tokens(i)
                with act.Else():
                    def copy_hg(i):
                        act.wait_ge(gather_out[l], i + 1)
                        nc.scalar.activation(hg[:, 0:4, :], PB[0][:, :].rearrange("p (k s) -> p k s", k=4), ACT.Copy)\
                            .then_inc(hg_lo[l], 1)

                    def pair(i, last):
                        act.wait_ge(gate_out[l], i + 1)
                        nc.scalar.activation(sg, PB[2][:, :], ACT.Silu).then_inc(silu_made[l], 1)
                        act.wait_ge(heT_out[l], i + 1)
                        nc.scalar.activation(heT, PB[6][:, :].rearrange("p (f s) -> p f s", f=FT), ACT.Copy)\
                            .then_inc(heT_made[l], 1)
                        if not last:
                            copy_hg(i + 1)
                        act.wait_ge(down_out[l], i + 1)
                        nc.scalar.activation(dr[:, 0:512], PB[4][:, :], ACT.Copy).then_inc(dr_lo[l], 1)
                    copy_hg(0)
                    with act.Fori(0, NPAIR - 1) as i:
                        pair(i, False)
                    pair(NPAIR - 1, True)
                act.nop()
            act.wait_ge(stored, 32)
            square_and_root(1, sqM, a_added, KT)
            moe(0)
            square_and_root(2, sqB, moe_done, 1)

            def rows_copy(g, rows):
                for t, (_, n) in enumerate(TILES):
                    act.wait_ge(rows_out, g + 1)
                    nc.scalar.activation(rows[0:n, t, 512 * (g % 2):512 * (g % 2 + 1)], PB[4 + t][0:n, :], ACT.Copy)\
                        .then_inc(rows_kept, 1)
            for g in range(2 * H + 1):
                if g < 2 * H:
                    act.wait_ge(kq_out, g + 1)
                    if g >= 2:
                        act.wait_ge(kq_ss, g - 1)
                    nc.scalar.activation(sqh[:, g % 2, :], PB[g % 2][:, 0:T], ACT.Square).then_inc(kq_sq, 1)
                if g >= 1:
                    act.wait_ge(kq_ss, g)
                    if g >= 2:
                        act.wait_ge(kq_normed, g - 1)
                    nc.scalar.activation(rmh, PB[2][:, 0:T], ACT.Sqrt, bias=eps[:, 0:1], scale=1.0 / HD)\
                        .then_inc(kq_rms, 1)
                if g - 4 in (3, 7):
                    rows_copy((g - 4) // 4, krows)
            for v in range(H):
                act.wait_ge(vp_out, v + 1)
                if v >= 2:
                    act.wait_ge(rows_out, 2)
                    act.wait_ge(v_rows_out, v - 1)
                nc.scalar.activation(vTh[:, v % 2, :], PB[v % 2][:, 0:T], ACT.Copy).then_inc(vp_kept, 1)
                nc.scalar.activation(vTs[:, v, :], PB[v % 2][:, NP_TOK:T], ACT.Copy).then_inc(vp_kept, 1)
                if v % 4 == 0 and v:
                    rows_copy(2 + v // 4 - 1, vrows)
            rows_copy(3, vrows)
            act.wait_ge(pad_set, 1)
            for s in range(NS + 1):
                if s < NS:
                    act.wait_ge(ps_max, s + 1)
                    for q, (lo, n) in enumerate(((0, P), (P, 2 * P))):
                        nc.scalar.activation(p3[:, lo:lo + n], s3[:, lo:lo + n], ACT.Exp, bias=mx3[:, q:q + 1],
                                             scale=SCALE, accum_out=rs3[:, q:q + 1]).then_inc(ps_exp, 1)
                if s >= 1:
                    c = (s - 1) % 2
                    act.wait_ge(sc_made, s)
                    nc.scalar.activation(pe4[:, c, :, 0:H], sc[:, c, :, :], ACT.Exp, scale=SCALE).then_inc(se_made, 1)
                if s < NS:
                    act.wait_ge(pT_out, s + 1)
                    nc.scalar.activation(pT3, PB[1][:, 0:3 * P], ACT.Copy).then_inc(pT_made, 1)
                if s >= 1:
                    act.wait_ge(pv_out, s)
                    if s >= 2:
                        act.wait_ge(o_out, s - 1)
                    nc.scalar.activation(ov, PB[4][:, :], ACT.Copy).then_inc(ov_made, 1)
                if s < NS:
                    act.wait_ge(po_out, s + 1)
                    if s == 0:
                        act.wait_ge(vp_out, H)
                    nc.scalar.activation(aT[:, s, 0:NP_TOK], PB[2][:, 0:NP_TOK], ACT.Copy).then_inc(po_kept, 1)
            act.wait_ge(stored, 64)
            square_and_root(3, sqM, wo_added, KT)
            moe(1)

        @block.tensor
        def _(pe):
            mm, tr = nc.tensor.matmul, nc.tensor.transpose

            pe.wait_ge(c_load, 16)
            pe.wait_ge(x_load, 32)
            for k in range(KT):
                if k >= 2:
                    pe.wait_ge(x_kept, k - 1)
                for t, (t0, n) in enumerate(TILES):
                    last = tr(PB[k % 2][:, t0:t0 + n], xr[0:n, t, k:D:KT], ident[0:n, 0:n])
                last.then_inc(x_turned, 1)
            pe.wait_ge(ws_masked, 1)
            for half in range(2):
                for g in range(4):
                    last = tr(PB[4 + half][:, g * P:(g + 1) * P], wsr[:, 4 * half + g, :], ident)
                last.then_inc(ws_turned, 1)
            mm(PB[6][0:NS, 0:NG], ones[0:1, 0:NS], wsr[0:1, :, 0], start=True, stop=True).then_inc(w00_out, 1)

            def sum_squares(n, sq):
                for k in range(KT):
                    if k % 4 == 0:
                        pe.wait_ge(sq_made, 2 * n + 1 + k // 4)
                    last = mm(PB[2][:, 0:T], ones, sq[:, k, :], start=(k == 0), stop=(k == KT - 1))
                last.then_inc(ss_out, 1)
            sum_squares(0, sqA)

            def turn_v(j):
                pe.wait_ge(v_gelu, j + 1)
                if j % 4 == 0:
                    if j:
                        pe.wait_ge(v_kept, 6 * (j // 4))
                    else:
                        pe.wait_ge(ws_kept, 2)
                        pe.wait_ge(d8_made, 1)
                for t, (t0, n) in enumerate(TILES):
                    last = tr(PB[4 + t][0:n, (j % 4) * P:(j % 4 + 1) * P], vT[:, j, t0:t0 + n], ident)
                if j % 4 == 3:
                    last.then_inc(v_turned, 1)

            def half_of_w_in(name, base, out, gelu, after):
                for j in range(CT):
                    if j >= 2:
                        pe.wait_ge(gelu, j - 1)
                    for k in range(KT):
                        if j == 0:
                            pe.wait_ge(h_made, k + 1)
                            if k % 2 == 0:
                                arrived(pe, name, base + k // 2)
                        last = mm(PB[j % 2][:, 0:T], slot(base + k // 2, 2)[:, k % 2, j * P:(j + 1) * P], hT[:, k, :],
                                  start=(k == 0), stop=(k == KT - 1))
                    last.then_inc(out, 1)
                    if after and j:
                        after(j - 1)
            half_of_w_in("v", 0, v_out, v_gelu, turn_v)
            turn_v(CT - 1)
            pe.wait_ge(v_gelu, CT)
            half_of_w_in("u", 4, u_out, u_gelu, None)

            pe.wait_ge(ln_done, 1)
            pe.wait_ge(bs_load, 16)
            pe.wait_ge(d8_made, 2)
            for c in range(CT):
                g = c // 2
                bank = PB[4 + c % 2]
                if c >= 2:
                    pe.wait_ge(um_made, c - 1)
                for t, (t0, n) in enumerate(TILES):
                    mm(bank[:, t0:t0 + n], ones[0:1, :], bs[0:1, g, :] if t < 2 else b00[0:1, g, :],
                       start=True, stop=False)
                    last = mm(bank[:, t0:t0 + n], vr[0:n, t, c * P:(c + 1) * P],
                              wsT[:, g, :] if t < 2 else d8[0:NS, g, :], start=False, stop=True)
                last.then_inc(mix_out, 1)
            for j in range(KT):
                if j >= 2:
                    pe.wait_ge(a_added, j - 1)
                else:
                    pe.wait_ge(u_gelu, CT)
                for c in range(CT):
                    if j == 0:
                        pe.wait_ge(um_made, c + 1)
                        if c % 4 == 0:
                            arrived(pe, "wout", c // 4)
                    last = mm(PB[j % 2][:, 0:T], slot(c // 4, 4)[:, c % 4, j:D:KT], vT[:, c, :],
                              start=(c == 0), stop=(c == CT - 1))
                last.then_inc(a_out, 1)

            def moe(l, n_norm, h_count):
                st = f"moe{l}"
                pe.wait_ge(h_made, h_count)
                if l == 0:
                    pe.wait_ge(wr_made, 4)
                for k in range(KT):
                    last = mm(PB[3][0:NGRP + NE, 0:T], wr[:, l, k, :], hT[:, k, :], start=(k == 0), stop=(k == KT - 1))
                last.then_inc(lgT_out, 1)

                def rows(i):
                    t, half = divmod(i, 2)
                    t0, n = TILES[t]
                    if i >= 4:
                        pe.wait_ge(hr_kept, 6 * l + i - 3)
                    for q in range(4):
                        last = tr(PB[4 + i % 4][0:n, q * P:(q + 1) * P], hT[:, 4 * half + q, t0:t0 + n], ident)
                    last.then_inc(hr_out, 1)
                rows(0)
                rows(1)
                pe.wait_ge(lgT_made, l + 1)
                for t, (t0, n) in enumerate(TILES):
                    last = tr(PB[2][0:n, t * 20:(t + 1) * 20], lgT[0:NGRP + NE, t0:t0 + n], ident[0:20, 0:20])
                last.then_inc(lg_out, 1)
                for i in range(2, 6):
                    rows(i)
                pe.wait_ge(chose_made, l + 1)
                for t in range(3):
                    for u in range(t + 1):
                        mm(PB[2][:, 64 + 16 * t:80 + 16 * t], earlier if u == t else ones, chose[:, u, :],
                           start=(u == 0), stop=(u == t))
                for u in range(3):
                    last = mm(PB[2][:, 112:128], ones, chose[:, u, :], start=(u == 0), stop=(u == 2))
                last.then_inc(rank_out, 1)
                pe.wait_ge(many_set, l + 1)
                flag = pe.value_load(many[0:1, 0:1], min_val=0, max_val=T)
                with pe.If(flag > LIMIT):
                    pe.wait_ge(hr_kept, 6 * l + 6)
                    def all_tokens(i):
                        for e in range(2):
                            pe.wait_ge(gb_made[l], i * 2 + e + 1)
                            for t, (t0, n) in enumerate(TILES):
                                last = mm(PB[7][:, t0:t0 + n], gb[0:n, t, :], ident[0:n, 0:n], start=True, stop=True)
                            last.then_inc(gcol_out[l], 1)
                            for s in (4 + e, 6 + e, e):
                                arrived(pe, st, s, i + 1)
                            for f in range(FT):
                                c = e * FT + f
                                wait_for(pe, hD_made[l], i * (2 * FT) + (c - 1 if c >= 2 else 0))
                                for base, bank in ((4, PB[f % 2]), (6, PB[2 + f % 2])):
                                    for k in range(KT):
                                        last = mm(bank[:, 0:T], slot(base + e, KT)[:, k, f * P:(f + 1) * P], hT[:, k, :],
                                                  start=(k == 0), stop=(k == KT - 1))
                                    if e == 1 and f == FT - 1 and base == 4:
                                        last.then_inc(gate_out[l], 1)
                                last.then_inc(gD_out[l], 1)
                            pe.wait_ge(hD_made[l], i * (2 * FT) + (e + 1) * FT)
                            for j in range(KT):
                                c = e * KT + j
                                wait_for(pe, yD_added[l], i * (2 * KT) + (c - 1 if c >= 2 else 0))
                                for f in range(FT):
                                    last = mm(PB[4 + j % 2][:, 0:T], slot(e, FT)[:, f, j:D:KT], heD[:, f, :],
                                              start=(f == 0), stop=(f == FT - 1))
                                last.then_inc(yD_out[l], 1)
                        pe.wait_ge(yD_out[l], i * (2 * KT) + 2 * KT)
                        pe.sem_inc(up_out[l], 1)
                        pe.sem_inc(down_out[l], 1)
                    all_tokens(0)
                    with pe.Fori(1, NPAIR) as i:
                        all_tokens(i)
                with pe.Else():
                    def gather(i):
                        pe.wait_ge(hot_made[l], i + 1)
                        for k in range(KT):
                            for t, (t0, n) in enumerate(TILES):
                                last = mm(PB[k // 4][:, (k % 4) * P:(k % 4 + 1) * P], hr[0:n, t, k * P:(k + 1) * P],
                                          hot[0:n, t, :, :].rearrange("p e s -> p (e s)"), start=(t == 0), stop=(t == 2))
                        last.then_inc(gather_out[l], 1)

                    def scatter(i):
                        pe.wait_ge(dr_lo[l], i + 1)
                        pe.wait_ge(dr_hi[l], i + 1)
                        pe.wait_ge(sT_made[l], i + 1)
                        for j in range(KT):
                            if j >= 2:
                                pe.wait_ge(y_added[l], i * KT + j - 1)
                            last = mm(PB[6 + j % 2][:, 0:T], dr[:, j:D:KT], sT, start=True, stop=True)
                            last.then_inc(y_out[l], 1)

                    def pair(i, first, last_pair):
                        pe.wait_ge(hg_lo[l], i + 1)
                        pe.wait_ge(hg_hi[l], i + 1)
                        for base, bank, out in ((4, PB[2], gate_out), (6, PB[3], up_out)):
                            for e in range(2):
                                arrived(pe, st, base + e, i + 1)
                            if not first:
                                pe.wait_ge(he_made[l], i)
                            for k in range(KT):
                                for e in range(2):
                                    last = mm(bank[64 * e:64 * e + 64, :], hg[:, k, CAP * e:CAP * (e + 1)],
                                              slot(base + e, KT)[:, k, :], start=(k == 0), stop=(k == KT - 1))
                            last.then_inc(out[l], 1)
                        if not first:
                            scatter(i - 1)
                        pe.wait_ge(he_made[l], i + 1)
                        if not first:
                            pe.wait_ge(y_added[l], i * KT)
                        for f in range(FT):
                            last = tr(PB[6][:, f * P:(f + 1) * P], he[:, f * P:(f + 1) * P], ident)
                        last.then_inc(heT_out[l], 1)
                        if not last_pair:
                            gather(i + 1)
                        pe.wait_ge(ghot_made[l], i + 1)
                        for t, (t0, n) in enumerate(TILES):
                            last = tr(PB[7][:, t0:t0 + n], ghot[0:n, t, :, :].rearrange("p e s -> p (e s)"), ident[0:n, 0:n])
                        last.then_inc(sT_out[l], 1)
                        for e in range(2):
                            arrived(pe, st, e, i + 1)
                        pe.wait_ge(heT_made[l], i + 1)
                        if not first:
                            pe.wait_ge(dr_lo[l], i)
                            pe.wait_ge(dr_hi[l], i)
                        for f in range(FT):
                            for half in range(2):
                                for e in range(2):
                                    last = mm(PB[4 + half][64 * e:64 * e + 64, :], heT[:, f, CAP * e:CAP * (e + 1)],
                                              slot(e, FT)[:, f, 512 * half:512 * (half + 1)],
                                              start=(f == 0), stop=(f == FT - 1))
                        last.then_inc(down_out[l], 1)
                    pe.wait_ge(hr_kept, 6 * l + 6)
                    gather(0)
                    pair(0, True, False)
                    with pe.Fori(1, NPAIR - 1) as i:
                        pair(i, False, False)
                    pair(NPAIR - 1, False, True)
                    scatter(NPAIR - 1)
                pe.nop()

            sum_squares(1, sqM)
            moe(0, 1, 2 * KT)
            sum_squares(2, sqB)

            pe.wait_ge(h_made, 4 * KT)

            def rows(g, src, group_first_wait):
                if g % 4 == 0 and g:
                    pe.wait_ge(rows_kept, 3 * (g // 4))
                for t, (t0, n) in enumerate(TILES):
                    last = tr(PB[4 + t][0:n, (g % 4) * P:(g % 4 + 1) * P], src[:, t0:t0 + n], ident)
                if g % 4 == 3:
                    last.then_inc(rows_out, 1)
                return last
            for g in range(2 * H + 3):
                if g < 2 * H:
                    if g >= 2:
                        pe.wait_ge(kq_normed, g - 1)
                    for k in range(KT):
                        if g < H:
                            if g == 0 and k % 2 == 0:
                                arrived(pe, "kv", 4 + k // 2)
                            w, h = slot(4 + k // 2, 2)[:, k % 2, g * HD:(g + 1) * HD], hk
                        else:
                            if g == H and k % 4 == 0:
                                arrived(pe, "q", 2 + k // 4)
                            w, h = slot(2 + k // 4, 4)[:, k % 4, (g - H) * HD:(g - H + 1) * HD], hq
                        last = mm(PB[g % 2][:, 0:T], w, h[:, k, :], start=(k == 0), stop=(k == KT - 1))
                    last.then_inc(kq_out, 1)
                if 1 <= g <= 2 * H:
                    pe.wait_ge(kq_sq, g)
                    if g >= 2:
                        pe.wait_ge(kq_rms, g - 1)
                    mm(PB[2][:, 0:T], ones, sqh[:, (g - 1) % 2, :], start=True, stop=True).then_inc(kq_ss, 1)
                if 2 <= g < 2 * H + 2:
                    pe.wait_ge(kq_normed, g - 1)
                    if g >= 3:
                        pe.wait_ge(kq_made, g - 2)
                    mm(PB[3][0:ROT, 0:T], const("rot"), kq[:, g - 2, :], start=True, stop=True).then_inc(kq_rot, 1)
                if 3 <= g < H + 3:
                    pe.wait_ge(kq_made, g - 2)
                    rows(g - 3, kq[:, g - 3, :], None)
            for v in range(H + 1):
                if v < H:
                    if v >= 2:
                        pe.wait_ge(vp_kept, 2 * (v - 1))
                    for k in range(KT):
                        last = mm(PB[v % 2][:, 0:T], slot(4 + k // 2, 2)[:, k % 2, D + v * HD:D + (v + 1) * HD], hk[:, k, :],
                                  start=(k == 0), stop=(k == KT - 1))
                    last.then_inc(vp_out, 1)
                if v >= 1:
                    pe.wait_ge(vp_kept, 2 * v - 1)
                    g = H + v - 1
                    if g % 4 == 0:
                        pe.wait_ge(rows_kept, 3 * (g // 4))
                    for t, (t0, n) in enumerate(TILES):
                        last = tr(PB[4 + t][0:n, (g % 4) * P:(g % 4 + 1) * P], vTh[:, (v - 1) % 2, t0:t0 + n], ident)
                    last.then_inc(v_rows_out, 1)
                    if g % 4 == 3:
                        pe.wait_ge(v_rows_out, v)
                        pe.sem_inc(rows_out, 1)
            pe.wait_ge(own_in, 1)
            mm(PB[3][:, 0:H * NS], ones, ownp.rearrange("p h s -> p (h s)"), start=True, stop=True).then_inc(own_out, 1)

            pe.wait_ge(vp_kept, 2 * H)
            pe.wait_ge(rows_kept, 12)
            pe.wait_ge(own_made, 1)
            for s in range(NS + 1):
                c = (s - 1) % 2
                if s < NS:
                    if s >= 1:
                        pe.wait_ge(s_made, s)
                    for h in range(H):
                        last = mm(PB[6 + h // 4][:, (h % 4) * P:(h % 4 + 1) * P],
                                  bc(kq[:, H + h, NP_TOK + s:NP_TOK + s + 1], [P, P]), ident, start=True, stop=True)
                    last.then_inc(qb_out, 1)
                if s >= 1:
                    pe.wait_ge(s_made, s)
                    if s >= 2:
                        pe.wait_ge(att_made, s - 1)
                    mm(PB[3][:, 64:128], ones, sc[:, c, 0:NPAGE, :].rearrange("p g h -> p (g h)"), start=True, stop=True)\
                        .then_inc(gs_out, 1)
                if s < NS:
                    if s >= 1:
                        pe.wait_ge(ps_max, s)
                    mm(PB[0][:, 0:P], kq[:, H + s, 0:P], kq[:, s, 0:P], start=True, stop=True)
                    mm(PB[0][:, P:3 * P], kq[:, H + s, P:2 * P], kq[:, s, 0:2 * P], start=True, stop=True).then_inc(ps_out, 1)
                if s >= 1:
                    pe.wait_ge(pm_made, s)
                    tr(PB[5][0:H, 128:256], pmx, ident).then_inc(pm_turned, 1)
                    pe.wait_ge(dg_made, s)
                    mm(PB[3][:, 256:264], ones[0:H, :], dg[0:H, :], start=True, stop=True).then_inc(mb_out, 1)
                if s < NS:
                    pe.wait_ge(ps_norm, s + 1)
                    if s >= 1:
                        pe.wait_ge(pT_made, s)
                    for b in range(3):
                        last = tr(PB[1][:, b * P:(b + 1) * P], p3[:, b * P:(b + 1) * P], ident)
                    last.then_inc(pT_out, 1)
                if s >= 1:
                    pe.wait_ge(rs_made, s)
                    mm(PB[5][:, 264:272], ones, rsum, start=True, stop=True).then_inc(den_out, 1)
                    v_slot = 4 * c + 2
                    if s >= 2:
                        pe.wait_ge(ov_made, s - 1)
                    for g in range(NPAGE):
                        if g % 4 == 0:
                            arrived(pe, "seqs", v_slot + g // 4, (s - 1) // 2 + 1, 64)
                        for half in range(2):
                            q = 2 * (g % 2) + half
                            last = mm(PB[4][32 * q:32 * q + 32, :], pe4[:, c, g, :],
                                      W[:, v_slot + g // 4, (g % 4) * D + 512 * half:(g % 4) * D + 512 * (half + 1)],
                                      start=(g < 2), stop=(g >= NPAGE - 2), tile_position=(0, 32 * q))
                    last.then_inc(pv_out, 1)
                if s < NS:
                    pe.wait_ge(pT_made, s + 1)
                    if s >= 1:
                        pe.wait_ge(po_kept, s)
                    mm(PB[2][:, 0:2 * P], vrows[:, 0, s * HD:(s + 1) * HD], pT3[:, 0:2 * P], start=True, stop=False)
                    mm(PB[2][:, P:2 * P], vrows[:, 1, s * HD:(s + 1) * HD], pT3[:, 2 * P:3 * P], start=False, stop=True)\
                        .then_inc(po_out, 1)
                if s >= 1:
                    pe.wait_ge(ov_made, s)
                    for b in range(4):
                        last = mm(PB[3][:, 272 + b:272 + b + 5:4], ov[:, b * P:(b + 1) * P],
                                  const("pick").rearrange("p (b n) -> p b n", n=2)[:, b, :], start=True, stop=True)
                    last.then_inc(o_out, 1)
            pe.wait_ge(att_made, NS)
            pe.wait_ge(po_kept, NS)
            for j in range(KT):
                if j >= 2:
                    pe.wait_ge(wo_added, j - 1)
                for h in range(H):
                    if j == 0 and h % 4 == 0:
                        arrived(pe, "wo", 2 + h // 4)
                    last = mm(PB[j % 2][:, 0:T], slot(2 + h // 4, 4)[:, h % 4, j:D:KT], aT[:, h, :],
                              start=(h == 0), stop=(h == H - 1))
                last.then_inc(wo_out, 1)
            sum_squares(3, sqM)
            moe(1, 3, 5 * KT)
            pe.wait_ge(moe_done, 2)
            for i in range(6):
                t, half = divmod(i, 2)
                t0, n = TILES[t]
                if i >= 4:
                    pe.wait_ge(yr_made, i - 3)
                for q in range(4):
                    last = tr(PB[i % 4][0:n, q * P:(q + 1) * P], xT[:, 4 * half + q, t0:t0 + n], ident)
                last.then_inc(y_turned, 1)

        @block.vector
        def _(dve):
            v = nc.vector
            steps = Chain(dve, vec)
            link, ran, settle = steps.link, steps.ran, steps.wait

            v.memset(eps[:, :], EPS).then_inc(eps_set, 1)
            link(v.memset(mv, 1.0))
            for k in range(KT):
                dve.wait_ge(x_turned, k + 1)
                v.tensor_copy(xT[:, k, :], PB[k % 2][:, 0:T]).then_inc(x_kept, 1)
            for half in range(2):
                dve.wait_ge(ws_turned, half + 1)
                v.tensor_copy(wsT[:, 4 * half:4 * half + 4, :], PB[4 + half][:, :].rearrange("p (g t) -> p g t", g=4))\
                    .then_inc(ws_kept, 1)
            dve.wait_ge(w00_out, 1)
            dve.wait_ge(c_load, 16)
            link(v.tensor_copy(rstd[0:NS, 0:NG], PB[6][0:NS, 0:NG]))
            v.tensor_tensor(d8[0:NS], bc(ident[0:NS, 0:NS].unsqueeze(1), [NS, NG, NS]),
                            bc(rstd[0:NS, 0:NG].unsqueeze(2), [NS, NG, NS]), ALU.mult).then_inc(d8_made, 1)
            dve.wait_ge(bs_load, 16)
            v.tensor_copy(b00[0:1], bc(bs[0:1, :, 0:1], [1, NG, NS])).then_inc(d8_made, 1)
            dve.wait_ge(d8_made, 2)
            dve.wait_ge(g_load, 16 * 11)

            def normed(n, targets):
                dve.wait_ge(rms_made, n + 1)
                v.reciprocal(rstd[:, :], rms[:, :]).then_inc(rstd_made, 1)
                dve.wait_ge(rstd_made, n + 1)
                for dst, g in targets:
                    for k in range(KT):
                        v.scalar_tensor_tensor(out=dst[:, k, :], in0=xT[:, k, :], scalar=gains[:, g, k:k + 1],
                                               in1=rstd[:, :], op0=ALU.mult, op1=ALU.mult).then_inc(h_made, 1)
            dve.wait_ge(x_kept, KT)
            normed(0, [(hT, G_A)])

            dve.wait_ge(wr_made, 4)
            for b in range(4):
                dve.wait_ge(v_turned, b + 1)
                for t, (_, n) in enumerate(TILES):
                    v.tensor_copy(vr[0:n, t, 512 * b:512 * (b + 1)], PB[4 + t][0:n, :]).then_inc(v_kept, 1)
                    v.bn_stats(stats[0:n, t, 6 * b:6 * b + 6], PB[4 + t][0:n, :]).then_inc(v_kept, 1)
            dve.wait_ge(v_kept, 24)
            for t, (_, n) in enumerate(TILES):
                ran(v.bn_aggr(mv[0:n, t, :], stats[0:n, t, :]))
            settle()
            v.sem_inc(mv_made, 1)
            dve.wait_ge(vsd_made, 1)
            link(v.reciprocal(vrstd, vrstd))
            for b in range(4):
                dve.wait_ge(ln_load, 32 * (b + 1))
                for t, (_, n) in enumerate(TILES):
                    part = vr[0:n, t, 512 * b:512 * (b + 1)]
                    ran(v.tensor_scalar(part, part, mv[0:n, t, 0:1], vrstd[0:n, t:t + 1], ALU.subtract, ALU.mult))
                settle()
                for i, op in ((0, ALU.mult), (1, ALU.add)):
                    for t, (_, n) in enumerate(TILES):
                        part = vr[0:n, t, 512 * b:512 * (b + 1)]
                        ran(v.tensor_tensor(part, part, lng[0:n, i, :], op))
                    settle()
                v.sem_inc(ln_used, 1)
            v.sem_inc(ln_done, 1)
            for c in range(CT):
                dve.wait_ge(mix_out, c + 1)
                dve.wait_ge(u_gelu, c + 1)
                v.tensor_tensor(vT[:, c, :], vT[:, c, :], PB[4 + c % 2][:, 0:T], ALU.mult).then_inc(um_made, 1)
            for j in range(KT):
                dve.wait_ge(a_out, j + 1)
                v.tensor_tensor(xT[:, j, :], xT[:, j, :], PB[j % 2][:, 0:T], ALU.add).then_inc(a_added, 1)
            dve.wait_ge(a_added, KT)

            def moe(l):
                link(v.memset(lg, 0.0))
                dve.wait_ge(lg_out, l + 1)
                ran(v.tensor_copy(lg[:, 0:2, :], PB[2][:, 0:40].rearrange("p (t n) -> p t n", t=2)))
                link(v.tensor_copy(lg[0:NS, 2, :], PB[2][0:NS, 40:60]))
                lgg = lg[:, :, 0:NGRP]
                s34 = [P, 3, 4]
                firsts = bc(const("first").unsqueeze(1), s34)

                def wide(x):
                    return bc(x.unsqueeze(2), s34)

                def argmax(x, top, onehot):
                    link(v.tensor_reduce(top, x, AX.X, ALU.max))
                    link(v.tensor_tensor(cand, x, wide(top), ALU.is_equal))
                    link(v.tensor_tensor(cand, cand, firsts, ALU.mult))
                    link(v.tensor_reduce(mn, cand, AX.X, ALU.min))
                    link(v.tensor_tensor(onehot, cand, wide(mn), ALU.is_equal))
                argmax(lgg, gm, ohg)
                link(v.tensor_tensor(ex, lgg, wide(gm), ALU.subtract))
                v.sem_inc(soft_in, 1)
                link(v.tensor_tensor(prod.rearrange("p t (j g) -> p t j g", g=4),
                                     lg[:, :, NGRP:].rearrange("p t (g j) -> p t j g", g=4),
                                     bc(ohg.unsqueeze(2), [P, 3, 4, 4]), ALU.mult))
                link(v.tensor_reduce(leg, prod.rearrange("p t (j g) -> p t j g", g=4), AX.X, ALU.add))
                argmax(leg, m1, oh1)
                link(v.scalar_tensor_tensor(out=le2, in0=oh1, scalar=-3e38, in1=leg, op0=ALU.mult, op1=ALU.add))
                argmax(le2, m2, oh2)
                link(v.tensor_tensor(e2, m2, m1, ALU.subtract))
                v.sem_inc(soft_in, 1)
                link(v.tensor_tensor(cand, oh1, oh2, ALU.add))
                g44 = [P, 3, 4, 4]
                link(v.tensor_tensor(chose.rearrange("p t (g j) -> p t g j", g=4), bc(ohg.unsqueeze(3), g44),
                                     bc(cand.unsqueeze(2), g44), ALU.mult))
                v.tensor_tensor(chose, chose, bc(const("valid").unsqueeze(2), [P, 3, 16]), ALU.mult)\
                    .then_inc(chose_made, 1)
                dve.wait_ge(soft_out, 2 * l + 2)
                link(v.tensor_reduce(pg, ex, AX.X, ALU.add))
                link(v.reciprocal(pg, pg))
                link(v.tensor_scalar(w1, e2, 1.0, None, ALU.add))
                link(v.reciprocal(w1, w1))
                link(v.tensor_tensor(w1, w1, pg, ALU.mult))
                link(v.tensor_tensor(w2, e2, w1, ALU.mult))
                link(v.tensor_tensor(oh1, oh1, wide(w1), ALU.mult))
                link(v.tensor_tensor(oh2, oh2, wide(w2), ALU.mult))
                link(v.tensor_tensor(oh1, oh1, oh2, ALU.add))
                link(v.tensor_tensor(gates.rearrange("p t (g j) -> p t g j", g=4), bc(ohg.unsqueeze(3), g44),
                                     bc(oh1.unsqueeze(2), g44), ALU.mult))
                dve.wait_ge(chose_made, l + 1)
                dve.wait_ge(rank_out, l + 1)
                ran(v.tensor_reduce(cmax, PB[2][:, 112:128], AX.X, ALU.max))
                link(v.scalar_tensor_tensor(out=rank, in0=PB[2][:, 64:112].rearrange("p (t e) -> p t e", t=3), scalar=1.0,
                                            in1=chose, op0=ALU.add, op1=ALU.mult))
                link(v.tensor_scalar(rank, rank, -1.0, None, ALU.add))
                link(v.tensor_copy(many[:, :], cmax[0:1, :]))
                v.sem_inc(many_set, 1)
                flag = dve.value_load(many[0:1, 0:1], min_val=0, max_val=T)
                with dve.If(flag > LIMIT):
                    own_steps = Chain(dve, vecD[l])
                    dve.wait_ge(hr_kept, 6 * l + 6)
                    def all_tokens(i):
                        own_steps.base, own_steps.n = i * (2 * FT), 0
                        for e in range(2):
                            wait_for(dve, gcol_out[l], i * 2 + e)
                            v.tensor_copy(gb, bc(gates[:, :, bass.ds(2 * i + e, 1)], [P, 3, P])).then_inc(gb_made[l], 1)
                            dve.wait_ge(gcol_out[l], i * 2 + e + 1)
                            wait_for(dve, hD_made[l], i * (2 * FT) + e * FT)
                            v.tensor_copy(gcol, PB[7][:, 0:T]).then_inc(gcol_made[l], 1)
                            dve.wait_ge(gcol_made[l], i * 2 + e + 1)
                            wait_for(dve, yD_out[l], i * (2 * KT) + e * KT)
                            for f in range(FT):
                                dve.wait_ge(sD_made[l], i * (2 * FT) + e * FT + f + 1)
                                own_steps.link(v.tensor_tensor(heD[:, f, :], sgD, PB[2 + f % 2][:, 0:T], ALU.mult))
                                v.tensor_tensor(heD[:, f, :], heD[:, f, :], gcol, ALU.mult).then_inc(hD_made[l], 1)
                            for j in range(KT):
                                dve.wait_ge(yD_out[l], i * (2 * KT) + e * KT + j + 1)
                                wait_for(dve, yD_added[l], i * (2 * KT) + e * KT + j)
                                v.tensor_tensor(xT[:, j, :], xT[:, j, :], PB[4 + j % 2][:, 0:T], ALU.add)\
                                    .then_inc(yD_added[l], 1)
                    all_tokens(0)
                    with dve.Fori(1, NPAIR) as i:
                        all_tokens(i)
                    dve.wait_ge(yD_added[l], NE * KT)
                    v.sem_inc(moe_done, 1)
                with dve.Else():
                    def onehot(i):
                        v.tensor_tensor(hot, bc(const("iota").unsqueeze(1).unsqueeze(1), [P, 3, 2, CAP]),
                                        bc(rank[:, :, bass.ds(2 * i, 2)].unsqueeze(3), [P, 3, 2, CAP]), ALU.is_equal)\
                            .then_inc(hot_made[l], 1)

                    def copy_hg(i):
                        dve.wait_ge(gather_out[l], i + 1)
                        v.tensor_copy(hg[:, 4:8, :], PB[1][:, :].rearrange("p (k s) -> p k s", k=4)).then_inc(hg_hi[l], 1)

                    def add_y(i):
                        for j in range(KT):
                            dve.wait_ge(y_out[l], i * KT + j + 1)
                            v.tensor_tensor(xT[:, j, :], xT[:, j, :], PB[6 + j % 2][:, 0:T], ALU.add).then_inc(y_added[l], 1)

                    def pair(i, first, last):
                        dve.wait_ge(silu_made[l], i + 1)
                        dve.wait_ge(up_out[l], i + 1)
                        v.tensor_tensor(he, sg, PB[3][:, :], ALU.mult).then_inc(he_made[l], 1)
                        if not first:
                            add_y(i - 1)
                        if not last:
                            copy_hg(i + 1)
                        dve.wait_ge(sT_out[l], i + 1)
                        v.tensor_copy(sT, PB[7][:, 0:T]).then_inc(sT_made[l], 1)
                        if not last:
                            if not isinstance(i, int) or i < NPAIR - 2:
                                dve.wait_ge(ghot_made[l], i + 2)
                                onehot(i + 2)
                        dve.wait_ge(down_out[l], i + 1)
                        v.tensor_copy(dr[:, 512:D], PB[5][:, :]).then_inc(dr_hi[l], 1)
                    onehot(0)
                    copy_hg(0)
                    dve.wait_ge(ghot_made[l], 1)
                    onehot(1)
                    pair(0, True, False)
                    with dve.Fori(1, NPAIR - 2) as i:
                        pair(i, False, False)
                    pair(NPAIR - 2, False, False)
                    pair(NPAIR - 1, False, True)
                    add_y(NPAIR - 1)
                    dve.wait_ge(y_added[l], NPAIR * KT)
                    v.sem_inc(moe_done, 1)
                dve.nop()

            normed(1, [(hT, G_M)])
            moe(0)
            dve.wait_ge(moe_done, 1)
            normed(2, [(hk, G_KV), (hq, G_B)])
            dve.wait_ge(sq_made, 6)

            for g in range(2 * H + 2):
                if g < 2 * H:
                    dve.wait_ge(kq_rms, g + 1)
                    link(v.reciprocal(rsh, rmh))
                    v.scalar_tensor_tensor(out=kq[:, g, :], in0=PB[g % 2][:, 0:T], scalar=hgain[:, g // H:g // H + 1],
                                           in1=rsh, op0=ALU.mult, op1=ALU.mult).then_inc(kq_normed, 1)
                    dve.wait_ge(kq_normed, g + 1)
                if g >= 1 and g <= 2 * H:
                    dve.wait_ge(kq_rot, g)
                    rot = kq[0:ROT, g - 1, :]
                    ran(v.tensor_tensor(turned[0:ROT, :], PB[3][0:ROT, 0:T], const("sin")[0:ROT, :], ALU.mult))
                    link(v.tensor_tensor(rot, rot, const("cos")[0:ROT, :], ALU.mult))
                    v.tensor_tensor(rot, rot, turned[0:ROT, :], ALU.add).then_inc(kq_made, 1)
                    dve.wait_ge(kq_made, g)
            v.tensor_tensor(ownp, kq[:, 0:H, NP_TOK:T], kq[:, H:2 * H, NP_TOK:T], ALU.mult).then_inc(own_in, 1)
            dve.wait_ge(own_out, 1)
            v.tensor_copy(own.rearrange("p h s -> p (h s)"), PB[3][:, 0:H * NS]).then_inc(own_made, 1)
            dve.wait_ge(own_made, 1)
            dve.wait_ge(pad_set, 1)

            def keys(s, g):
                c = s % 2
                k_slot = 4 * c + g // 4
                if g % 4 == 0:
                    arrived(dve, "seqs", k_slot, s // 2 + 1, 64)
                for h in range(H):
                    kb = W[:, k_slot, (g % 4) * D + h * HD:(g % 4) * D + (h + 1) * HD]
                    last = v.tensor_tensor_reduce(kb, kb, PB[6 + h // 4][:, (h % 4) * P:(h % 4 + 1) * P], 1.0, 0.0,
                                                  ALU.mult, ALU.add, sc[:, c, g, h:h + 1])
                if g == 3:
                    last.then_inc(k_used, 1)
                if g == NPAGE - 1:
                    last.then_inc(k_used, 1)
                    dve.wait_ge(k_used, 2 * (s + 1))
                    v.sem_inc(s_made, 1)

            for s in range(NS + 1):
                c = (s - 1) % 2
                scp = sc[:, c, 0:NPAGE, :]

                def prompt_max():
                    dve.wait_ge(ps_out, s + 1)
                    if s:
                        dve.wait_ge(ps_exp, 2 * s)
                    link(v.tensor_tensor(s3, PB[0][:, 0:3 * P], const("causal"), ALU.add))
                    ran(v.tensor_reduce(mx3[:, 0:1], s3[:, 0:P], AX.X, ALU.max))
                    link(v.tensor_reduce(mx3[:, 1:2], s3[:, P:3 * P], AX.X, ALU.max))
                    if s:
                        dve.wait_ge(pT_out, s)
                    v.tensor_scalar(mx3, mx3, -SCALE, None, ALU.mult).then_inc(ps_max, 1)

                def blocks():
                    dve.wait_ge(gs_out, s)
                    link(v.tensor_reduce(gsum, PB[3][:, 64:128].rearrange("p (b g h) -> p b h g", b=NBLK, g=2),
                                         AX.X, ALU.add))
                    link(v.tensor_reduce(mnb, gsum.rearrange("p b h -> p h b"), AX.X, ALU.min))
                    link(v.tensor_tensor(eqb, gsum, bc(mnb.unsqueeze(1), [P, NBLK, H]), ALU.is_equal))
                    link(v.tensor_tensor(eqb, eqb, bc(const("blk").unsqueeze(2), [P, NBLK, H]), ALU.mult))
                    link(v.tensor_reduce(vmb, eqb.rearrange("p b h -> p h b"), AX.X, ALU.max))
                    link(v.tensor_tensor(drop, eqb, bc(vmb.unsqueeze(1), [P, NBLK, H]), ALU.is_equal))
                    for g in range(2):
                        half = scp.rearrange("p (b g) h -> p b g h", g=2)[:, :, g, :]
                        ran(v.scalar_tensor_tensor(out=half, in0=drop, scalar=NEG, in1=half, op0=ALU.mult, op1=ALU.add))
                    settle()
                    v.tensor_reduce(pmx, scp.rearrange("p g h -> p h g"), AX.X, ALU.max).then_inc(pm_made, 1)

                def maxima():
                    dve.wait_ge(pm_turned, s)
                    link(v.tensor_reduce(hm[0:H, :], PB[5][0:H, 128:256], AX.X, ALU.max))
                    v.tensor_scalar(dg[0:H, :], ident[0:H, 0:H], hm[0:H, 0:1], None, ALU.mult).then_inc(dg_made, 1)

                def shift():
                    dve.wait_ge(mb_out, s)
                    mine = own[:, :, s - 1]
                    link(v.tensor_tensor(mall, PB[3][:, 256:264], mine, ALU.max))
                    ran(v.tensor_tensor(sc[:, c, NPAGE, :], mine, mall, ALU.subtract))
                    ran(v.tensor_tensor(scp, scp, bc(mall.unsqueeze(1), [P, NPAGE, H]), ALU.subtract))
                    settle()
                    v.sem_inc(sc_made, 1)

                def prompt_norm():
                    dve.wait_ge(ps_exp, 2 * (s + 1))
                    link(v.reciprocal(ri3, rs3))
                    ran(v.tensor_scalar(p3[:, 0:P], p3[:, 0:P], ri3[:, 0:1], None, ALU.mult))
                    ran(v.tensor_scalar(p3[:, P:3 * P], p3[:, P:3 * P], ri3[:, 1:2], None, ALU.mult))
                    settle()
                    v.sem_inc(ps_norm, 1)

                def row_sums():
                    dve.wait_ge(se_made, s)
                    v.tensor_reduce(rsum, pe4[:, c, 0:NPAGE, 0:H].rearrange("p g h -> p h g"), AX.X, ALU.add)\
                        .then_inc(rs_made, 1)

                def denominators():
                    dve.wait_ge(den_out, s)
                    link(v.tensor_tensor(den, PB[5][:, 264:272], pe4[:, c, NPAGE, 0:H], ALU.add))
                    link(v.reciprocal(rden, den))
                    link(v.tensor_tensor(tmp8, vTs[:, :, s - 1], pe4[:, c, NPAGE, 0:H], ALU.mult))

                def result():
                    dve.wait_ge(o_out, s)
                    link(v.tensor_tensor(tmp8, tmp8, PB[3][:, 272:280], ALU.add))
                    v.tensor_tensor(aT[:, :, NP_TOK + s - 1], tmp8, rden, ALU.mult).then_inc(att_made, 1)
                    dve.wait_ge(att_made, s)

                after = {0: [prompt_max] if s < NS else [], 1: [blocks], 2: [maxima], 3: [shift],
                         4: [prompt_norm] if s < NS else [], 5: [row_sums], 6: [denominators], 7: [result]}
                if s < NS:
                    dve.wait_ge(qb_out, s + 1)
                for g in range(NPAGE):
                    if s < NS:
                        keys(s, g)
                    for part in after[g]:
                        if part in (prompt_max, prompt_norm) or s >= 1:
                            part()
            for j in range(KT):
                dve.wait_ge(wo_out, j + 1)
                v.tensor_tensor(xT[:, j, :], xT[:, j, :], PB[j % 2][:, 0:T], ALU.add).then_inc(wo_added, 1)
            dve.wait_ge(wo_added, KT)
            normed(3, [(hT, G_M + 1)])
            moe(1)
            for i in range(6):
                t, half = divmod(i, 2)
                n = TILES[t][1]
                dve.wait_ge(y_turned, i + 1)
                v.tensor_copy(yr[0:n, t, :].rearrange("q (p k) -> q k p", k=KT)[:, 4 * half:4 * half + 4, :],
                              PB[i % 4][0:n, :].rearrange("q (k p) -> q k p", k=4)).then_inc(yr_made, 1)


_OUTS = [("y_prompt", (1, 256, 1024)), ("y_sample", (8, 1, 1024)), ("v_rows_prompt", (1, 1, 128, 2048)),
         ("v_rows_sample", (1, 8, 1, 2048)), ("k_prompt", (1, 256, 8, 128)), ("v_prompt", (1, 256, 8, 128)),
         ("k_sample", (8, 1, 8, 128)), ("v_sample", (8, 1, 8, 128))]


def kernel(**inputs):
    import numpy as np
    import concourse.bacc as bacc
    from concourse.bass_utils import run_bass_kernel_spmd

    nc = bacc.Bacc("TRN2", target_bir_lowering=False, num_devices=1)
    arrays, a, o = {}, {}, {}
    for name, value in {**inputs, "consts": constants()}.items():
        value = np.ascontiguousarray(value)
        arrays["in_" + name] = value
        a[name] = nc.dram_tensor("in_" + name, value.shape, mybir.dt.from_np(value.dtype), kind="ExternalInput").ap()
    for name, shape in _OUTS:
        o[name] = nc.dram_tensor("out_" + name, shape, F32, kind="ExternalOutput").ap()
    program(nc, a, o)
    r = run_bass_kernel_spmd(nc, [arrays], core_ids=[0])
    return tuple(r.results[0]["out_" + name] for name, _ in _OUTS)
```

```python
from contextlib import ExitStack

import concourse.bass as bass
from concourse import mybir

F32, I32 = mybir.dt.float32, mybir.dt.int32
ACT, ALU, AX = mybir.ActivationFunctionType, mybir.AluOpType, mybir.AxisListType

P = 128
D = 1024
KT = D // P
NP_TOK, NS = 256, 8
T = NP_TOK + NS
TILES = [(0, P), (P, P), (2 * P, NS)]
GW = 2 * D
CT = GW // P
NG = 8
H, HD = 8, 128
ROT = HD // 4
V_HEADS = [tuple(range(H))] + [()] * NS
PROMPT_HEADS = [(), (0,), (1,), (2,), (3,), (4,), (5,), (6, 7), ()]
NE, NPAIR, EF = 16, 8, 512
FT = EF // P
NGRP, EPG = 4, 4
NPAGE, PAGE, NBLK = 8, 128, 4
CAP = 64
LIMIT = CAP
EPS = 1e-6
SCALE = HD ** -0.5
NEG = -1e30
SMALL_LOADS = 15
SLOT = 4096


def const_layout():
    at, off = {}, 0
    for name, n in [("ident", P), ("ones", P), ("earlier", P), ("causal", 3 * P), ("iota", CAP), ("rot", ROT),
                    ("cos", T), ("sin", T), ("pick", 2 * NBLK), ("first", EPG), ("blk", NBLK), ("valid", 3)]:
        at[name] = (off, n)
        off += n
    return at, off


def constants():
    import numpy as np
    at, n = const_layout()
    c = np.zeros((P, n), np.float32)

    def put(name, value):
        o, w = at[name]
        c[:value.shape[0], o:o + w] = value.reshape(value.shape[0], w)
    i = np.arange(P)
    put("ident", np.eye(P))
    put("ones", np.ones((P, P)))
    put("earlier", i[:, None] < i[None, :])
    m = np.where(i[:, None] >= i[None, :], 0.0, NEG)
    put("causal", np.concatenate([m, np.zeros((P, P)), m], 1))
    put("iota", np.tile(np.arange(CAP), (P, 1)))
    r = np.zeros((P, ROT))
    half = ROT // 2
    for j in range(half):
        r[j + half, j], r[j, j + half] = -1.0, 1.0
    put("rot", r)
    freq = (500000.0 ** (-np.arange(half, dtype=np.float32) / half)).astype(np.float32)
    pos = np.concatenate([np.arange(NP_TOK), np.full(NS, NPAGE * PAGE)]).astype(np.float32)
    ang = (np.tile(freq, 2)[:, None] * pos[None]).astype(np.float32).astype(np.float64)
    put("cos", np.cos(ang))
    put("sin", np.sin(ang))
    s = np.zeros((P, NBLK, 2))
    for h in range(H):
        for parity in range(2):
            s[32 * (2 * parity + h // 4) + h, h % 4, h // 4] = 1.0
    put("pick", s)
    put("first", np.tile(np.arange(EPG) - 9.0, (P, 1)))
    put("blk", np.tile(np.arange(NBLK) + 1.0, (P, 1)))
    v = np.ones((P, 3))
    v[NS:, 2] = 0.0
    put("valid", v)
    return c


class Chain:

    def __init__(self, eng, sem):
        self.eng, self.sem, self.base, self.n = eng, sem, 0, 0

    def ran(self, ins):
        self.n += 1
        return ins.then_inc(self.sem, 1)

    def wait(self):
        self.eng.wait_ge(self.sem, self.base + self.n)

    def link(self, ins):
        self.ran(ins)
        self.wait()


def wait_for(eng, sem, n):
    if not isinstance(n, int) or n > 0:
        eng.wait_ge(sem, n)


def bc(ap, shape):
    return ap.to_broadcast(list(shape))


def program(nc, a, o):
    ctx = ExitStack()
    with ctx:
        def sb(name, shape, dt=F32):
            return ctx.enter_context(nc.sbuf_tensor(name, list(shape), dt))

        def sem(name):
            return ctx.enter_context(nc.semaphore(name))

        W = sb("ring", [P, 8, SLOT])
        xT = sb("xT", [P, KT, T])
        CL, CN = const_layout()
        C = sb("consts", [P, CN])

        def const(name):
            off, n = CL[name]
            return C[:, off:off + n]
        ident, ones, earlier = const("ident"), const("ones"), const("earlier")
        gains = sb("gains", [P, 5, KT])
        G_A, G_M, G_KV, G_B = 0, 1, 3, 4
        hgain = sb("hgain", [P, 2])
        wr = sb("wr", [P, 2, KT, NGRP + NE])
        rbias = sb("rbias", [NGRP + NE, 2])
        eps = sb("eps", [P, 1])
        table_used = sb("table_used", [P, 1])
        rms = sb("rms", [P, T])
        rstd = sb("rstd", [P, T])
        pages = sb("pages", [1, NS * NPAGE], I32)
        many = sb("many", [P, 1], I32)

        ARENA = 15920
        A = sb("arena", [P, ARENA])

        def region(off, *shape):
            n = 1
            for s in shape:
                n *= s
            assert off + n <= ARENA, (off, n)
            v = A[:, off:off + n]
            if len(shape) == 1:
                return v
            names = "abc"[:len(shape)]
            return v.rearrange(f"p ({' '.join(names)}) -> p {' '.join(names)}", **dict(zip(names, shape)))
        hT = region(0, KT, T)
        vT = region(2112, CT, T)
        vr = region(6336, 3, GW)
        lng = region(12480, 2, 512)
        wsT = region(13504, NG, P)
        bs = region(14528, NG, P)
        xr = region(6336, 3, D)
        wsr = region(2112 + 12 * T, NG, P)
        sqA = region(2112, KT, T)
        raw_g = [region(12480 + l * KT * NGRP, KT, NGRP) for l in range(2)]
        raw_e = [region(12544 + l * KT * NE, KT, NE) for l in range(2)]
        w00 = region(15768, NG)
        b00 = region(15552, NG, NS)
        d8 = region(15616, NG, NS)
        stats = region(15680, 3, 4 * 6)
        mv = region(15752, 3, 2)
        vrstd = region(15758, 3)
        hr = region(2112, 3, D)
        sqM = region(5184, KT, T)
        hot = region(7296, 3, 2, CAP)
        ghot = region(7680, 3, 2, CAP)
        sT = region(8064, T)
        hg = region(8328, KT, P)
        sg = region(9352, EF)
        he = region(9864, EF)
        heT = region(10376, FT, P)
        dr = region(10888, D)
        lgT = region(11912, T)
        lg = region(12176, 3, NGRP + NE)
        ro = 12236

        def small(*shape):
            nonlocal ro
            n = 1
            for s in shape:
                n *= s
            ro += n
            return region(ro - n, *shape)
        gm, pg, mn, m1, m2, e2, w1, w2 = (small(3) for _ in range(8))
        ohg, oh1, oh2, leg, le2, cand, ex = (small(3, 4) for _ in range(7))
        prod = small(3, 16)
        gates = small(3, 16)
        chose = small(3, 16)
        rank = small(3, 16)
        sgD = region(2112, T)
        heD = region(2376, FT, T)
        gb = region(3432, 3, P)
        gcol = region(3816, T)
        hk, hq = region(0, KT, T), region(2112, KT, T)
        kq = region(4224, 2 * H, T)
        krows = region(8448, 3, D)
        vrows = region(11520, 3, D)
        sqB = region(8448, KT, T)
        sqh = region(14592, 2, T)
        rmh = region(15120, T)
        rsh = region(15384, T)
        turned = region(15648, T)
        vTh = region(14592, 2, T)
        vTs = region(15384, H, NS)
        own = region(15448, H, NS)
        ownp = region(15512, H, NS)
        own_w = region(15576, H, NS)
        aT = region(2112, H, T)
        s3 = region(8448, 3 * P)
        p3 = region(8832, 3 * P)
        pT3 = region(9216, 3 * P)
        mx3, rs3, ri3 = region(9600, 2), region(9602, 2), region(9604, 2)
        sc = region(9608, 2, NPAGE + 1, H)
        pe4 = region(9752, 2, NPAGE + 1, 32)
        ov = region(10328, 512)
        gsum, eqb, drop = region(10840, NBLK, H), region(10872, NBLK, H), region(10904, NBLK, H)
        mnb, vmb, pmx, mall, rsum, den, rden, tmp8 = (region(10936 + 8 * i, H) for i in range(8))
        dg = region(11000, H)
        hm = region(11008, 1)
        yr = region(2112, 3, D)

        PB = [ctx.enter_context(nc.psum_tensor(f"bank{i}", [P, 512], F32)) for i in range(8)]

        def acc(g):
            return PB[(0, 1, 7)[g % 3]]

        def v_acc(h):
            return PB[(h + 1) % 2]

        GATE0, UP0, DOWN0 = (4, 0), (6, 2), (0, 6)
        GATE, UP, DOWN = (2, 4), (4, 0), (6, 2)
        W_K, W_Q, W_V, W_O = 0, 2, 4, 4
        K_SLOT = [6, 2, 4, 2, 4, 2, 4, 2]
        V_SLOT = [0, 6, 0, 6, 0, 6, 0, 6]
        filled, before = [0] * 8, {}

        def stage(name, first, slots=2, each=16, times=1):
            before[name] = list(filled)
            for s in range(first, first + slots):
                filled[s] += each * times

        def expert_stages(l):
            for name, first in (("gate", GATE0), ("up", UP0), ("down", DOWN0)):
                stage(f"{name}0_{l}", first[l])
            for name, others in (("gate", GATE), ("up", UP), ("down", DOWN)):
                stage(f"{name}{l}", others[l], times=NPAIR - 1)
        stage("v", 0, 4)
        stage("u", 4, 4)
        stage("wout", 0, 4)
        expert_stages(0)
        stage("w_k", W_K)
        stage("w_q", W_Q)
        stage("w_v", W_V)
        for s in range(NS):
            stage(f"K{s}", K_SLOT[s], each=64)
            stage(f"V{s}", V_SLOT[s], each=64)
        stage("w_o", W_O)
        expert_stages(1)

        full = [sem(f"full{s}") for s in range(8)]

        def arrived(eng, name, slot, nth=1, each=16):
            eng.wait_ge(full[slot], before[name][slot] + each * nth)

        c_load, x_load, g_load, page_load = sem("c_load"), sem("x_load"), sem("g_load"), sem("page_load")
        ga_load, ws_load = sem("ga_load"), sem("ws_load")
        eps_set, wr_made, ws_masked = sem("eps_set"), sem("wr_made"), sem("ws_masked")
        ws_turned, ws_kept, d8_made = sem("ws_turned"), sem("ws_kept"), sem("d8_made")
        x_turned, x_kept = sem("x_turned"), sem("x_kept")
        sq_made, ss_out, rms_made, rstd_made, h_made = (sem(n) for n in
                                                        ["sq_made", "ss_out", "rms_made", "rstd_made", "h_made"])
        v_out, v_gelu, v_turned, v_kept = sem("v_out"), sem("v_gelu"), sem("v_turned"), sem("v_kept")
        mv_made, vsd_made, ln_load, ln_used, ln_done = (sem(n) for n in
                                                        ["mv_made", "vsd_made", "ln_load", "ln_used", "ln_done"])
        u_out, u_gelu, mix_out, um_made = sem("u_out"), sem("u_gelu"), sem("mix_out"), sem("um_made")
        a_out, a_added = sem("a_out"), sem("a_added")
        vec, v_rows_out, vec_own = sem("vector_steps"), sem("v_rows_out"), sem("own_weights_made")
        stored = sem("stored")
        L2 = range(2)

        def pair_of(name):
            return [sem(f"{name}{l}") for l in L2]
        lgT_out, lgT_made, lg_out, hr_out, hr_kept = (sem(n) for n in ["lgT_out", "lgT_made", "lg_out", "hr_out", "hr_kept"])
        gates_made = sem("gates_made")
        soft_in, soft_out, chose_made, rank_out, many_set, moe_done = (sem(n) for n in [
            "soft_in", "soft_out", "chose_made", "rank_out", "many_set", "moe_done"])
        gate_out, up_out, down_out = (pair_of(n) for n in ["gate_out", "up_out", "down_out"])
        hot_made, ghot_made, gather_out, hg_lo, hg_hi = (pair_of(n) for n in [
            "hot_made", "ghot_made", "gather_out", "hg_lo", "hg_hi"])
        silu_made, he_made, heT_out, heT_made = (pair_of(n) for n in ["silu_made", "he_made", "heT_out", "heT_made"])
        dr_lo, dr_hi, sT_out, sT_made, y_out, y_added = (pair_of(n) for n in [
            "dr_lo", "dr_hi", "sT_out", "sT_made", "y_out", "y_added"])
        gb_made, gcol_out, gcol_made, gD_out, sD_made, hD_made, yD_out, yD_added = (pair_of(n) for n in [
            "gb_made", "gcol_out", "gcol_made", "gD_out", "sD_made", "hD_made", "yD_out", "yD_added"])
        vecD = pair_of("vector_steps_all")
        kq_out, kq_sq, kq_ss, kq_rms, kq_normed, kq_rot, kq_made = (sem(n) for n in [
            "kq_out", "kq_sq", "kq_ss", "kq_rms", "kq_normed", "kq_rot", "kq_made"])
        vp_out, vp_kept, rows_out, rows_kept, v_rows_kept = (
            sem(n) for n in ["vp_out", "vp_kept", "rows_out", "rows_kept", "v_rows_kept"])
        own_in, own_out, own_made, k_stored, pad_set = (sem(n) for n in ["own_in", "own_out", "own_made", "k_stored", "pad_set"])
        ps_out, ps_max, ps_exp, ps_norm, pT_out, pT_made, po_out, po_kept = (sem(n) for n in [
            "ps_out", "ps_max", "ps_exp", "ps_norm", "pT_out", "pT_made", "po_out", "po_kept"])
        qb_out, s_made, gs_out, pm_made, pm_turned, dg_made, mb_out, sc_made, se_made, rs_made, den_out = (
            sem(n) for n in ["qb_out", "s_made", "gs_out", "pm_made", "pm_turned", "dg_made", "mb_out",
                             "sc_made", "se_made", "rs_made", "den_out"])
        pv_out, ov_made, o_out, att_made = sem("pv_out"), sem("ov_made"), sem("o_out"), sem("att_made")
        wo_out, wo_added = sem("wo_out"), sem("wo_added")
        y_turned, yr_made = sem("y_turned"), sem("yr_made")

        block = ctx.enter_context(nc.Block())

        def w_rows(ap, k):
            return ap.rearrange("(p k) n -> p k n", k=k)

        def slot(s, k):
            return W[:, s, :].rearrange("p (k n) -> p k n", k=k)

        @block.sync
        def _(sp):
            sp.dma_start(xr[:, 0:2, :], a["x_prompt"][0].rearrange("(t p) d -> p t d", p=P)).then_inc(x_load, 16)
            sp.dma_start(xr[0:NS, 2, :], a["x_sample"].rearrange("b s d -> (b s) d")).then_inc(x_load, 16)
            w_in = w_rows(a["a_w_in"][0], KT)
            for q in range(4):
                sp.dma_start(slot(q, 2), w_in[:, 2 * q:2 * q + 2, GW:2 * GW]).then_inc(full[q], 16)
            for q in range(4):
                sp.dma_start(slot(4 + q, 2), w_in[:, 2 * q:2 * q + 2, 0:GW]).then_inc(full[4 + q], 16)
            w_out = a["a_w_out"][0].rearrange("(c p) n -> p c n", p=P)
            sp.wait_ge(v_out, CT)
            for q in range(4):
                sp.dma_start(slot(q, 4), w_out[:, 4 * q:4 * q + 4, :]).then_inc(full[q], 16)

            def experts(layer):
                gate = a["moe_w_gate"][layer].rearrange("e (p k) n -> e p k n", k=KT)
                up = a["moe_w_up"][layer].rearrange("e (p k) n -> e p k n", k=KT)
                down = a["moe_w_down"][layer].rearrange("e (f p) n -> e p f n", p=P)

                def load(i, first, weights, k):
                    for e in range(2):
                        sp.dma_start(slot(first + e, k), weights[bass.ds(2 * i + e, 1)].rearrange("e p k n -> (e p) k n"))\
                            .then_inc(full[first + e], 16)

                load(0, GATE0[layer], gate, KT)
                if layer == 1:
                    sp.wait_ge(s_made, 2 * NS)
                load(0, UP0[layer], up, KT)
                if layer == 0:
                    sp.wait_ge(a_out, KT)
                else:
                    sp.wait_ge(pv_out, NS)
                load(0, DOWN0[layer], down, FT)
                if layer == 1:
                    sp.wait_ge(wo_out, KT)
                load(1, GATE[layer], gate, KT)
                sp.wait_ge(gate_out[layer], 1)
                load(1, UP[layer], up, KT)
                sp.wait_ge(up_out[layer], 1)
                load(1, DOWN[layer], down, FT)
                with sp.Fori(2, NPAIR) as i:
                    sp.wait_ge(gate_out[layer], i)
                    load(i, GATE[layer], gate, KT)
                    sp.wait_ge(up_out[layer], i)
                    load(i, UP[layer], up, KT)
                    sp.wait_ge(down_out[layer], i)
                    load(i, DOWN[layer], down, FT)

            sp.wait_ge(u_out, CT)
            experts(0)

            def load_square(w, first):
                for q in range(2):
                    sp.dma_start(slot(first + q, 4), w[:, 4 * q:4 * q + 4, :]).then_inc(full[first + q], 16)
            w_kv = w_rows(a["w_kv"], KT)
            load_square(w_kv[:, :, 0:D], W_K)
            sp.wait_ge(gate_out[0], NPAIR)
            load_square(w_rows(a["b_w_q"][0], KT), W_Q)
            sp.wait_ge(up_out[0], NPAIR)
            load_square(w_kv[:, :, D:2 * D], W_V)

            sp.wait_ge(page_load, 16)

            def load_pages(pool, s, first):
                for g in range(NPAGE):
                    page = sp.value_load(pages[0:1, s * NPAGE + g:s * NPAGE + g + 1],
                                         min_val=0, max_val=pool.shape[0] - 1)
                    sp.dma_start(W[:, first + g // 4, (g % 4) * D:(g % 4 + 1) * D],
                                 pool[bass.ds(page, 1)].rearrange("a p h d -> (a p) (h d)"))\
                        .then_inc(full[first + g // 4], 16)
            keys_free = [(down_out[0], NPAIR), (kq_out, 2 * H), (vp_out, H)] + [(s_made, 2 * (s - 1)) for s in range(3, NS)]
            values_free = [(kq_out, H), (s_made, 2)] + [(pv_out, s - 1) for s in range(2, NS)]
            for s in range(NS):
                sp.wait_ge(*keys_free[s])
                load_pages(a["cache_k"], s, K_SLOT[s])
                sp.wait_ge(*values_free[s])
                load_pages(a["cache_v"], s, V_SLOT[s])
            sp.wait_ge(s_made, 2 * (NS - 1))
            w_o = a["b_w_o"][0].rearrange("(h p) n -> p h n", p=P)
            load_square(w_o, W_O)
            sp.wait_ge(pv_out, NS - 1)
            experts(1)
            sp.wait_ge(stored, 16 * 7)
            sp.wait_ge(k_stored, 16 * 2)

        @block.gpsimd
        def _(pool):
            pool.wait_ge(ws_load, 16)
            nc.gpsimd.affine_select(out=wsr, in_=wsr, compare_op=ALU.is_ge, fill=0.0, base=0,
                                    pattern=[[0, NG], [-1, P]], channel_multiplier=1).then_inc(ws_masked, 1)
            pool.wait_ge(g_load, 16 * SMALL_LOADS)
            for l in L2:
                for src, lo, n in ((raw_g[l], 0, NGRP), (raw_e[l], NGRP, NE)):
                    nc.gpsimd.tensor_copy(wr[:, l, :, lo:lo + n], src).then_inc(wr_made, 1)
            for c in range(4):
                if c == 0:
                    pool.wait_ge(wr_made, 4)
                else:
                    pool.wait_ge(ln_used, c)
                for i, name in enumerate(("a_ln_g", "a_ln_b")):
                    pool.dma_start(lng[:, i, :], a[name][0:1, 512 * c:512 * (c + 1)].partition_broadcast(P))\
                        .then_inc(ln_load, 16)
            pool.wait_ge(ln_done, 1)
            pool.dma_start(o["v_rows_prompt"][0, 0], vr[:, 1, :]).then_inc(stored, 16)
            pool.dma_start(o["v_rows_sample"][0].rearrange("b s n -> (b s) n"), vr[0:NS, 2, :]).then_inc(stored, 16)

            def moe(l):
                pool.wait_ge(many_set, l + 1)
                flag = pool.value_load(many[P - 1:P, 0:1], min_val=0, max_val=T)
                with pool.If(flag > LIMIT):
                    pool.nop()
                with pool.Else():
                    def weigh(i):
                        if isinstance(i, int) and i == 0:
                            pool.wait_ge(gates_made, l + 1)
                        pool.wait_ge(hot_made[l], i + 1)
                        if not isinstance(i, int):
                            pool.wait_ge(sT_out[l], i)
                        elif i:
                            pool.wait_ge(sT_out[l], i)
                        nc.gpsimd.tensor_tensor(ghot, hot, bc(gates[:, :, bass.ds(2 * i, 2)].unsqueeze(3),
                                                              [P, 3, 2, CAP]), ALU.mult).then_inc(ghot_made[l], 1)
                    weigh(0)
                    with pool.Fori(1, NPAIR) as i:
                        weigh(i)
                pool.nop()
            moe(0)
            nc.gpsimd.wait_ge(rows_kept, 6)
            for rows, kname in ((krows, "k"), (vrows, "v")):
                if kname == "v":
                    pool.wait_ge(v_rows_kept, 2 * H)
                s_ = k_stored if kname == "k" else stored
                pool.dma_start(o[kname + "_prompt"][0].rearrange("(t p) h d -> p t (h d)", p=P),
                               rows[:, 0:2, :]).then_inc(s_, 16)
                pool.dma_start(o[kname + "_sample"].rearrange("b s h d -> (b s) (h d)"),
                               rows[0:NS, 2, :]).then_inc(s_, 16)
                if kname == "k":
                    pool.wait_ge(k_stored, 32)
                    nc.gpsimd.memset(pe4, 0.0).then_inc(pad_set, 1)
            moe(1)
            for t, (t0, n) in enumerate(TILES):
                pool.wait_ge(yr_made, 2 * (t + 1))
                dst = o["y_prompt"][0, t0:t0 + n, :] if t < 2 else o["y_sample"].rearrange("b s d -> (b s) d")
                pool.dma_start(dst, yr[0:n, t, :]).then_inc(stored, 16)

        @block.scalar
        def _(act):
            act.dma_start(C[:, :], a["consts"]).then_inc(c_load, 16)
            act.dma_start(gains[:, G_A, :], a["a_norm_g"][0].rearrange("(p k) -> p k", k=KT)).then_inc(ga_load, 16)
            act.wait_ge(eps_set, 1)

            def load_table(func):
                nc.scalar.activation(table_used[:, 0:1], eps[:, 0:1], func)

            def square_and_root(n, sq, ready, base):
                load_table(ACT.Sqrt)
                for k in range(KT):
                    act.wait_ge(ready, base + k + 1)
                    nc.scalar.activation(sq[:, k, :], xT[:, k, :], ACT.Square).then_inc(sq_made, 1)
                act.wait_ge(ss_out, n + 1)
                nc.scalar.activation(rms[:, :], PB[2][:, 0:T], ACT.Sqrt, bias=eps[:, 0:1], scale=1.0 / D)\
                    .then_inc(rms_made, 1)
            square_and_root(0, sqA, x_kept, 0)

            act.dma_start(wsr, a["a_w_s"][0].rearrange("g t s -> t g s")).then_inc(ws_load, 16)
            act.dma_start(bs[0:1], a["a_b_s"]).then_inc(g_load, 16)
            for i, g in ((G_M, a["moe_norm_g"][0]), (G_M + 1, a["moe_norm_g"][1]), (G_KV, a["kv_norm_g"]),
                         (G_B, a["b_norm_g"][0])):
                act.dma_start(gains[:, i, :], g.rearrange("(p k) -> p k", k=KT)).then_inc(g_load, 16)
            act.dma_start(hgain[:, 0:1], a["k_norm_g"].rearrange("(p k) -> p k", k=1)).then_inc(g_load, 16)
            act.dma_start(hgain[:, 1:2], a["q_norm_g"][0].rearrange("(p k) -> p k", k=1)).then_inc(g_load, 16)
            for l in L2:
                act.dma_start(rbias[0:NGRP, l:l + 1], a["moe_b_rg"][l].rearrange("(p k) -> p k", k=1)).then_inc(g_load, 16)
                act.dma_start(rbias[NGRP:NGRP + NE, l:l + 1], a["moe_b_re"][l].rearrange("(p k) -> p k", k=1))\
                    .then_inc(g_load, 16)
                act.dma_start(raw_g[l], a["moe_w_rg"][l].rearrange("(p k) n -> p k n", k=KT)).then_inc(g_load, 16)
                act.dma_start(raw_e[l], a["moe_w_re"][l].rearrange("(p k) n -> p k n", k=KT)).then_inc(g_load, 16)
            act.dma_start(pages[:, :], a["page_table"].rearrange("b n -> (b n)").rearrange("(a n) -> a n", a=1))\
                .then_inc(page_load, 16)

            for j in range(CT):
                if j == 12:
                    act.wait_ge(ws_turned, 3)
                act.wait_ge(v_out, j + 1)
                nc.scalar.activation(vT[:, j, :], PB[j % 2][:, 0:T], ACT.Gelu_apprx_tanh).then_inc(v_gelu, 1)
            act.wait_ge(mv_made, 1)
            nc.scalar.activation(vrstd, mv[:, :, 1], ACT.Sqrt, bias=eps[:, 0:1]).then_inc(vsd_made, 1)
            for j in range(CT):
                act.wait_ge(u_out, j + 1)
                nc.scalar.activation(vT[:, j, :], PB[j % 2][:, 0:T], ACT.Gelu_apprx_tanh).then_inc(u_gelu, 1)

            def moe(l):
                act.wait_ge(lgT_out, l + 1)
                act.wait_ge(g_load, 16 * SMALL_LOADS)
                nc.scalar.activation(lgT[0:NGRP + NE, :], PB[3][0:NGRP + NE, 0:T], ACT.Identity,
                                     bias=rbias[:, l:l + 1]).then_inc(lgT_made, 1)
                load_table(ACT.Exp)
                for i in range(6):
                    t, half = divmod(i, 2)
                    n = TILES[t][1]
                    act.wait_ge(hr_out, 6 * l + i + 1)
                    nc.scalar.activation(hr[0:n, t, 512 * half:512 * (half + 1)], PB[4 + i % 4][0:n, :], ACT.Copy)\
                        .then_inc(hr_kept, 1)
                act.wait_ge(soft_in, 2 * l + 1)
                nc.scalar.activation(ex, ex, ACT.Exp).then_inc(soft_out, 1)
                act.wait_ge(soft_in, 2 * l + 2)
                nc.scalar.activation(e2, e2, ACT.Exp).then_inc(soft_out, 1)

                def copy_hg(i):
                    act.wait_ge(gather_out[l], i + 1)
                    nc.scalar.activation(hg[:, 0:4, :], PB[0][:, :].rearrange("p (k s) -> p k s", k=4), ACT.Copy)\
                        .then_inc(hg_lo[l], 1)
                load_table(ACT.Silu)
                copy_hg(0)
                act.wait_ge(many_set, l + 1)
                flag = act.value_load(many[P - 1:P, 0:1], min_val=0, max_val=T)
                with act.If(flag > LIMIT):
                    def all_tokens(i):
                        for c in range(2 * FT):
                            act.wait_ge(gD_out[l], i * (2 * FT) + c + 1)
                            wait_for(act, hD_made[l], i * (2 * FT) + c)
                            nc.scalar.activation(sgD, PB[c % 2][:, 0:T], ACT.Silu).then_inc(sD_made[l], 1)
                    all_tokens(0)
                    with act.Fori(1, NPAIR) as i:
                        all_tokens(i)
                with act.Else():
                    def pair(i, last):
                        act.wait_ge(gate_out[l], i + 1)
                        nc.scalar.activation(sg, PB[2][:, :], ACT.Silu).then_inc(silu_made[l], 1)
                        act.wait_ge(heT_out[l], i + 1)
                        nc.scalar.activation(heT, PB[6][:, :].rearrange("p (f s) -> p f s", f=FT), ACT.Copy)\
                            .then_inc(heT_made[l], 1)
                        if not last:
                            copy_hg(i + 1)
                        act.wait_ge(down_out[l], i + 1)
                        nc.scalar.activation(dr[:, 0:512], PB[4][:, :], ACT.Copy).then_inc(dr_lo[l], 1)
                    with act.Fori(0, NPAIR - 1) as i:
                        pair(i, False)
                    pair(NPAIR - 1, True)
                act.nop()
            act.wait_ge(stored, 32)
            square_and_root(1, sqB, a_added, 0)
            moe(0)
            square_and_root(2, sqB, moe_done, 0)

            def rows_copy(g, rows):
                for t, (_, n) in enumerate(TILES):
                    act.wait_ge(rows_out, g + 1)
                    nc.scalar.activation(rows[0:n, t, 512 * (g % 2):512 * (g % 2 + 1)], PB[4 + t][0:n, :], ACT.Copy)\
                        .then_inc(rows_kept, 1)
            for g in range(2 * H + 1):
                if g < 2 * H:
                    act.wait_ge(kq_out, g + 1)
                    if g >= 2:
                        act.wait_ge(kq_ss, g - 1)
                    nc.scalar.activation(sqh[:, g % 2, :], acc(g)[:, 0:T], ACT.Square).then_inc(kq_sq, 1)
                if g >= 1:
                    act.wait_ge(kq_ss, g)
                    if g >= 2:
                        act.wait_ge(kq_normed, g - 1)
                    nc.scalar.activation(rmh, PB[2][:, 0:T], ACT.Sqrt, bias=eps[:, 0:1], scale=1.0 / HD)\
                        .then_inc(kq_rms, 1)
                if g - 4 in (3, 7):
                    rows_copy((g - 4) // 4, krows)
            def exp_prompt(h):
                act.wait_ge(ps_max, h + 1)
                for q, (lo, n) in enumerate(((0, P), (P, 2 * P))):
                    nc.scalar.activation(p3[:, lo:lo + n], s3[:, lo:lo + n], ACT.Exp, bias=mx3[:, q:q + 1],
                                         scale=SCALE, accum_out=rs3[:, q:q + 1]).then_inc(ps_exp, 1)

            def keep_pT(h):
                act.wait_ge(pT_out, h + 1)
                if h:
                    act.wait_ge(po_out, h)
                nc.scalar.activation(pT3, PB[1][:, 0:3 * P], ACT.Copy).then_inc(pT_made, 1)

            def keep_po(h):
                act.wait_ge(po_out, h + 1)
                nc.scalar.activation(aT[:, h, 0:NP_TOK], PB[2][:, 0:NP_TOK], ACT.Copy).then_inc(po_kept, 1)

            def keep_v(h):
                if h == 0:
                    act.wait_ge(kq_normed, 2 * H)
                act.wait_ge(vp_out, h + 1)
                if h >= 2:
                    act.wait_ge(v_rows_out, h - 1)
                nc.scalar.activation(vTh[:, h % 2, :], v_acc(h)[:, 0:T], ACT.Copy).then_inc(vp_kept, 1)
                nc.scalar.activation(vTs[:, h, :], v_acc(h)[:, NP_TOK:T], ACT.Copy).then_inc(vp_kept, 1)

            def keep_v_rows(h):
                act.wait_ge(v_rows_out, h + 1)
                nc.scalar.activation(vrows[:, 0:2, h * HD:(h + 1) * HD],
                                     PB[2][:, 0:2 * P].rearrange("p (t d) -> p t d", t=2), ACT.Copy)\
                    .then_inc(v_rows_kept, 1)
                nc.scalar.activation(vrows[0:NS, 2, h * HD:(h + 1) * HD], PB[2][0:NS, 2 * P:3 * P], ACT.Copy)\
                    .then_inc(v_rows_kept, 1)
            act.wait_ge(pad_set, 1)
            for s in range(NS + 1):
                prompt = PROMPT_HEADS[s]
                if prompt:
                    exp_prompt(prompt[0])
                if s >= 1:
                    c = (s - 1) % 2
                    act.wait_ge(sc_made, s)
                    nc.scalar.activation(pe4[:, c, :, 0:H], sc[:, c, :, :], ACT.Exp, scale=SCALE).then_inc(se_made, 1)
                if prompt:
                    keep_pT(prompt[0])
                for h in prompt[1:]:
                    exp_prompt(h)
                if s >= 1:
                    act.wait_ge(pv_out, s)
                    if s >= 2:
                        act.wait_ge(o_out, s - 1)
                    nc.scalar.activation(ov, PB[4][:, :], ACT.Copy).then_inc(ov_made, 1)
                if prompt:
                    keep_po(prompt[0])
                for h in prompt[1:]:
                    keep_pT(h)
                    keep_po(h)
                for h in V_HEADS[s]:
                    keep_v(h)
                    if h:
                        keep_v_rows(h - 1)
                    if h == H - 1:
                        keep_v_rows(h)
            act.wait_ge(stored, 64)
            square_and_root(3, sqM, wo_added, 0)
            moe(1)

        @block.tensor
        def _(pe):
            mm, tr = nc.tensor.matmul, nc.tensor.transpose

            pe.wait_ge(c_load, 16)
            pe.wait_ge(x_load, 32)
            def sum_square(n, sq, k):
                pe.wait_ge(sq_made, KT * n + k + 1)
                last = mm(PB[2][:, 0:T], ones, sq[:, k, :], start=(k == 0), stop=(k == KT - 1))
                if k == KT - 1:
                    last.then_inc(ss_out, 1)
            for k in range(KT):
                if k >= 2:
                    pe.wait_ge(x_kept, k - 1)
                for t, (t0, n) in enumerate(TILES):
                    last = tr(PB[k % 2][:, t0:t0 + n], xr[0:n, t, k:D:KT], ident[0:n, 0:n])
                last.then_inc(x_turned, 1)
                if k >= 2:
                    sum_square(0, sqA, k - 2)
            sum_square(0, sqA, KT - 2)
            sum_square(0, sqA, KT - 1)

            def turn_mixing():
                pe.wait_ge(ws_masked, 1)
                for half, bank in ((0, PB[3]), (1, PB[7])):
                    for g in range(4):
                        last = tr(bank[:, g * P:(g + 1) * P], wsr[:, 4 * half + g, :], ident)
                    last.then_inc(ws_turned, 1)
                pe.wait_ge(rms_made, 1)
                mm(PB[2][0:NS, 0:NG], ones[0:1, 0:NS], wsr[0:1, :, 0], start=True, stop=True).then_inc(ws_turned, 1)

            def turn_v(j):
                pe.wait_ge(v_gelu, j + 1)
                if j % 4 == 0:
                    if j:
                        pe.wait_ge(v_kept, 6 * (j // 4))
                    if j == 8:
                        turn_mixing()
                for t, (t0, n) in enumerate(TILES):
                    last = tr(PB[4 + t][0:n, (j % 4) * P:(j % 4 + 1) * P], vT[:, j, t0:t0 + n], ident)
                if j % 4 == 3:
                    last.then_inc(v_turned, 1)

            def half_of_w_in(name, base, out, gelu, after):
                for j in range(CT):
                    if j >= 2:
                        pe.wait_ge(gelu, j - 1)
                    for k in range(KT):
                        if j == 0:
                            pe.wait_ge(h_made, k + 1)
                            if k % 2 == 0:
                                arrived(pe, name, base + k // 2)
                        last = mm(PB[j % 2][:, 0:T], slot(base + k // 2, 2)[:, k % 2, j * P:(j + 1) * P], hT[:, k, :],
                                  start=(k == 0), stop=(k == KT - 1))
                    last.then_inc(out, 1)
                    if after and j:
                        after(j - 1)
            half_of_w_in("v", 0, v_out, v_gelu, turn_v)
            turn_v(CT - 1)
            pe.wait_ge(v_gelu, CT)
            half_of_w_in("u", 4, u_out, u_gelu, None)

            pe.wait_ge(ln_done, 1)
            pe.wait_ge(g_load, 16 * SMALL_LOADS)
            pe.wait_ge(ws_kept, 2)
            pe.wait_ge(d8_made, 2)
            for c in range(CT):
                g = c // 2
                bank = PB[4 + c % 2]
                if c >= 2:
                    pe.wait_ge(um_made, c - 1)
                for t, (t0, n) in enumerate(TILES):
                    mm(bank[:, t0:t0 + n], ones[0:1, :], bs[0:1, g, :] if t < 2 else b00[0:1, g, :],
                       start=True, stop=False)
                    last = mm(bank[:, t0:t0 + n], vr[0:n, t, c * P:(c + 1) * P],
                              wsT[:, g, :] if t < 2 else d8[0:NS, g, :], start=False, stop=True)
                last.then_inc(mix_out, 1)
            for j in range(KT):
                if j >= 2:
                    pe.wait_ge(a_added, j - 1)
                else:
                    pe.wait_ge(u_gelu, CT)
                for c in range(CT):
                    if j == 0:
                        pe.wait_ge(um_made, c + 1)
                        if c % 4 == 0:
                            arrived(pe, "wout", c // 4)
                    last = mm(PB[j % 2][:, 0:T], slot(c // 4, 4)[:, c % 4, j:D:KT], vT[:, c, :],
                              start=(c == 0), stop=(c == CT - 1))
                last.then_inc(a_out, 1)
                if j >= 2:
                    sum_square(1, sqB, j - 2)
            sum_square(1, sqB, KT - 2)
            sum_square(1, sqB, KT - 1)

            def moe(l, h_before):
                def weights_of(i):
                    if isinstance(i, int) and i == 0:
                        return (GATE0[l], f"gate0_{l}", 1), (UP0[l], f"up0_{l}", 1), (DOWN0[l], f"down0_{l}", 1)
                    return (GATE[l], f"gate{l}", i), (UP[l], f"up{l}", i), (DOWN[l], f"down{l}", i)

                if l == 0:
                    pe.wait_ge(wr_made, 4)
                for k in range(KT):
                    pe.wait_ge(h_made, h_before + k + 1)
                    last = mm(PB[3][0:NGRP + NE, 0:T], wr[:, l, k, :], hT[:, k, :], start=(k == 0), stop=(k == KT - 1))
                last.then_inc(lgT_out, 1)

                def rows(i):
                    t, half = divmod(i, 2)
                    t0, n = TILES[t]
                    if i >= 4:
                        pe.wait_ge(hr_kept, 6 * l + i - 3)
                    for q in range(4):
                        last = tr(PB[4 + i % 4][0:n, q * P:(q + 1) * P], hT[:, 4 * half + q, t0:t0 + n], ident)
                    last.then_inc(hr_out, 1)
                rows(0)
                pe.wait_ge(lgT_made, l + 1)
                for t, (t0, n) in enumerate(TILES):
                    last = tr(PB[2][0:n, t * 20:(t + 1) * 20], lgT[0:NGRP + NE, t0:t0 + n], ident[0:20, 0:20])
                last.then_inc(lg_out, 1)
                for i in range(1, 6):
                    rows(i)
                pe.wait_ge(chose_made, l + 1)
                ranks = PB[3][:, 0:3 * NE]
                mm(ranks, earlier, chose.rearrange("p t e -> p (t e)"), start=True, stop=False)
                mm(ranks[:, NE:3 * NE].rearrange("p (t e) -> p t e", t=2), ones,
                   bc(chose[:, 0:1, :], [P, 2, NE]), start=False, stop=False)
                mm(ranks[:, 2 * NE:3 * NE], ones, chose[:, 1, :], start=False, stop=True).then_inc(rank_out, 1)

                def gather(i):
                    pe.wait_ge(hot_made[l], i + 1)
                    for k in range(KT):
                        for t, (t0, n) in enumerate(TILES):
                            last = mm(PB[k // 4][:, (k % 4) * P:(k % 4 + 1) * P], hr[0:n, t, k * P:(k + 1) * P],
                                      hot[0:n, t, :, :].rearrange("p e s -> p (e s)"), start=(t == 0), stop=(t == 2))
                    last.then_inc(gather_out[l], 1)
                pe.wait_ge(hr_kept, 6 * l + 6)
                gather(0)
                pe.wait_ge(many_set, l + 1)
                flag = pe.value_load(many[P - 1:P, 0:1], min_val=0, max_val=T)
                with pe.If(flag > LIMIT):
                    pe.wait_ge(hg_lo[l], 1)
                    pe.wait_ge(hg_hi[l], 1)

                    def all_tokens(i):
                        for e in range(2):
                            pe.wait_ge(gb_made[l], i * 2 + e + 1)
                            for t, (t0, n) in enumerate(TILES):
                                last = mm(PB[7][:, t0:t0 + n], gb[0:n, t, :], ident[0:n, 0:n], start=True, stop=True)
                            last.then_inc(gcol_out[l], 1)
                            gate, up, down = weights_of(i)
                            for first, name, nth in (gate, up, down):
                                arrived(pe, name, first + e, nth)
                            for f in range(FT):
                                c = e * FT + f
                                wait_for(pe, hD_made[l], i * (2 * FT) + (c - 1 if c >= 2 else 0))
                                for base, bank in ((gate[0], PB[f % 2]), (up[0], PB[2 + f % 2])):
                                    for k in range(KT):
                                        last = mm(bank[:, 0:T], slot(base + e, KT)[:, k, f * P:(f + 1) * P], hT[:, k, :],
                                                  start=(k == 0), stop=(k == KT - 1))
                                    if e == 1 and f == FT - 1 and base == gate[0]:
                                        last.then_inc(gate_out[l], 1)
                                last.then_inc(gD_out[l], 1)
                            pe.wait_ge(hD_made[l], i * (2 * FT) + (e + 1) * FT)
                            for j in range(KT):
                                c = e * KT + j
                                wait_for(pe, yD_added[l], i * (2 * KT) + (c - 1 if c >= 2 else 0))
                                for f in range(FT):
                                    last = mm(PB[4 + j % 2][:, 0:T], slot(down[0] + e, FT)[:, f, j:D:KT], heD[:, f, :],
                                              start=(f == 0), stop=(f == FT - 1))
                                last.then_inc(yD_out[l], 1)
                        pe.wait_ge(yD_out[l], i * (2 * KT) + 2 * KT)
                        pe.sem_inc(up_out[l], 1)
                        pe.sem_inc(down_out[l], 1)
                    all_tokens(0)
                    with pe.Fori(1, NPAIR) as i:
                        all_tokens(i)
                    if l == 0:
                        for k in range(KT):
                            sum_square(2, sqB, k)
                with pe.Else():
                    def scatter(i):
                        pe.wait_ge(dr_lo[l], i + 1)
                        pe.wait_ge(dr_hi[l], i + 1)
                        pe.wait_ge(sT_made[l], i + 1)
                        for j in range(KT):
                            if j >= 2:
                                if isinstance(i, int) and i == NPAIR - 1:
                                    pe.wait_ge(moe_done, l * KT + j - 1)
                                else:
                                    pe.wait_ge(y_added[l], i * KT + j - 1)
                            last = mm(PB[6 + j % 2][:, 0:T], dr[:, j:D:KT], sT, start=True, stop=True)
                            last.then_inc(y_out[l], 1)
                            if l == 0 and isinstance(i, int) and i == NPAIR - 1 and j >= 2:
                                sum_square(2, sqB, j - 2)

                    def pair(i, first, last_pair):
                        pe.wait_ge(hg_lo[l], i + 1)
                        pe.wait_ge(hg_hi[l], i + 1)
                        gate, up, down = weights_of(i)
                        for (base, name, nth), bank, out in ((gate, PB[2], gate_out), (up, PB[3], up_out)):
                            for e in range(2):
                                arrived(pe, name, base + e, nth)
                            if not first:
                                pe.wait_ge(he_made[l], i)
                            for k in range(KT):
                                for e in range(2):
                                    last = mm(bank[64 * e:64 * e + 64, :], hg[:, k, CAP * e:CAP * (e + 1)],
                                              slot(base + e, KT)[:, k, :], start=(k == 0), stop=(k == KT - 1))
                            last.then_inc(out[l], 1)
                        if not first:
                            scatter(i - 1)
                        pe.wait_ge(he_made[l], i + 1)
                        if not first:
                            pe.wait_ge(y_added[l], i * KT)
                        for f in range(FT):
                            last = tr(PB[6][:, f * P:(f + 1) * P], he[:, f * P:(f + 1) * P], ident)
                        last.then_inc(heT_out[l], 1)
                        if not last_pair:
                            gather(i + 1)
                        pe.wait_ge(ghot_made[l], i + 1)
                        for t, (t0, n) in enumerate(TILES):
                            last = tr(PB[7][:, t0:t0 + n], ghot[0:n, t, :, :].rearrange("p e s -> p (e s)"), ident[0:n, 0:n])
                        last.then_inc(sT_out[l], 1)
                        for e in range(2):
                            arrived(pe, down[1], down[0] + e, down[2])
                        pe.wait_ge(heT_made[l], i + 1)
                        if not first:
                            pe.wait_ge(dr_lo[l], i)
                            pe.wait_ge(dr_hi[l], i)
                        for f in range(FT):
                            for half in range(2):
                                for e in range(2):
                                    last = mm(PB[4 + half][64 * e:64 * e + 64, :], heT[:, f, CAP * e:CAP * (e + 1)],
                                              slot(down[0] + e, FT)[:, f, 512 * half:512 * (half + 1)],
                                              start=(f == 0), stop=(f == FT - 1))
                        last.then_inc(down_out[l], 1)
                    pair(0, True, False)
                    with pe.Fori(1, NPAIR - 1) as i:
                        pair(i, False, False)
                    pair(NPAIR - 1, False, True)
                    scatter(NPAIR - 1)
                    if l == 0:
                        sum_square(2, sqB, KT - 2)
                        sum_square(2, sqB, KT - 1)
                pe.nop()

            moe(0, KT)

            def rows(g, src):
                if g % 4 == 0 and g:
                    pe.wait_ge(rows_kept, 3 * (g // 4))
                for t, (t0, n) in enumerate(TILES):
                    last = tr(PB[4 + t][0:n, (g % 4) * P:(g % 4 + 1) * P], src[:, t0:t0 + n], ident)
                if g % 4 == 3:
                    last.then_inc(rows_out, 1)
            def project_v(h):
                if h >= 2:
                    pe.wait_ge(vp_kept, 2 * (h - 1))
                else:
                    pe.wait_ge(kq_normed, 2 * H - 2 + h)
                for k in range(KT):
                    if h == 0 and k % 4 == 0:
                        arrived(pe, "w_v", W_V + k // 4)
                    last = mm(v_acc(h)[:, 0:T], slot(W_V + k // 4, 4)[:, k % 4, h * HD:(h + 1) * HD], hk[:, k, :],
                              start=(k == 0), stop=(k == KT - 1))
                last.then_inc(vp_out, 1)

            for g in range(2 * H + 3):
                if g < 2 * H:
                    if g >= 3:
                        pe.wait_ge(kq_normed, g - 2)
                    for k in range(KT):
                        if g % H == 0:
                            pe.wait_ge(h_made, (3 if g else 2) * KT + k + 1)
                        if g < H:
                            if g == 0 and k % 4 == 0:
                                arrived(pe, "w_k", W_K + k // 4)
                            w, h = slot(W_K + k // 4, 4)[:, k % 4, g * HD:(g + 1) * HD], hk
                        else:
                            if g == H and k % 4 == 0:
                                arrived(pe, "w_q", W_Q + k // 4)
                            w, h = slot(W_Q + k // 4, 4)[:, k % 4, (g - H) * HD:(g - H + 1) * HD], hq
                        last = mm(acc(g)[:, 0:T], w, h[:, k, :], start=(k == 0), stop=(k == KT - 1))
                    last.then_inc(kq_out, 1)
                if 1 <= g <= 2 * H:
                    pe.wait_ge(kq_sq, g)
                    if g >= 2:
                        pe.wait_ge(kq_rms, g - 1)
                    mm(PB[2][:, 0:T], ones, sqh[:, (g - 1) % 2, :], start=True, stop=True).then_inc(kq_ss, 1)
                if g == 2 * H:
                    project_v(0)
                if 2 <= g < 2 * H + 2:
                    pe.wait_ge(kq_normed, g - 1)
                    if g >= 3:
                        pe.wait_ge(kq_made, g - 2)
                    mm(PB[3][0:ROT, 0:T], const("rot"), kq[:, g - 2, :], start=True, stop=True).then_inc(kq_rot, 1)
                if 3 <= g < H + 3:
                    pe.wait_ge(kq_made, g - 2)
                    rows(g - 3, kq[:, g - 3, :])
            pe.wait_ge(kq_normed, 2 * H)
            pe.wait_ge(rows_kept, 6)

            def queries(s, half):
                for h in range(4):
                    last = mm(PB[6 + half][:, h * P:(h + 1) * P],
                              bc(kq[:, H + 4 * half + h, NP_TOK + s:NP_TOK + s + 1], [P, P]), ident, start=True, stop=True)
                last.then_inc(qb_out, 1)

            def turn_v_head(h):
                pe.wait_ge(vp_kept, 2 * h + 1)
                if h:
                    pe.wait_ge(v_rows_kept, 2 * h)
                for t, (t0, n) in enumerate(TILES):
                    last = tr(PB[2][0:n, t * P:(t + 1) * P], vTh[:, h % 2, t0:t0 + n], ident)
                last.then_inc(v_rows_out, 1)

            def prompt_logits(h):
                if h == 0:
                    pe.wait_ge(vp_kept, 2 * H)
                else:
                    pe.wait_ge(ps_max, h)
                mm(PB[0][:, 0:P], kq[:, H + h, 0:P], kq[:, h, 0:P], start=True, stop=True)
                mm(PB[0][:, P:3 * P], kq[:, H + h, P:2 * P], kq[:, h, 0:2 * P], start=True, stop=True).then_inc(ps_out, 1)

            def prompt_turn(h):
                pe.wait_ge(ps_norm, h + 1)
                if h:
                    pe.wait_ge(pT_made, h)
                for b in range(3):
                    last = tr(PB[1][:, b * P:(b + 1) * P], p3[:, b * P:(b + 1) * P], ident)
                last.then_inc(pT_out, 1)

            def prompt_values(h):
                pe.wait_ge(pT_made, h + 1)
                if h:
                    pe.wait_ge(po_kept, h)
                else:
                    pe.wait_ge(v_rows_kept, 2 * H)
                mm(PB[2][:, 0:2 * P], vrows[:, 0, h * HD:(h + 1) * HD], pT3[:, 0:2 * P], start=True, stop=False)
                mm(PB[2][:, P:2 * P], vrows[:, 1, h * HD:(h + 1) * HD], pT3[:, 2 * P:3 * P], start=False, stop=True)\
                    .then_inc(po_out, 1)

            def open_step(s):
                if s >= 1:
                    pe.wait_ge(s_made, 2 * s)
                    if s >= 2:
                        pe.wait_ge(att_made, s - 1)
                    else:
                        pe.wait_ge(own_made, 1)
                    mm(PB[3][:, 64:128], ones, sc[:, (s - 1) % 2, 0:NPAGE, :].rearrange("p g h -> p (g h)"),
                       start=True, stop=True).then_inc(gs_out, 1)
                if s < NS:
                    queries(s, 1)

            def next_queries(s):
                if s + 1 < NS:
                    pe.wait_ge(s_made, 2 * s + 1)
                    queries(s + 1, 0)

            pe.wait_ge(kq_made, 2 * H)
            queries(0, 0)
            open_step(0)
            pe.wait_ge(own_in, 1)
            mm(PB[3][:, 0:H * NS], ones, ownp.rearrange("p h s -> p (h s)"), start=True, stop=True).then_inc(own_out, 1)

            for s in range(NS + 1):
                c = (s - 1) % 2
                prompt = PROMPT_HEADS[s]
                if prompt:
                    prompt_logits(prompt[0])
                if s >= 1:
                    pe.wait_ge(pm_made, s)
                    tr(PB[5][0:H, 128:256], pmx, ident).then_inc(pm_turned, 1)
                    pe.wait_ge(dg_made, s)
                    mm(PB[3][:, 256:264], ones[0:H, :], dg[0:H, :], start=True, stop=True).then_inc(mb_out, 1)
                if prompt:
                    prompt_turn(prompt[0])
                for h in prompt[1:]:
                    prompt_logits(h)
                if s >= 1:
                    pe.wait_ge(rs_made, s)
                    mm(PB[5][:, 264:272], ones, rsum, start=True, stop=True).then_inc(den_out, 1)
                    v_slot = V_SLOT[s - 1]
                    if s >= 2:
                        pe.wait_ge(ov_made, s - 1)
                    for g in range(NPAGE):
                        if g % 4 == 0:
                            arrived(pe, f"V{s - 1}", v_slot + g // 4, each=64)
                        for half in range(2):
                            q = 2 * (g % 2) + half
                            last = mm(PB[4][32 * q:32 * q + 32, :], pe4[:, c, g, :],
                                      W[:, v_slot + g // 4, (g % 4) * D + 512 * half:(g % 4) * D + 512 * (half + 1)],
                                      start=(g < 2), stop=(g >= NPAGE - 2), tile_position=(0, 32 * q))
                    last.then_inc(pv_out, 1)
                if prompt:
                    prompt_values(prompt[0])
                if s >= 1:
                    pe.wait_ge(ov_made, s)
                    for b in range(4):
                        last = mm(PB[3][:, 272 + b:272 + b + 5:4], ov[:, b * P:(b + 1) * P],
                                  const("pick").rearrange("p (b n) -> p b n", n=2)[:, b, :], start=True, stop=True)
                    last.then_inc(o_out, 1)
                for h in V_HEADS[s]:
                    if h:
                        project_v(h)
                        turn_v_head(h - 1)
                    if h == 3:
                        next_queries(s)
                    elif h == 5:
                        open_step(s + 1)
                    elif h == H - 1:
                        turn_v_head(h)
                if not V_HEADS[s]:
                    next_queries(s)
                for h in prompt[1:]:
                    prompt_turn(h)
                    prompt_values(h)
                if not V_HEADS[s] and s < NS:
                    open_step(s + 1)
            pe.wait_ge(att_made, NS + 1)
            pe.wait_ge(po_kept, H)
            for j in range(KT):
                if j >= 2:
                    pe.wait_ge(wo_added, j - 1)
                for h in range(H):
                    if j == 0 and h % 4 == 0:
                        arrived(pe, "w_o", W_O + h // 4)
                    last = mm(PB[j % 2][:, 0:T], slot(W_O + h // 4, 4)[:, h % 4, j:D:KT], aT[:, h, :],
                              start=(h == 0), stop=(h == H - 1))
                last.then_inc(wo_out, 1)
                if j >= 2:
                    sum_square(3, sqM, j - 2)
            sum_square(3, sqM, KT - 2)
            sum_square(3, sqM, KT - 1)
            moe(1, 4 * KT)
            pe.wait_ge(moe_done, 2 * KT)
            for i in range(6):
                t, half = divmod(i, 2)
                t0, n = TILES[t]
                if i >= 4:
                    pe.wait_ge(yr_made, i - 3)
                for q in range(4):
                    last = tr(PB[i % 4][0:n, q * P:(q + 1) * P], xT[:, 4 * half + q, t0:t0 + n], ident)
                last.then_inc(y_turned, 1)

        @block.vector
        def _(dve):
            v = nc.vector
            steps = Chain(dve, vec)
            link, ran, settle = steps.link, steps.ran, steps.wait

            v.memset(eps[:, :], EPS).then_inc(eps_set, 1)
            link(v.memset(mv, 1.0))
            for k in range(KT):
                dve.wait_ge(x_turned, k + 1)
                v.tensor_copy(xT[:, k, :], PB[k % 2][:, 0:T]).then_inc(x_kept, 1)
            dve.wait_ge(ga_load, 16)

            def normed(n, targets):
                dve.wait_ge(rms_made, n + 1)
                v.reciprocal(rstd[:, :], rms[:, :]).then_inc(rstd_made, 1)
                dve.wait_ge(rstd_made, n + 1)
                for dst, g in targets:
                    for k in range(KT):
                        v.scalar_tensor_tensor(out=dst[:, k, :], in0=xT[:, k, :], scalar=gains[:, g, k:k + 1],
                                               in1=rstd[:, :], op0=ALU.mult, op1=ALU.mult).then_inc(h_made, 1)
            dve.wait_ge(x_kept, KT)
            normed(0, [(hT, G_A)])

            def keep_mixing():
                for half, bank in ((0, PB[3]), (1, PB[7])):
                    dve.wait_ge(ws_turned, half + 1)
                    v.tensor_copy(wsT[:, 4 * half:4 * half + 4, :], bank[:, :].rearrange("p (g t) -> p g t", g=4))\
                        .then_inc(ws_kept, 1)
                dve.wait_ge(ws_turned, 3)
                link(v.tensor_copy(w00[0:NS], PB[2][0:NS, 0:NG]))
                v.tensor_tensor(d8[0:NS], bc(ident[0:NS, 0:NS].unsqueeze(1), [NS, NG, NS]),
                                bc(w00[0:NS].unsqueeze(2), [NS, NG, NS]), ALU.mult).then_inc(d8_made, 1)
                dve.wait_ge(g_load, 16 * SMALL_LOADS)
                v.tensor_copy(b00[0:1], bc(bs[0:1, :, 0:1], [1, NG, NS])).then_inc(d8_made, 1)
            for b in range(4):
                dve.wait_ge(v_turned, b + 1)
                for t, (_, n) in enumerate(TILES):
                    v.tensor_copy(vr[0:n, t, 512 * b:512 * (b + 1)], PB[4 + t][0:n, :]).then_inc(v_kept, 1)
                    v.bn_stats(stats[0:n, t, 6 * b:6 * b + 6], PB[4 + t][0:n, :]).then_inc(v_kept, 1)
                if b == 1:
                    keep_mixing()
            dve.wait_ge(v_kept, 24)
            for t, (_, n) in enumerate(TILES):
                ran(v.bn_aggr(mv[0:n, t, :], stats[0:n, t, :]))
            settle()
            v.sem_inc(mv_made, 1)
            dve.wait_ge(vsd_made, 1)
            link(v.reciprocal(vrstd, vrstd))
            for b in range(4):
                dve.wait_ge(ln_load, 32 * (b + 1))
                for t, (_, n) in enumerate(TILES):
                    part = vr[0:n, t, 512 * b:512 * (b + 1)]
                    ran(v.tensor_scalar(part, part, mv[0:n, t, 0:1], vrstd[0:n, t:t + 1], ALU.subtract, ALU.mult))
                settle()
                for i, op in ((0, ALU.mult), (1, ALU.add)):
                    for t, (_, n) in enumerate(TILES):
                        part = vr[0:n, t, 512 * b:512 * (b + 1)]
                        ran(v.tensor_tensor(part, part, lng[0:n, i, :], op))
                    settle()
                v.sem_inc(ln_used, 1)
            v.sem_inc(ln_done, 1)
            for c in range(CT):
                dve.wait_ge(mix_out, c + 1)
                dve.wait_ge(u_gelu, c + 1)
                v.tensor_tensor(vT[:, c, :], vT[:, c, :], PB[4 + c % 2][:, 0:T], ALU.mult).then_inc(um_made, 1)
            for j in range(KT):
                dve.wait_ge(a_out, j + 1)
                v.tensor_tensor(xT[:, j, :], xT[:, j, :], PB[j % 2][:, 0:T], ALU.add).then_inc(a_added, 1)
            dve.wait_ge(a_added, KT)

            def moe(l):
                link(v.memset(lg, 0.0))
                dve.wait_ge(lg_out, l + 1)
                ran(v.tensor_copy(lg[:, 0:2, :], PB[2][:, 0:40].rearrange("p (t n) -> p t n", t=2)))
                link(v.tensor_copy(lg[0:NS, 2, :], PB[2][0:NS, 40:60]))
                lgg = lg[:, :, 0:NGRP]
                s34 = [P, 3, 4]
                firsts = bc(const("first").unsqueeze(1), s34)

                def wide(x):
                    return bc(x.unsqueeze(2), s34)

                def argmax(x, top, onehot):
                    link(v.tensor_reduce(top, x, AX.X, ALU.max))
                    link(v.tensor_tensor(cand, x, wide(top), ALU.is_equal))
                    link(v.tensor_tensor(cand, cand, firsts, ALU.mult))
                    link(v.tensor_reduce(mn, cand, AX.X, ALU.min))
                    link(v.tensor_tensor(onehot, cand, wide(mn), ALU.is_equal))
                argmax(lgg, gm, ohg)
                link(v.tensor_tensor(ex, lgg, wide(gm), ALU.subtract))
                v.sem_inc(soft_in, 1)
                link(v.tensor_tensor(prod.rearrange("p t (j g) -> p t j g", g=4),
                                     lg[:, :, NGRP:].rearrange("p t (g j) -> p t j g", g=4),
                                     bc(ohg.unsqueeze(2), [P, 3, 4, 4]), ALU.mult))
                link(v.tensor_reduce(leg, prod.rearrange("p t (j g) -> p t j g", g=4), AX.X, ALU.add))
                argmax(leg, m1, oh1)
                link(v.scalar_tensor_tensor(out=le2, in0=oh1, scalar=-3e38, in1=leg, op0=ALU.mult, op1=ALU.add))
                argmax(le2, m2, oh2)
                link(v.tensor_tensor(e2, m2, m1, ALU.subtract))
                v.sem_inc(soft_in, 1)
                link(v.tensor_tensor(cand, oh1, oh2, ALU.add))
                g44 = [P, 3, 4, 4]
                link(v.tensor_tensor(chose.rearrange("p t (g j) -> p t g j", g=4), bc(ohg.unsqueeze(3), g44),
                                     bc(cand.unsqueeze(2), g44), ALU.mult))
                v.tensor_tensor(chose, chose, bc(const("valid").unsqueeze(2), [P, 3, 16]), ALU.mult)\
                    .then_inc(chose_made, 1)
                dve.wait_ge(chose_made, l + 1)
                dve.wait_ge(rank_out, l + 1)
                counted = PB[3][:, 0:3 * NE].rearrange("p (t e) -> p t e", t=3)
                v.tensor_reduce(many[:, :], counted[:, 2, :], AX.X, ALU.max).then_inc(many_set, 1)
                link(v.scalar_tensor_tensor(out=rank, in0=counted, scalar=1.0, in1=chose, op0=ALU.add, op1=ALU.mult))
                link(v.tensor_scalar(rank, rank, -1.0, None, ALU.add))

                def onehot(i):
                    v.tensor_tensor(hot, bc(const("iota").unsqueeze(1).unsqueeze(1), [P, 3, 2, CAP]),
                                    bc(rank[:, :, bass.ds(2 * i, 2)].unsqueeze(3), [P, 3, 2, CAP]), ALU.is_equal)\
                        .then_inc(hot_made[l], 1)

                def copy_hg(i):
                    dve.wait_ge(gather_out[l], i + 1)
                    v.tensor_copy(hg[:, 4:8, :], PB[1][:, :].rearrange("p (k s) -> p k s", k=4)).then_inc(hg_hi[l], 1)
                onehot(0)
                dve.wait_ge(soft_out, 2 * l + 2)
                link(v.tensor_reduce(pg, ex, AX.X, ALU.add))
                link(v.reciprocal(pg, pg))
                link(v.tensor_scalar(w1, e2, 1.0, None, ALU.add))
                link(v.reciprocal(w1, w1))
                link(v.tensor_tensor(w1, w1, pg, ALU.mult))
                link(v.tensor_tensor(w2, e2, w1, ALU.mult))
                link(v.tensor_tensor(oh1, oh1, wide(w1), ALU.mult))
                link(v.tensor_tensor(oh2, oh2, wide(w2), ALU.mult))
                link(v.tensor_tensor(oh1, oh1, oh2, ALU.add))
                link(v.tensor_tensor(gates.rearrange("p t (g j) -> p t g j", g=4), bc(ohg.unsqueeze(3), g44),
                                     bc(oh1.unsqueeze(2), g44), ALU.mult))
                v.sem_inc(gates_made, 1)
                copy_hg(0)
                dve.wait_ge(many_set, l + 1)
                flag = dve.value_load(many[P - 1:P, 0:1], min_val=0, max_val=T)
                with dve.If(flag > LIMIT):
                    own_steps = Chain(dve, vecD[l])
                    def all_tokens(i):
                        own_steps.base, own_steps.n = i * (2 * FT), 0
                        for e in range(2):
                            wait_for(dve, gcol_out[l], i * 2 + e)
                            v.tensor_copy(gb, bc(gates[:, :, bass.ds(2 * i + e, 1)], [P, 3, P])).then_inc(gb_made[l], 1)
                            dve.wait_ge(gcol_out[l], i * 2 + e + 1)
                            wait_for(dve, hD_made[l], i * (2 * FT) + e * FT)
                            v.tensor_copy(gcol, PB[7][:, 0:T]).then_inc(gcol_made[l], 1)
                            dve.wait_ge(gcol_made[l], i * 2 + e + 1)
                            wait_for(dve, yD_out[l], i * (2 * KT) + e * KT)
                            for f in range(FT):
                                dve.wait_ge(sD_made[l], i * (2 * FT) + e * FT + f + 1)
                                own_steps.link(v.tensor_tensor(heD[:, f, :], sgD, PB[2 + f % 2][:, 0:T], ALU.mult))
                                v.tensor_tensor(heD[:, f, :], heD[:, f, :], gcol, ALU.mult).then_inc(hD_made[l], 1)
                            for j in range(KT):
                                dve.wait_ge(yD_out[l], i * (2 * KT) + e * KT + j + 1)
                                wait_for(dve, yD_added[l], i * (2 * KT) + e * KT + j)
                                v.tensor_tensor(xT[:, j, :], xT[:, j, :], PB[4 + j % 2][:, 0:T], ALU.add)\
                                    .then_inc(yD_added[l], 1)
                    all_tokens(0)
                    with dve.Fori(1, NPAIR) as i:
                        all_tokens(i)
                    dve.wait_ge(yD_added[l], NE * KT)
                    v.sem_inc(moe_done, KT)
                with dve.Else():
                    def add_y(i):
                        for j in range(KT):
                            dve.wait_ge(y_out[l], i * KT + j + 1)
                            v.tensor_tensor(xT[:, j, :], xT[:, j, :], PB[6 + j % 2][:, 0:T], ALU.add).then_inc(
                                moe_done if isinstance(i, int) and i == NPAIR - 1 else y_added[l], 1)

                    def pair(i, first, last):
                        dve.wait_ge(silu_made[l], i + 1)
                        dve.wait_ge(up_out[l], i + 1)
                        v.tensor_tensor(he, sg, PB[3][:, :], ALU.mult).then_inc(he_made[l], 1)
                        if not first:
                            add_y(i - 1)
                        if not last:
                            copy_hg(i + 1)
                        dve.wait_ge(sT_out[l], i + 1)
                        v.tensor_copy(sT, PB[7][:, 0:T]).then_inc(sT_made[l], 1)
                        if not last:
                            if not isinstance(i, int) or i < NPAIR - 2:
                                dve.wait_ge(ghot_made[l], i + 2)
                                onehot(i + 2)
                        dve.wait_ge(down_out[l], i + 1)
                        v.tensor_copy(dr[:, 512:D], PB[5][:, :]).then_inc(dr_hi[l], 1)
                    dve.wait_ge(ghot_made[l], 1)
                    onehot(1)
                    pair(0, True, False)
                    with dve.Fori(1, NPAIR - 2) as i:
                        pair(i, False, False)
                    pair(NPAIR - 2, False, False)
                    pair(NPAIR - 1, False, True)
                    add_y(NPAIR - 1)
                dve.nop()

            normed(1, [(hT, G_M)])
            moe(0)
            dve.wait_ge(moe_done, KT)
            normed(2, [(hk, G_KV)])

            for g in range(2 * H + 2):
                if g < 2 * H:
                    dve.wait_ge(kq_rms, g + 1)
                    link(v.reciprocal(rsh, rmh))
                    v.scalar_tensor_tensor(out=kq[:, g, :], in0=acc(g)[:, 0:T], scalar=hgain[:, g // H:g // H + 1],
                                           in1=rsh, op0=ALU.mult, op1=ALU.mult).then_inc(kq_normed, 1)
                    dve.wait_ge(kq_normed, g + 1)
                if g < KT // 2:
                    for k in (2 * g, 2 * g + 1):
                        v.scalar_tensor_tensor(out=hq[:, k, :], in0=xT[:, k, :], scalar=gains[:, G_B, k:k + 1],
                                               in1=rstd[:, :], op0=ALU.mult, op1=ALU.mult).then_inc(h_made, 1)
                if g >= 1 and g <= 2 * H:
                    dve.wait_ge(kq_rot, g)
                    rot = kq[0:ROT, g - 1, :]
                    ran(v.tensor_tensor(turned[0:ROT, :], PB[3][0:ROT, 0:T], const("sin")[0:ROT, :], ALU.mult))
                    link(v.tensor_tensor(rot, rot, const("cos")[0:ROT, :], ALU.mult))
                    v.tensor_tensor(rot, rot, turned[0:ROT, :], ALU.add).then_inc(kq_made, 1)
                    dve.wait_ge(kq_made, g)
            v.tensor_tensor(ownp, kq[:, 0:H, NP_TOK:T], kq[:, H:2 * H, NP_TOK:T], ALU.mult).then_inc(own_in, 1)
            dve.wait_ge(own_out, 1)
            v.tensor_copy(own.rearrange("p h s -> p (h s)"), PB[3][:, 0:H * NS]).then_inc(own_made, 1)
            dve.wait_ge(own_made, 1)
            dve.wait_ge(pad_set, 1)

            def keys(s, half, g):
                c = s % 2
                k_slot = K_SLOT[s] + g // 4
                if g == 0:
                    dve.wait_ge(qb_out, 2 * s + half + 1)
                if g % 4 == 0 and half == 0:
                    arrived(dve, f"K{s}", k_slot, each=64)
                for i in range(4):
                    h = 4 * half + i
                    kb = W[:, k_slot, (g % 4) * D + h * HD:(g % 4) * D + (h + 1) * HD]
                    last = v.tensor_tensor_reduce(kb, kb, PB[6 + half][:, i * P:(i + 1) * P], 1.0, 0.0,
                                                  ALU.mult, ALU.add, sc[:, c, g, h:h + 1])
                if g == NPAGE - 1:
                    last.then_inc(s_made, 1)

            for s in range(NS + 1):
                c = (s - 1) % 2
                scp = sc[:, c, 0:NPAGE, :]

                def prompt_max(h):
                    dve.wait_ge(ps_out, h + 1)
                    if h:
                        dve.wait_ge(ps_exp, 2 * h)
                    link(v.tensor_tensor(s3, PB[0][:, 0:3 * P], const("causal"), ALU.add))
                    ran(v.tensor_reduce(mx3[:, 0:1], s3[:, 0:P], AX.X, ALU.max))
                    link(v.tensor_reduce(mx3[:, 1:2], s3[:, P:3 * P], AX.X, ALU.max))
                    if h:
                        dve.wait_ge(pT_out, h)
                    v.tensor_scalar(mx3, mx3, -SCALE, None, ALU.mult).then_inc(ps_max, 1)

                def blocks():
                    dve.wait_ge(gs_out, s)
                    link(v.tensor_reduce(gsum, PB[3][:, 64:128].rearrange("p (b g h) -> p b h g", b=NBLK, g=2),
                                         AX.X, ALU.add))
                    link(v.tensor_reduce(mnb, gsum.rearrange("p b h -> p h b"), AX.X, ALU.min))
                    link(v.tensor_tensor(eqb, gsum, bc(mnb.unsqueeze(1), [P, NBLK, H]), ALU.is_equal))
                    link(v.tensor_tensor(eqb, eqb, bc(const("blk").unsqueeze(2), [P, NBLK, H]), ALU.mult))
                    link(v.tensor_reduce(vmb, eqb.rearrange("p b h -> p h b"), AX.X, ALU.max))
                    link(v.tensor_tensor(drop, eqb, bc(vmb.unsqueeze(1), [P, NBLK, H]), ALU.is_equal))
                    for g in range(2):
                        half = scp.rearrange("p (b g) h -> p b g h", g=2)[:, :, g, :]
                        ran(v.scalar_tensor_tensor(out=half, in0=drop, scalar=NEG, in1=half, op0=ALU.mult, op1=ALU.add))
                    settle()
                    v.tensor_reduce(pmx, scp.rearrange("p g h -> p h g"), AX.X, ALU.max).then_inc(pm_made, 1)

                def maxima():
                    dve.wait_ge(pm_turned, s)
                    link(v.tensor_reduce(hm[0:H, :], PB[5][0:H, 128:256], AX.X, ALU.max))
                    v.tensor_scalar(dg[0:H, :], ident[0:H, 0:H], hm[0:H, 0:1], None, ALU.mult).then_inc(dg_made, 1)

                def shift():
                    dve.wait_ge(mb_out, s)
                    mine = own[:, :, s - 1]
                    link(v.tensor_tensor(mall, PB[3][:, 256:264], mine, ALU.max))
                    ran(v.tensor_tensor(sc[:, c, NPAGE, :], mine, mall, ALU.subtract))
                    ran(v.tensor_tensor(scp, scp, bc(mall.unsqueeze(1), [P, NPAGE, H]), ALU.subtract))
                    settle()
                    v.sem_inc(sc_made, 1)

                def prompt_norm(h):
                    dve.wait_ge(ps_exp, 2 * (h + 1))
                    link(v.reciprocal(ri3, rs3))
                    ran(v.tensor_scalar(p3[:, 0:P], p3[:, 0:P], ri3[:, 0:1], None, ALU.mult))
                    ran(v.tensor_scalar(p3[:, P:3 * P], p3[:, P:3 * P], ri3[:, 1:2], None, ALU.mult))
                    settle()
                    v.sem_inc(ps_norm, 1)

                def row_sums():
                    dve.wait_ge(se_made, s)
                    v.tensor_reduce(rsum, pe4[:, c, 0:NPAGE, 0:H].rearrange("p g h -> p h g"), AX.X, ALU.add)\
                        .then_inc(rs_made, 1)

                def denominators():
                    dve.wait_ge(den_out, s)
                    link(v.tensor_tensor(den, PB[5][:, 264:272], pe4[:, c, NPAGE, 0:H], ALU.add))
                    link(v.reciprocal(rden, den))
                    v.tensor_tensor(own_w[:, :, s - 1], rden, pe4[:, c, NPAGE, 0:H], ALU.mult).then_inc(vec_own, 1)

                def result():
                    dve.wait_ge(o_out, s)
                    v.tensor_tensor(aT[:, :, NP_TOK + s - 1], rden, PB[3][:, 272:280], ALU.mult).then_inc(att_made, 1)

                after = {(0, 0): blocks, (0, 2): maxima, (0, 4): shift, (0, 6): row_sums, (1, 0): denominators,
                         (1, 6): result}
                prompt_after = {(0, 1): (prompt_max, 0), (0, 5): (prompt_norm, 0),
                                (1, 2): (prompt_max, 1), (1, 5): (prompt_norm, 1)}
                for half in range(2):
                    for g in range(NPAGE):
                        if s < NS:
                            keys(s, half, g)
                        if s >= 1 and (half, g) in after:
                            after[half, g]()
                        if (half, g) in prompt_after:
                            part, nth = prompt_after[half, g]
                            for h in PROMPT_HEADS[s][nth:nth + 1]:
                                part(h)
            dve.wait_ge(att_made, NS)
            dve.wait_ge(vec_own, NS)
            dve.wait_ge(vp_kept, 2 * H)
            link(v.tensor_tensor(own_w, own_w, vTs, ALU.mult))
            v.tensor_tensor(aT[:, :, NP_TOK:T], aT[:, :, NP_TOK:T], own_w, ALU.add).then_inc(att_made, 1)
            for j in range(KT):
                dve.wait_ge(wo_out, j + 1)
                v.tensor_tensor(xT[:, j, :], xT[:, j, :], PB[j % 2][:, 0:T], ALU.add).then_inc(wo_added, 1)
            dve.wait_ge(wo_added, KT)
            normed(3, [(hT, G_M + 1)])
            moe(1)
            for i in range(6):
                t, half = divmod(i, 2)
                n = TILES[t][1]
                dve.wait_ge(y_turned, i + 1)
                v.tensor_copy(yr[0:n, t, :].rearrange("q (p k) -> q k p", k=KT)[:, 4 * half:4 * half + 4, :],
                              PB[i % 4][0:n, :].rearrange("q (k p) -> q k p", k=4)).then_inc(yr_made, 1)


_OUTS = [("y_prompt", (1, 256, 1024)), ("y_sample", (8, 1, 1024)), ("v_rows_prompt", (1, 1, 128, 2048)),
         ("v_rows_sample", (1, 8, 1, 2048)), ("k_prompt", (1, 256, 8, 128)), ("v_prompt", (1, 256, 8, 128)),
         ("k_sample", (8, 1, 8, 128)), ("v_sample", (8, 1, 8, 128))]


def kernel(**inputs):
    import numpy as np
    import concourse.bacc as bacc
    from concourse.bass_utils import run_bass_kernel_spmd

    nc = bacc.Bacc("TRN2", target_bir_lowering=False, num_devices=1)
    arrays, a, o = {}, {}, {}
    for name, value in {**inputs, "consts": constants()}.items():
        value = np.ascontiguousarray(value)
        arrays["in_" + name] = value
        a[name] = nc.dram_tensor("in_" + name, value.shape, mybir.dt.from_np(value.dtype), kind="ExternalInput").ap()
    for name, shape in _OUTS:
        o[name] = nc.dram_tensor("out_" + name, shape, F32, kind="ExternalOutput").ap()
    program(nc, a, o)
    r = run_bass_kernel_spmd(nc, [arrays], core_ids=[0])
    return tuple(r.results[0]["out_" + name] for name, _ in _OUTS)
```

```python
from contextlib import ExitStack

import concourse.bass as bass
from concourse import mybir

F32, I32 = mybir.dt.float32, mybir.dt.int32
ACT, ALU, AX = mybir.ActivationFunctionType, mybir.AluOpType, mybir.AxisListType

P = 128
D = 1024
KT = D // P
NP_TOK, NS = 256, 8
T = NP_TOK + NS
TILES = [(0, P), (P, P), (2 * P, NS)]
GW = 2 * D
CT = GW // P
NG = 8
H, HD = 8, 128
ROT = HD // 4
V_HEADS = [tuple(range(H))] + [()] * NS
PROMPT_HEADS = [(), (0,), (1,), (2,), (3,), (4,), (5,), (6, 7), ()]
NE, NPAIR, EF = 16, 8, 512
FT = EF // P
NGRP, EPG = 4, 4
NPAGE, PAGE, NBLK = 8, 128, 4
CAP = 64
LIMIT = CAP
EPS = 1e-6
SCALE = HD ** -0.5
NEG = -1e30
MIX_AFTER = [6, 7, 9, 10, 12, 13, 14, 15]
ROWS_AT = [3, 4, 5, 6, 9, 10, 11, 12]
SMALL_LOADS = 16
SLOT = 4096


def const_layout():
    at, off = {}, 0
    for name, n in [("ident", P), ("ones", P), ("earlier", P), ("causal", 3 * P), ("iota", CAP), ("rot", ROT),
                    ("cos", T), ("sin", T), ("pick", 2 * NBLK), ("first", EPG), ("blk", NBLK), ("valid", 3)]:
        at[name] = (off, n)
        off += n
    return at, off


def constants():
    import numpy as np
    at, n = const_layout()
    c = np.zeros((P, n), np.float32)

    def put(name, value):
        o, w = at[name]
        c[:value.shape[0], o:o + w] = value.reshape(value.shape[0], w)
    i = np.arange(P)
    put("ident", np.eye(P))
    put("ones", np.ones((P, P)))
    put("earlier", i[:, None] < i[None, :])
    m = np.where(i[:, None] >= i[None, :], 0.0, NEG)
    put("causal", np.concatenate([m, np.zeros((P, P)), m], 1))
    put("iota", np.tile(np.arange(CAP), (P, 1)))
    r = np.zeros((P, ROT))
    half = ROT // 2
    for j in range(half):
        r[j + half, j], r[j, j + half] = -1.0, 1.0
    put("rot", r)
    freq = (500000.0 ** (-np.arange(half, dtype=np.float32) / half)).astype(np.float32)
    pos = np.concatenate([np.arange(NP_TOK), np.full(NS, NPAGE * PAGE)]).astype(np.float32)
    ang = (np.tile(freq, 2)[:, None] * pos[None]).astype(np.float32).astype(np.float64)
    put("cos", np.cos(ang))
    put("sin", np.sin(ang))
    s = np.zeros((P, NBLK, 2))
    for h in range(H):
        for parity in range(2):
            s[32 * (2 * parity + h // 4) + h, h % 4, h // 4] = 1.0
    put("pick", s)
    put("first", np.tile(np.arange(EPG) - 9.0, (P, 1)))
    put("blk", np.tile(np.arange(NBLK) + 1.0, (P, 1)))
    v = np.ones((P, 3))
    v[NS:, 2] = 0.0
    put("valid", v)
    return c


class Chain:

    def __init__(self, eng, sem):
        self.eng, self.sem, self.base, self.n = eng, sem, 0, 0

    def ran(self, ins):
        self.n += 1
        return ins.then_inc(self.sem, 1)

    def wait(self):
        self.eng.wait_ge(self.sem, self.base + self.n)

    def link(self, ins):
        self.ran(ins)
        self.wait()


def wait_for(eng, sem, n):
    if not isinstance(n, int) or n > 0:
        eng.wait_ge(sem, n)


def bc(ap, shape):
    return ap.to_broadcast(list(shape))


def program(nc, a, o):
    ctx = ExitStack()
    with ctx:
        def sb(name, shape, dt=F32):
            return ctx.enter_context(nc.sbuf_tensor(name, list(shape), dt))

        def sem(name):
            return ctx.enter_context(nc.semaphore(name))

        W = sb("ring", [P, 8, SLOT])
        xT = sb("xT", [P, KT, T])
        CL, CN = const_layout()
        C = sb("consts", [P, CN])

        def const(name):
            off, n = CL[name]
            return C[:, off:off + n]
        ident, ones, earlier = const("ident"), const("ones"), const("earlier")
        gains = sb("gains", [P, 5, KT])
        G_A, G_M, G_KV, G_B = 0, 1, 3, 4
        hgain = sb("hgain", [P, 2])
        wr = sb("wr", [P, 2, KT, NGRP + NE])
        rbias = sb("rbias", [P, 2, NGRP + NE])
        eps = sb("eps", [P, 1])
        table_used = sb("table_used", [P, 1])
        roots = sb("roots", [P, 2, T])
        rms, rstd = roots[:, 0, :], roots[:, 1, :]
        mixed = roots
        pages = sb("pages", [1, NS * NPAGE], I32)
        many = sb("many", [P, 1], I32)

        ARENA = 15880
        A = sb("arena", [P, ARENA])

        def region(off, *shape):
            n = 1
            for s in shape:
                n *= s
            assert off + n <= ARENA, (off, n)
            v = A[:, off:off + n]
            if len(shape) == 1:
                return v
            names = "abc"[:len(shape)]
            return v.rearrange(f"p ({' '.join(names)}) -> p {' '.join(names)}", **dict(zip(names, shape)))
        hT = region(0, KT, T)
        vT = region(2112, CT, T)
        vr = region(6336, 3, GW)
        lng = region(12480, 2, 512)
        wsT = region(13504, NG, P)
        bs = region(14528, NG, P)
        xr = region(6336, 3, D)
        wsr = region(2112 + 12 * T, NG, P)
        sqA = region(2112, KT, T)
        raw_g = [region(12480 + l * KT * NGRP, KT, NGRP) for l in range(2)]
        raw_e = [region(12544 + l * KT * NE, KT, NE) for l in range(2)]
        w00 = region(15768, NG)
        d8 = region(15616, NG, NS)
        stats = region(15680, 3, 4 * 6)
        mv = region(15752, 3, 2)
        vrstd = region(15758, 3)
        hr = region(2112, 3, D)
        sqM = region(5184, KT, T)
        hot = region(7296, 3, 2, CAP)
        ghot = region(7680, 3, 2, CAP)
        sT = region(8064, T)
        hg = region(8328, KT, P)
        sg = region(9352, EF)
        he = region(9864, EF)
        heT = region(10376, FT, P)
        dr = region(10888, D)
        lgT = region(11912, T)
        lg = region(12176, 3, NGRP + NE)
        ro = 12236

        def small(*shape):
            nonlocal ro
            n = 1
            for s in shape:
                n *= s
            ro += n
            return region(ro - n, *shape)
        gm, pg, mn, m1, m2, e2, w1, w2 = (small(3) for _ in range(8))
        ohg, oh1, oh2, leg, le2, cand, ex = (small(3, 4) for _ in range(7))
        prod = small(3, 16)
        gates = small(3, 16)
        chose = small(3, 16)
        rank = small(3, 16)
        sgD = region(2112, T)
        heD = region(2376, FT, T)
        gb = region(3432, 3, P)
        gcol = region(3816, T)
        hk, hq = region(0, KT, T), region(2112, KT, T)
        kq = region(4224, 2 * H, T)
        krows = region(8448, 3, D)
        vrows = region(11520, 3, D)
        sqB = region(8448, KT, T)
        sqh = region(14592, 2, T)
        rmh = region(15120, T)
        rsh = region(15384, T)
        turned = region(11520, T)
        vTh = region(14592, 2, T)
        vTs = region(15384, H, NS)
        own = region(15448, H, NS)
        ownp = region(15512, H, NS)
        own_w = region(15576, H, NS)
        aT = region(2112, H, T)
        s3 = region(8448, 3 * P)
        p3 = region(8832, 3 * P)
        pT3 = region(9216, 3 * P)
        mx3, rs3, ri3 = region(9600, 2), region(9602, 2), region(9604, 2)
        sc = region(9608, 2, NPAGE + 1, H)
        pe4 = region(9752, 2, NPAGE + 1, 32)
        ov = region(10328, 512)
        gsum, eqb, drop = region(10840, NBLK, H), region(10872, NBLK, H), region(10904, NBLK, H)
        mnb, vmb, pmx, mall, rsum, den, rden, tmp8 = (region(10936 + 8 * i, H) for i in range(8))
        dg = region(11000, H)
        hm = region(11008, 1)
        yr = region(2112, 3, D)

        PB = [ctx.enter_context(nc.psum_tensor(f"bank{i}", [P, 512], F32)) for i in range(8)]

        V_FIRST = 4

        def y_half(t, n, half):
            return yr[0:n, t, :].rearrange("q (p k) -> q k p", k=KT)[:, 4 * half:4 * half + 4, :]

        def v_bank(j):
            return PB[(0, 1, 3, 7)[j]] if j < V_FIRST else PB[j % 2]

        def y_bank(i, j):
            last_pair = isinstance(i, int) and i == NPAIR - 1
            return PB[(6, 7)[j % 2] if last_pair else (6, 7, 0, 1)[j % 4]]

        def acc(g):
            return PB[(0, 1, 7)[g % 3]]

        def v_acc(h):
            return PB[(h + 1) % 2]

        GATE0, UP0, DOWN0 = (4, 0), (6, 2), (0, 6)
        GATE_ODD, GATE_EVEN, UP, DOWN = (2, 4), (0, 6), (4, 0), (6, 2)
        W_K, W_Q, W_V, W_O = 0, 2, 4, 4
        K_SLOT = [6, 2, 4, 2, 4, 2, 4, 2]
        V_SLOT = [0, 6, 0, 6, 0, 6, 0, 6]
        filled, before = [0] * 8, {}

        def stage(name, first, slots=2, each=16, times=1):
            before[name] = list(filled)
            for s in range(first, first + slots):
                filled[s] += each * times

        def expert_stages(l):
            for name, first in (("gate", GATE0), ("up", UP0), ("down", DOWN0)):
                stage(f"{name}0_{l}", first[l])
            stage(f"gate_odd{l}", GATE_ODD[l], times=NPAIR // 2)
            stage(f"gate_even{l}", GATE_EVEN[l], times=NPAIR // 2 - 1)
            stage(f"up{l}", UP[l], times=NPAIR - 1)
            stage(f"down{l}", DOWN[l], times=NPAIR - 1)
        stage("v", 0, 4)
        stage("u", 4, 4)
        stage("wout", 0, 4)
        expert_stages(0)
        stage("w_k", W_K)
        stage("w_q", W_Q)
        stage("w_v", W_V)
        for s in range(NS):
            stage(f"K{s}", K_SLOT[s], each=64)
            stage(f"V{s}", V_SLOT[s], each=64)
        stage("w_o", W_O)
        expert_stages(1)

        full = [sem(f"full{s}") for s in range(8)]

        def arrived(eng, name, slot, nth=1, each=16):
            eng.wait_ge(full[slot], before[name][slot] + each * nth)

        c_load, x_load, g_load, page_load = sem("c_load"), sem("x_load"), sem("g_load"), sem("page_load")
        ga_load, ws_load = sem("ga_load"), sem("ws_load")
        eps_set, wr_made, ws_masked = sem("eps_set"), sem("wr_made"), sem("ws_masked")
        ws_turned, ws_kept = sem("ws_turned"), sem("ws_kept")
        x_turned, x_kept = sem("x_turned"), sem("x_kept")
        sq_made, ss_out, rms_made, rstd_made, h_made = (sem(n) for n in
                                                        ["sq_made", "ss_out", "rms_made", "rstd_made", "h_made"])
        v_out, v_gelu, v_turned, v_kept = sem("v_out"), sem("v_gelu"), sem("v_turned"), sem("v_kept")
        mv_made, vsd_made, ln_load, ln_used = (sem(n) for n in
                                                        ["mv_made", "vsd_made", "ln_load", "ln_used"])
        u_out, u_gelu, mix_out, um_made = sem("u_out"), sem("u_gelu"), sem("mix_out"), sem("um_made")
        a_out, a_added = sem("a_out"), sem("a_added")
        vec, v_rows_out, vec_own = sem("vector_steps"), sem("v_rows_out"), sem("own_weights_made")
        stored, y_stored = sem("stored"), sem("y_stored")
        L2 = range(2)

        def pair_of(name):
            return [sem(f"{name}{l}") for l in L2]
        lgT_out, lgT_made, lg_out, hr_out, hr_kept = (sem(n) for n in ["lgT_out", "lgT_made", "lg_out", "hr_out", "hr_kept"])
        gates_made = sem("gates_made")
        soft_in, soft_out, chose_made, rank_out, many_set, moe_done = (sem(n) for n in [
            "soft_in", "soft_out", "chose_made", "rank_out", "many_set", "moe_done"])
        gate_out, up_out, down_out = (pair_of(n) for n in ["gate_out", "up_out", "down_out"])
        hot_made, ghot_made, gather_out, hg_lo, hg_hi = (pair_of(n) for n in [
            "hot_made", "ghot_made", "gather_out", "hg_lo", "hg_hi"])
        silu_made, he_made, heT_out, heT_made = (pair_of(n) for n in ["silu_made", "he_made", "heT_out", "heT_made"])
        dr_lo, dr_hi, sT_out, sT_made, y_out, y_added = (pair_of(n) for n in [
            "dr_lo", "dr_hi", "sT_out", "sT_made", "y_out", "y_added"])
        gb_made, gcol_out, gcol_made, gD_out, sD_made, hD_made, yD_out, yD_added = (pair_of(n) for n in [
            "gb_made", "gcol_out", "gcol_made", "gD_out", "sD_made", "hD_made", "yD_out", "yD_added"])
        vecD = pair_of("vector_steps_all")
        kq_out, kq_sq, kq_ss, kq_rms, kq_normed, kq_rot, kq_made = (sem(n) for n in [
            "kq_out", "kq_sq", "kq_ss", "kq_rms", "kq_normed", "kq_rot", "kq_made"])
        vp_out, vp_kept, rows_out, rows_kept, v_rows_kept = (
            sem(n) for n in ["vp_out", "vp_kept", "rows_out", "rows_kept", "v_rows_kept"])
        own_in, own_out, own_made, k_stored, pad_set = (sem(n) for n in ["own_in", "own_out", "own_made", "k_stored", "pad_set"])
        ps_out, ps_max, ps_exp, ps_norm, pT_out, pT_made, po_out, po_kept = (sem(n) for n in [
            "ps_out", "ps_max", "ps_exp", "ps_norm", "pT_out", "pT_made", "po_out", "po_kept"])
        qb_out, s_made, gs_out, pm_made, pm_turned, dg_made, mb_out, sc_made, se_made, rs_made, den_out = (
            sem(n) for n in ["qb_out", "s_made", "gs_out", "pm_made", "pm_turned", "dg_made", "mb_out",
                             "sc_made", "se_made", "rs_made", "den_out"])
        pv_out, ov_made, o_out, att_made = sem("pv_out"), sem("ov_made"), sem("o_out"), sem("att_made")
        wo_out, wo_added = sem("wo_out"), sem("wo_added")
        y_turned, yr_made, yr_late = sem("y_turned"), sem("yr_made"), sem("yr_late")

        block = ctx.enter_context(nc.Block())

        def w_rows(ap, k):
            return ap.rearrange("(p k) n -> p k n", k=k)

        def slot(s, k):
            return W[:, s, :].rearrange("p (k n) -> p k n", k=k)

        @block.sync
        def _(sp):
            sp.dma_start(xr[:, 0:2, :], a["x_prompt"][0].rearrange("(t p) d -> p t d", p=P)).then_inc(x_load, 16)
            sp.dma_start(xr[0:NS, 2, :], a["x_sample"].rearrange("b s d -> (b s) d")).then_inc(x_load, 16)
            w_in = w_rows(a["a_w_in"][0], KT)
            for q in range(4):
                sp.dma_start(slot(q, 2), w_in[:, 2 * q:2 * q + 2, GW:2 * GW]).then_inc(full[q], 16)
            for q in range(4):
                sp.dma_start(slot(4 + q, 2), w_in[:, 2 * q:2 * q + 2, 0:GW]).then_inc(full[4 + q], 16)
            w_out = a["a_w_out"][0].rearrange("(c p) n -> p c n", p=P)
            sp.wait_ge(v_out, CT)
            for q in range(4):
                sp.wait_ge(ln_load, 32 * (q + 1))
                sp.dma_start(slot(q, 4), w_out[:, 4 * q:4 * q + 4, :]).then_inc(full[q], 16)

            def experts(layer):
                gate = a["moe_w_gate"][layer].rearrange("e (p k) n -> e p k n", k=KT)
                up = a["moe_w_up"][layer].rearrange("e (p k) n -> e p k n", k=KT)
                down = a["moe_w_down"][layer].rearrange("e (f p) n -> e p f n", p=P)

                def load(i, first, weights, k):
                    for e in range(2):
                        sp.dma_start(slot(first + e, k), weights[bass.ds(2 * i + e, 1)].rearrange("e p k n -> (e p) k n"))\
                            .then_inc(full[first + e], 16)

                load(0, GATE0[layer], gate, KT)
                if layer == 1:
                    sp.wait_ge(s_made, 2 * NS)
                load(0, UP0[layer], up, KT)
                if layer == 0:
                    sp.wait_ge(a_out, KT)
                else:
                    sp.wait_ge(pv_out, NS)
                load(0, DOWN0[layer], down, FT)
                if layer == 1:
                    sp.wait_ge(wo_out, KT)
                load(1, GATE_ODD[layer], gate, KT)
                sp.wait_ge(gate_out[layer], 1)
                load(1, UP[layer], up, KT)
                sp.wait_ge(up_out[layer], 1)
                load(1, DOWN[layer], down, FT)
                sp.wait_ge(down_out[layer], 1)

                def load_pair(i, gate_slot):
                    sp.wait_ge(gate_out[layer], i - 1)
                    load(i, gate_slot, gate, KT)
                    sp.wait_ge(up_out[layer], i)
                    load(i, UP[layer], up, KT)
                    sp.wait_ge(down_out[layer], i)
                    load(i, DOWN[layer], down, FT)
                with sp.Fori(1, NPAIR // 2) as j:
                    load_pair(2 * j, GATE_EVEN[layer])
                    load_pair(2 * j + 1, GATE_ODD[layer])

            sp.wait_ge(u_out, CT)
            experts(0)

            def load_square(w, first):
                for q in range(2):
                    sp.dma_start(slot(first + q, 4), w[:, 4 * q:4 * q + 4, :]).then_inc(full[first + q], 16)
            w_kv = w_rows(a["w_kv"], KT)
            sp.wait_ge(gate_out[0], NPAIR - 1)
            load_square(w_kv[:, :, 0:D], W_K)
            sp.wait_ge(gate_out[0], NPAIR)
            load_square(w_rows(a["b_w_q"][0], KT), W_Q)
            sp.wait_ge(up_out[0], NPAIR)
            load_square(w_kv[:, :, D:2 * D], W_V)

            sp.wait_ge(page_load, 16)

            def load_pages(pool, s, first):
                for g in range(NPAGE):
                    page = sp.value_load(pages[0:1, s * NPAGE + g:s * NPAGE + g + 1],
                                         min_val=0, max_val=pool.shape[0] - 1)
                    sp.dma_start(W[:, first + g // 4, (g % 4) * D:(g % 4 + 1) * D],
                                 pool[bass.ds(page, 1)].rearrange("a p h d -> (a p) (h d)"))\
                        .then_inc(full[first + g // 4], 16)
            keys_free = [(down_out[0], NPAIR), (kq_out, 2 * H), (vp_out, H)] + [(s_made, 2 * (s - 1)) for s in range(3, NS)]
            values_free = [(kq_out, H), (s_made, 2)] + [(pv_out, s - 1) for s in range(2, NS)]
            for s in range(NS):
                sp.wait_ge(*keys_free[s])
                load_pages(a["cache_k"], s, K_SLOT[s])
                sp.wait_ge(*values_free[s])
                load_pages(a["cache_v"], s, V_SLOT[s])
            sp.wait_ge(s_made, 2 * (NS - 1))
            w_o = a["b_w_o"][0].rearrange("(h p) n -> p h n", p=P)
            load_square(w_o, W_O)
            sp.wait_ge(pv_out, NS - 1)
            experts(1)
            for t, (t0, n) in enumerate(TILES):
                sp.wait_ge(yr_made, t + 1)
                sp.wait_ge(yr_late, t + 1)
                dst = o["y_prompt"][0, t0:t0 + n, :] if t < 2 else o["y_sample"].rearrange("b s d -> (b s) d")
                sp.dma_start(dst, yr[0:n, t, :]).then_inc(y_stored, 16)
            sp.wait_ge(y_stored, 16 * 3)
            sp.wait_ge(stored, 16 * 4)
            sp.wait_ge(k_stored, 16 * 2)

        @block.gpsimd
        def _(pool):
            pool.wait_ge(ws_load, 16)
            nc.gpsimd.affine_select(out=wsr, in_=wsr, compare_op=ALU.is_ge, fill=0.0, base=0,
                                    pattern=[[0, NG], [-1, P]], channel_multiplier=1).then_inc(ws_masked, 1)
            pool.wait_ge(g_load, 16 * SMALL_LOADS)
            for l in L2:
                for src, lo, n in ((raw_g[l], 0, NGRP), (raw_e[l], NGRP, NE)):
                    nc.gpsimd.tensor_tensor(wr[:, l, :, lo:lo + n], src, bc(gains[:, G_M + l, :].unsqueeze(2), [P, KT, n]),
                                            ALU.mult).then_inc(wr_made, 1)
            for c in range(4):
                if c == 0:
                    pool.wait_ge(wr_made, 4)
                else:
                    pool.wait_ge(ln_used, c)
                for i, name in enumerate(("a_ln_g", "a_ln_b")):
                    pool.dma_start(lng[:, i, :], a[name][0:1, 512 * c:512 * (c + 1)].partition_broadcast(P))\
                        .then_inc(ln_load, 16)
            pool.wait_ge(ln_used, 4)
            pool.dma_start(o["v_rows_prompt"][0, 0], vr[:, 1, :]).then_inc(stored, 16)
            pool.dma_start(o["v_rows_sample"][0].rearrange("b s n -> (b s) n"), vr[0:NS, 2, :]).then_inc(stored, 16)

            def moe(l):
                pool.wait_ge(rstd_made, 2 * l + 2)
                for k in range(KT):
                    nc.gpsimd.tensor_tensor(hT[:, k, :], hT[:, k, :], rstd, ALU.mult).then_inc(h_made, 1)
                pool.wait_ge(many_set, l + 1)
                flag = pool.value_load(many[P - 1:P, 0:1], min_val=0, max_val=T)
                with pool.If(flag > LIMIT):
                    pool.nop()
                with pool.Else():
                    def weigh(i):
                        if isinstance(i, int) and i == 0:
                            pool.wait_ge(gates_made, l + 1)
                        pool.wait_ge(hot_made[l], i + 1)
                        if not isinstance(i, int):
                            pool.wait_ge(sT_out[l], i)
                        elif i:
                            pool.wait_ge(sT_out[l], i)
                        nc.gpsimd.tensor_tensor(ghot, hot, bc(gates[:, :, bass.ds(2 * i, 2)].unsqueeze(3),
                                                              [P, 3, 2, CAP]), ALU.mult).then_inc(ghot_made[l], 1)
                    weigh(0)
                    with pool.Fori(1, NPAIR) as i:
                        weigh(i)
                pool.nop()
            moe(0)
            nc.gpsimd.wait_ge(rows_kept, 6)
            for rows, kname in ((krows, "k"), (vrows, "v")):
                if kname == "v":
                    pool.wait_ge(v_rows_kept, 2 * H)
                s_ = k_stored if kname == "k" else stored
                pool.dma_start(o[kname + "_prompt"][0].rearrange("(t p) h d -> p t (h d)", p=P),
                               rows[:, 0:2, :]).then_inc(s_, 16)
                pool.dma_start(o[kname + "_sample"].rearrange("b s h d -> (b s) (h d)"),
                               rows[0:NS, 2, :]).then_inc(s_, 16)
                if kname == "k":
                    pool.wait_ge(k_stored, 32)
                    nc.gpsimd.memset(pe4, 0.0).then_inc(pad_set, 1)
            moe(1)

        @block.scalar
        def _(act):
            act.dma_start(C[:, 0:2 * P], a["consts"][:, 0:2 * P]).then_inc(c_load, 16)
            act.dma_start(gains[:, G_A, :], a["a_norm_g"][0].rearrange("(p k) -> p k", k=KT)).then_inc(ga_load, 16)
            act.wait_ge(eps_set, 1)

            def load_table(func):
                nc.scalar.activation(table_used[:, 0:1], eps[:, 0:1], func)

            def square_and_root(n, sq, ready, base):
                load_table(ACT.Sqrt)
                for k in range(KT):
                    act.wait_ge(ready, base + k + 1)
                    nc.scalar.activation(sq[:, k, :], xT[:, k, :], ACT.Square).then_inc(sq_made, 1)
                    if n in (1, 3):
                        nc.scalar.activation(hT[:, k, :], xT[:, k, :], ACT.Copy, scale=gains[:, G_M + n // 2, k:k + 1])
                act.wait_ge(ss_out, n + 1)
                nc.scalar.activation(rms[:, :], PB[2][:, 0:T], ACT.Sqrt, bias=eps[:, 0:1], scale=1.0 / D)\
                    .then_inc(rms_made, 1)
            square_and_root(0, sqA, x_kept, 0)

            act.dma_start(C[:, 2 * P:CN], a["consts"][:, 2 * P:CN]).then_inc(g_load, 16)
            act.dma_start(wsr, a["a_w_s"][0].rearrange("g t s -> t g s")).then_inc(ws_load, 16)
            act.dma_start(bs.rearrange("p g t -> p (g t)"), a["a_b_s"].rearrange("a g t -> a (g t)").partition_broadcast(P))\
                .then_inc(g_load, 16)
            for i, g in ((G_M, a["moe_norm_g"][0]), (G_M + 1, a["moe_norm_g"][1]), (G_KV, a["kv_norm_g"]),
                         (G_B, a["b_norm_g"][0])):
                act.dma_start(gains[:, i, :], g.rearrange("(p k) -> p k", k=KT)).then_inc(g_load, 16)
            act.dma_start(hgain[:, 0:1], a["k_norm_g"].rearrange("(p k) -> p k", k=1)).then_inc(g_load, 16)
            act.dma_start(hgain[:, 1:2], a["q_norm_g"][0].rearrange("(p k) -> p k", k=1)).then_inc(g_load, 16)
            for l in L2:
                act.dma_start(rbias[:, l, 0:NGRP], a["moe_b_rg"][l:l + 1, :].partition_broadcast(P)).then_inc(g_load, 16)
                act.dma_start(rbias[:, l, NGRP:], a["moe_b_re"][l:l + 1, :].partition_broadcast(P)).then_inc(g_load, 16)
                act.dma_start(raw_g[l], a["moe_w_rg"][l].rearrange("(p k) n -> p k n", k=KT)).then_inc(g_load, 16)
                act.dma_start(raw_e[l], a["moe_w_re"][l].rearrange("(p k) n -> p k n", k=KT)).then_inc(g_load, 16)
            act.dma_start(pages[:, :], a["page_table"].rearrange("b n -> (b n)").rearrange("(a n) -> a n", a=1))\
                .then_inc(page_load, 16)

            for j in range(CT):
                if j == 12:
                    act.wait_ge(ws_turned, 3)
                act.wait_ge(v_out, j + 1)
                nc.scalar.activation(vT[:, j, :], v_bank(j)[:, 0:T], ACT.Gelu_apprx_tanh).then_inc(v_gelu, 1)
            act.wait_ge(mv_made, 1)
            nc.scalar.activation(vrstd, mv[:, :, 1], ACT.Sqrt, bias=eps[:, 0:1]).then_inc(vsd_made, 1)
            for j in range(CT):
                act.wait_ge(u_out, j + 1)
                nc.scalar.activation(vT[:, j, :], PB[j % 2][:, 0:T], ACT.Gelu_apprx_tanh).then_inc(u_gelu, 1)

            def moe(l):
                load_table(ACT.Exp)
                for i in range(6):
                    half, t = divmod(i, 3)
                    n = TILES[t][1]
                    act.wait_ge(hr_out, 6 * l + i + 1)
                    nc.scalar.activation(hr[0:n, t, 512 * half:512 * (half + 1)], PB[4 + i % 4][0:n, :], ACT.Copy)\
                        .then_inc(hr_kept, 1)
                act.wait_ge(soft_in, 2 * l + 1)
                nc.scalar.activation(ex, ex, ACT.Exp).then_inc(soft_out, 1)
                act.wait_ge(soft_in, 2 * l + 2)
                nc.scalar.activation(e2, e2, ACT.Exp).then_inc(soft_out, 1)

                def copy_hg(i):
                    act.wait_ge(gather_out[l], i + 1)
                    nc.scalar.activation(hg[:, 0:4, :], PB[0][:, :].rearrange("p (k s) -> p k s", k=4), ACT.Copy)\
                        .then_inc(hg_lo[l], 1)
                load_table(ACT.Silu)
                copy_hg(0)
                act.wait_ge(many_set, l + 1)
                flag = act.value_load(many[P - 1:P, 0:1], min_val=0, max_val=T)
                with act.If(flag > LIMIT):
                    def all_tokens(i):
                        for c in range(2 * FT):
                            act.wait_ge(gD_out[l], i * (2 * FT) + c + 1)
                            wait_for(act, hD_made[l], i * (2 * FT) + c)
                            nc.scalar.activation(sgD, PB[c % 2][:, 0:T], ACT.Silu).then_inc(sD_made[l], 1)
                    all_tokens(0)
                    with act.Fori(1, NPAIR) as i:
                        all_tokens(i)
                with act.Else():
                    def pair(i, last):
                        act.wait_ge(gate_out[l], i + 1)
                        nc.scalar.activation(sg, PB[2][:, :], ACT.Silu).then_inc(silu_made[l], 1)
                        act.wait_ge(heT_out[l], i + 1)
                        nc.scalar.activation(heT, PB[6][:, :].rearrange("p (f s) -> p f s", f=FT), ACT.Copy)\
                            .then_inc(heT_made[l], 1)
                        if not last:
                            copy_hg(i + 1)
                        act.wait_ge(down_out[l], i + 1)
                        nc.scalar.activation(dr[:, 0:512], PB[4][:, :], ACT.Copy).then_inc(dr_lo[l], 1)
                    with act.Fori(0, NPAIR - 1) as i:
                        pair(i, False)
                    pair(NPAIR - 1, True)
                act.nop()
            act.wait_ge(stored, 32)
            square_and_root(1, sqB, a_added, 0)
            moe(0)
            square_and_root(2, sqB, moe_done, 0)

            def rows_copy(g, rows):
                for t, (_, n) in enumerate(TILES):
                    act.wait_ge(rows_out, g + 1)
                    nc.scalar.activation(rows[0:n, t, 512 * (g % 2):512 * (g % 2 + 1)], PB[4 + t][0:n, :], ACT.Copy)\
                        .then_inc(rows_kept, 1)
            for g in range(2 * H + 1):
                if g < 2 * H:
                    act.wait_ge(kq_out, g + 1)
                    if g >= 2:
                        act.wait_ge(kq_ss, g - 1)
                    nc.scalar.activation(sqh[:, g % 2, :], acc(g)[:, 0:T], ACT.Square).then_inc(kq_sq, 1)
                if g >= 1:
                    act.wait_ge(kq_ss, g)
                    if g >= 2:
                        act.wait_ge(kq_normed, g - 1)
                    nc.scalar.activation(rmh, PB[2][:, 0:T], ACT.Sqrt, bias=eps[:, 0:1], scale=1.0 / HD)\
                        .then_inc(kq_rms, 1)
                if g - 1 in (ROWS_AT[3], ROWS_AT[7]):
                    rows_copy(ROWS_AT.index(g - 1) // 4, krows)
            def exp_prompt(h):
                act.wait_ge(ps_max, h + 1)
                for q, (lo, n) in enumerate(((0, P), (P, 2 * P))):
                    nc.scalar.activation(p3[:, lo:lo + n], s3[:, lo:lo + n], ACT.Exp, bias=mx3[:, q:q + 1],
                                         scale=SCALE, accum_out=rs3[:, q:q + 1]).then_inc(ps_exp, 1)

            def keep_pT(h):
                act.wait_ge(pT_out, h + 1)
                if h:
                    act.wait_ge(po_out, h)
                nc.scalar.activation(pT3, PB[1][:, 0:3 * P], ACT.Copy).then_inc(pT_made, 1)

            def keep_po(h):
                act.wait_ge(po_out, h + 1)
                nc.scalar.activation(aT[:, h, 0:NP_TOK], PB[2][:, 0:NP_TOK], ACT.Copy).then_inc(po_kept, 1)

            def keep_v(h):
                if h == 0:
                    act.wait_ge(kq_normed, 2 * H)
                act.wait_ge(vp_out, h + 1)
                if h >= 2:
                    act.wait_ge(v_rows_out, h - 1)
                nc.scalar.activation(vTh[:, h % 2, :], v_acc(h)[:, 0:T], ACT.Copy).then_inc(vp_kept, 1)
                nc.scalar.activation(vTs[:, h, :], v_acc(h)[:, NP_TOK:T], ACT.Copy).then_inc(vp_kept, 1)

            def keep_v_rows(h):
                act.wait_ge(v_rows_out, h + 1)
                nc.scalar.activation(vrows[:, 0:2, h * HD:(h + 1) * HD],
                                     PB[2][:, 0:2 * P].rearrange("p (t d) -> p t d", t=2), ACT.Copy)\
                    .then_inc(v_rows_kept, 1)
                nc.scalar.activation(vrows[0:NS, 2, h * HD:(h + 1) * HD], PB[2][0:NS, 2 * P:3 * P], ACT.Copy)\
                    .then_inc(v_rows_kept, 1)
            act.wait_ge(pad_set, 1)
            for s in range(NS + 1):
                prompt = PROMPT_HEADS[s]
                if prompt:
                    exp_prompt(prompt[0])
                if s >= 1:
                    c = (s - 1) % 2
                    act.wait_ge(sc_made, s)
                    nc.scalar.activation(pe4[:, c, :, 0:H], sc[:, c, :, :], ACT.Exp, scale=SCALE).then_inc(se_made, 1)
                if prompt:
                    keep_pT(prompt[0])
                for h in prompt[1:]:
                    exp_prompt(h)
                if s >= 1:
                    act.wait_ge(pv_out, s)
                    if s >= 2:
                        act.wait_ge(o_out, s - 1)
                    nc.scalar.activation(ov, PB[4][:, :], ACT.Copy).then_inc(ov_made, 1)
                if prompt:
                    keep_po(prompt[0])
                for h in prompt[1:]:
                    keep_pT(h)
                    keep_po(h)
                for h in V_HEADS[s]:
                    keep_v(h)
                    if h:
                        keep_v_rows(h - 1)
                    if h == H - 1:
                        keep_v_rows(h)
            act.wait_ge(stored, 64)
            square_and_root(3, sqM, wo_added, 0)
            moe(1)
            act.wait_ge(y_turned, 2)
            for t, (_, n) in enumerate(TILES):
                nc.scalar.activation(y_half(t, n, 1), PB[3 + t][0:n, :].rearrange("q (k p) -> q k p", k=4), ACT.Copy)\
                    .then_inc(yr_late, 1)

        @block.tensor
        def _(pe):
            mm, tr = nc.tensor.matmul, nc.tensor.transpose

            pe.wait_ge(c_load, 16)
            pe.wait_ge(x_load, 32)
            def sum_square(n, sq, k):
                pe.wait_ge(sq_made, KT * n + k + 1)
                last = mm(PB[2][:, 0:T], ones, sq[:, k, :], start=(k == 0), stop=(k == KT - 1))
                if k == KT - 1:
                    last.then_inc(ss_out, 1)

            def sum_and_route(l, sq, k):
                sum_square(2 * l + 1, sq, k)
                if k == 0 and l == 0:
                    pe.wait_ge(wr_made, 4)
                    pe.wait_ge(g_load, 16 * SMALL_LOADS)
                last = mm(PB[3][0:NGRP + NE, 0:T], wr[:, l, k, :], xT[:, k, :], start=(k == 0), stop=(k == KT - 1))
                if k == KT - 1:
                    last.then_inc(lgT_out, 1)
            for k in range(KT):
                if k >= 2:
                    pe.wait_ge(x_kept, k - 1)
                for t, (t0, n) in enumerate(TILES):
                    last = tr(PB[k % 2][:, t0:t0 + n], xr[0:n, t, k:D:KT], ident[0:n, 0:n])
                last.then_inc(x_turned, 1)
                if k >= 2:
                    sum_square(0, sqA, k - 2)
            sum_square(0, sqA, KT - 2)
            sum_square(0, sqA, KT - 1)

            def turn_mixing():
                pe.wait_ge(ws_masked, 1)
                for half, bank in ((0, PB[3]), (1, PB[7])):
                    for g in range(4):
                        last = tr(bank[:, g * P:(g + 1) * P], wsr[:, 4 * half + g, :], ident)
                    last.then_inc(ws_turned, 1)
                pe.wait_ge(rms_made, 1)
                mm(PB[2][0:NS, 0:NG], ones[0:1, 0:NS], wsr[0:1, :, 0], start=True, stop=True).then_inc(ws_turned, 1)

            def turn_v(j):
                pe.wait_ge(v_gelu, j + 1)
                if j % 4 == 0:
                    if j:
                        pe.wait_ge(v_kept, 6 * (j // 4))
                    if j == 8:
                        turn_mixing()
                for t, (t0, n) in enumerate(TILES):
                    last = tr(PB[4 + t][0:n, (j % 4) * P:(j % 4 + 1) * P], vT[:, j, t0:t0 + n], ident)
                if j % 4 == 3:
                    last.then_inc(v_turned, 1)

            def mix(g):
                if g == 0:
                    pe.wait_ge(ws_kept, 3)
                pe.wait_ge(ln_used, g // 2 + 1)
                if g >= 2:
                    pe.wait_ge(um_made, 2 * (g - 1))
                for i in range(2):
                    for t, (t0, n) in enumerate(TILES):
                        to = PB[4 + g % 2][:, (2 * i + t) * P:(2 * i + t + 1) * P] if t < 2 else \
                            PB[6 + g % 2][:, i * NS:(i + 1) * NS]
                        last = mm(to, vr[0:n, t, (2 * g + i) * P:(2 * g + i + 1) * P],
                                  wsT[:, g, :] if t < 2 else d8[0:NS, g, :], start=True, stop=True)
                last.then_inc(mix_out, 1)

            def w_in_product(base, j, k, bank):
                return mm(bank[:, 0:T], slot(base + k // 2, 2)[:, k % 2, j * P:(j + 1) * P], hT[:, k, :],
                          start=(k == 0), stop=(k == KT - 1))

            for k in range(KT):
                pe.wait_ge(h_made, k + 1)
                if k % 2 == 0:
                    arrived(pe, "v", k // 2)
                for j in range(V_FIRST):
                    last = w_in_product(0, j, k, v_bank(j))
                    if k == KT - 1:
                        last.then_inc(v_out, 1)
            for j in range(V_FIRST, CT):
                pe.wait_ge(v_gelu, (j - 1 if j > V_FIRST + 1 else j - V_FIRST + 1))
                for k in range(KT):
                    last = w_in_product(0, j, k, v_bank(j))
                last.then_inc(v_out, 1)
                if j == V_FIRST:
                    for i in range(V_FIRST - 1):
                        turn_v(i)
                turn_v(j - 1)
            turn_v(CT - 1)
            pe.wait_ge(v_gelu, CT)
            for j in range(CT):
                if j >= 2:
                    pe.wait_ge(u_gelu, j - 1)
                for k in range(KT):
                    if j == 0 and k % 2 == 0:
                        arrived(pe, "u", 4 + k // 2)
                    last = w_in_product(4, j, k, PB[j % 2])
                last.then_inc(u_out, 1)
                if j in MIX_AFTER:
                    mix(MIX_AFTER.index(j))

            for j in range(KT):
                if j >= 2:
                    pe.wait_ge(a_added, j - 1)
                else:
                    pe.wait_ge(u_gelu, CT)
                for c in range(CT):
                    if j == 0 and c % 2 == 0:
                        pe.wait_ge(um_made, c + 2)
                    if j == 0:
                        if c % 4 == 0:
                            arrived(pe, "wout", c // 4)
                    last = mm(PB[j % 2][:, 0:T], slot(c // 4, 4)[:, c % 4, j:D:KT], vT[:, c, :],
                              start=(c == 0), stop=(c == CT - 1))
                last.then_inc(a_out, 1)
                if j >= 2:
                    sum_and_route(0, sqB, j - 2)
            sum_and_route(0, sqB, KT - 2)
            sum_and_route(0, sqB, KT - 1)

            def keep_clock(n):
                for _ in range(n):
                    mm(PB[0][:, 0:P], ident, ident, start=True, stop=True)

            def turn_y(k):
                pe.wait_ge(moe_done, KT + k + 1)
                for t, (t0, n) in enumerate(TILES):
                    last = tr(PB[3 * (k // 4) + t][0:n, (k % 4) * P:(k % 4 + 1) * P], xT[:, k, t0:t0 + n], ident)
                if k % 4 == 3:
                    last.then_inc(y_turned, 1)

            def moe(l, h_before):
                def weights_of(i, odd, nth):
                    if isinstance(i, int) and i == 0:
                        return (GATE0[l], f"gate0_{l}", 1), (UP0[l], f"up0_{l}", 1), (DOWN0[l], f"down0_{l}", 1)
                    gate = (GATE_ODD[l], f"gate_odd{l}", nth) if odd else (GATE_EVEN[l], f"gate_even{l}", nth)
                    return gate, (UP[l], f"up{l}", i), (DOWN[l], f"down{l}", i)

                keep_clock(10)
                pe.wait_ge(lgT_made, l + 1)
                for t, (t0, n) in enumerate(TILES):
                    last = tr(PB[2][0:n, t * 20:(t + 1) * 20], lgT[0:NGRP + NE, t0:t0 + n], ident[0:20, 0:20])
                last.then_inc(lg_out, 1)

                def rows(i):
                    half, t = divmod(i, 3)
                    t0, n = TILES[t]
                    if i >= 4:
                        pe.wait_ge(hr_kept, 6 * l + i - 3)
                    for q in range(4):
                        if t == 0:
                            pe.wait_ge(h_made, h_before + 4 * half + q + 1)
                        last = tr(PB[4 + i % 4][0:n, q * P:(q + 1) * P], hT[:, 4 * half + q, t0:t0 + n], ident)
                    last.then_inc(hr_out, 1)
                for i in range(4):
                    rows(i)
                pe.wait_ge(chose_made, l + 1)
                ranks = PB[3][:, 0:3 * NE]
                mm(ranks, earlier, chose.rearrange("p t e -> p (t e)"), start=True, stop=False)
                mm(ranks[:, NE:3 * NE].rearrange("p (t e) -> p t e", t=2), ones,
                   bc(chose[:, 0:1, :], [P, 2, NE]), start=False, stop=False)
                mm(ranks[:, 2 * NE:3 * NE], ones, chose[:, 1, :], start=False, stop=True).then_inc(rank_out, 1)
                rows(4)
                rows(5)

                def gather(i):
                    pe.wait_ge(hot_made[l], i + 1)
                    for k in range(KT):
                        for t, (t0, n) in enumerate(TILES):
                            last = mm(PB[k // 4][:, (k % 4) * P:(k % 4 + 1) * P], hr[0:n, t, k * P:(k + 1) * P],
                                      hot[0:n, t, :, :].rearrange("p e s -> p (e s)"), start=(t == 0), stop=(t == 2))
                    last.then_inc(gather_out[l], 1)
                keep_clock(4)
                pe.wait_ge(hr_kept, 6 * l + 6)
                gather(0)
                pe.wait_ge(many_set, l + 1)
                flag = pe.value_load(many[P - 1:P, 0:1], min_val=0, max_val=T)
                with pe.If(flag > LIMIT):
                    pe.wait_ge(hg_lo[l], 1)
                    pe.wait_ge(hg_hi[l], 1)

                    def all_tokens(i, odd, nth):
                        for e in range(2):
                            pe.wait_ge(gb_made[l], i * 2 + e + 1)
                            for t, (t0, n) in enumerate(TILES):
                                last = mm(PB[7][:, t0:t0 + n], gb[0:n, t, :], ident[0:n, 0:n], start=True, stop=True)
                            last.then_inc(gcol_out[l], 1)
                            gate, up, down = weights_of(i, odd, nth)
                            for first, name, fill in (gate, up, down):
                                arrived(pe, name, first + e, fill)
                            for f in range(FT):
                                c = e * FT + f
                                wait_for(pe, hD_made[l], i * (2 * FT) + (c - 1 if c >= 2 else 0))
                                for base, bank in ((gate[0], PB[f % 2]), (up[0], PB[2 + f % 2])):
                                    for k in range(KT):
                                        last = mm(bank[:, 0:T], slot(base + e, KT)[:, k, f * P:(f + 1) * P], hT[:, k, :],
                                                  start=(k == 0), stop=(k == KT - 1))
                                    if e == 1 and f == FT - 1 and base == gate[0]:
                                        last.then_inc(gate_out[l], 1)
                                last.then_inc(gD_out[l], 1)
                            pe.wait_ge(hD_made[l], i * (2 * FT) + (e + 1) * FT)
                            for j in range(KT):
                                c = e * KT + j
                                wait_for(pe, yD_added[l], i * (2 * KT) + (c - 1 if c >= 2 else 0))
                                for f in range(FT):
                                    last = mm(PB[4 + j % 2][:, 0:T], slot(down[0] + e, FT)[:, f, j:D:KT], heD[:, f, :],
                                              start=(f == 0), stop=(f == FT - 1))
                                last.then_inc(yD_out[l], 1)
                        pe.wait_ge(yD_out[l], i * (2 * KT) + 2 * KT)
                        pe.sem_inc(up_out[l], 1)
                        pe.sem_inc(down_out[l], 1)
                    all_tokens(0, False, None)
                    with pe.Fori(0, NPAIR // 2 - 1) as j:
                        all_tokens(2 * j + 1, True, j + 1)
                        all_tokens(2 * j + 2, False, j + 1)
                    all_tokens(NPAIR - 1, True, NPAIR // 2)
                    if l == 0:
                        for k in range(KT):
                            sum_square(2, sqB, k)
                    else:
                        for k in range(KT):
                            turn_y(k)
                with pe.Else():
                    def scatter(i):
                        pe.wait_ge(dr_lo[l], i + 1)
                        pe.wait_ge(dr_hi[l], i + 1)
                        pe.wait_ge(sT_made[l], i + 1)
                        for j in range(KT):
                            if isinstance(i, int) and i == NPAIR - 1:
                                if j >= 2:
                                    pe.wait_ge(moe_done, l * KT + j - 1)
                            elif j >= 4:
                                pe.wait_ge(y_added[l], i * KT + j - 3)
                            last = mm(y_bank(i, j)[:, 0:T], dr[:, j:D:KT], sT, start=True, stop=True)
                            last.then_inc(y_out[l], 1)
                            if l == 0 and isinstance(i, int) and i == NPAIR - 1 and j >= 2:
                                sum_square(2, sqB, j - 2)
                            if l == 1 and isinstance(i, int) and i == NPAIR - 1 and j >= 2:
                                turn_y(j - 2)

                    def pair(i, odd, nth):
                        first, last_pair = (isinstance(i, int) and i == n for n in (0, NPAIR - 1))
                        pe.wait_ge(hg_lo[l], i + 1)
                        pe.wait_ge(hg_hi[l], i + 1)
                        gate, up, down = weights_of(i, odd, nth)
                        for (base, name, fill), bank, out in ((gate, PB[2], gate_out), (up, PB[3], up_out)):
                            for e in range(2):
                                arrived(pe, name, base + e, fill)
                            if not first:
                                pe.wait_ge(he_made[l], i)
                            for k in range(KT):
                                for e in range(2):
                                    last = mm(bank[64 * e:64 * e + 64, :], hg[:, k, CAP * e:CAP * (e + 1)],
                                              slot(base + e, KT)[:, k, :], start=(k == 0), stop=(k == KT - 1))
                            last.then_inc(out[l], 1)
                        if not first:
                            scatter(i - 1)
                        pe.wait_ge(he_made[l], i + 1)
                        if not first:
                            pe.wait_ge(y_added[l], i * KT - 3)
                        for f in range(FT):
                            last = tr(PB[6][:, f * P:(f + 1) * P], he[:, f * P:(f + 1) * P], ident)
                        last.then_inc(heT_out[l], 1)
                        if not first:
                            pe.wait_ge(y_added[l], i * KT)
                        if not last_pair:
                            gather(i + 1)
                        pe.wait_ge(ghot_made[l], i + 1)
                        for t, (t0, n) in enumerate(TILES):
                            last = tr(PB[7][:, t0:t0 + n], ghot[0:n, t, :, :].rearrange("p e s -> p (e s)"), ident[0:n, 0:n])
                        last.then_inc(sT_out[l], 1)
                        for e in range(2):
                            arrived(pe, down[1], down[0] + e, down[2])
                        pe.wait_ge(heT_made[l], i + 1)
                        if not first:
                            pe.wait_ge(dr_lo[l], i)
                            pe.wait_ge(dr_hi[l], i)
                        for f in range(FT):
                            for half in range(2):
                                for e in range(2):
                                    last = mm(PB[4 + half][64 * e:64 * e + 64, :], heT[:, f, CAP * e:CAP * (e + 1)],
                                              slot(down[0] + e, FT)[:, f, 512 * half:512 * (half + 1)],
                                              start=(f == 0), stop=(f == FT - 1))
                        last.then_inc(down_out[l], 1)
                    pair(0, False, None)
                    with pe.Fori(0, NPAIR // 2 - 1) as j:
                        pair(2 * j + 1, True, j + 1)
                        pair(2 * j + 2, False, j + 1)
                    pair(NPAIR - 1, True, NPAIR // 2)
                    scatter(NPAIR - 1)
                    if l == 0:
                        sum_square(2, sqB, KT - 2)
                        sum_square(2, sqB, KT - 1)
                    else:
                        turn_y(KT - 2)
                        turn_y(KT - 1)
                pe.nop()

            moe(0, KT)

            def rows(g, src):
                if g % 4 == 0 and g:
                    pe.wait_ge(rows_kept, 3 * (g // 4))
                for t, (t0, n) in enumerate(TILES):
                    last = tr(PB[4 + t][0:n, (g % 4) * P:(g % 4 + 1) * P], src[:, t0:t0 + n], ident)
                if g % 4 == 3:
                    last.then_inc(rows_out, 1)
            def project_v(h):
                if h >= 2:
                    pe.wait_ge(vp_kept, 2 * (h - 1))
                else:
                    pe.wait_ge(kq_normed, 2 * H - 2 + h)
                for k in range(KT):
                    if h == 0 and k % 4 == 0:
                        arrived(pe, "w_v", W_V + k // 4)
                    last = mm(v_acc(h)[:, 0:T], slot(W_V + k // 4, 4)[:, k % 4, h * HD:(h + 1) * HD], hk[:, k, :],
                              start=(k == 0), stop=(k == KT - 1))
                last.then_inc(vp_out, 1)

            for g in range(2 * H + 3):
                if g < 2 * H:
                    if g >= 3:
                        pe.wait_ge(kq_normed, g - 2)
                    for k in range(KT):
                        if g % H == 0:
                            pe.wait_ge(h_made, (3 if g else 2) * KT + k + 1)
                        if g < H:
                            if g == 0 and k % 4 == 0:
                                arrived(pe, "w_k", W_K + k // 4)
                            w, h = slot(W_K + k // 4, 4)[:, k % 4, g * HD:(g + 1) * HD], hk
                        else:
                            if g == H and k % 4 == 0:
                                arrived(pe, "w_q", W_Q + k // 4)
                            w, h = slot(W_Q + k // 4, 4)[:, k % 4, (g - H) * HD:(g - H + 1) * HD], hq
                        last = mm(acc(g)[:, 0:T], w, h[:, k, :], start=(k == 0), stop=(k == KT - 1))
                    last.then_inc(kq_out, 1)
                if 1 <= g <= 2 * H:
                    pe.wait_ge(kq_sq, g)
                    if g >= 2:
                        pe.wait_ge(kq_rms, g - 1)
                    mm(PB[2][:, 0:T], ones, sqh[:, (g - 1) % 2, :], start=True, stop=True).then_inc(kq_ss, 1)
                if g == 2 * H:
                    project_v(0)
                if 2 <= g < 2 * H + 2:
                    pe.wait_ge(kq_normed, g - 1)
                    if g >= 3:
                        pe.wait_ge(kq_made, g - 2)
                    mm(PB[3][0:ROT, 0:T], const("rot"), kq[:, g - 2, :], start=True, stop=True).then_inc(kq_rot, 1)
                if g in ROWS_AT:
                    r = ROWS_AT.index(g)
                    pe.wait_ge(kq_made, r + 1)
                    rows(r, kq[:, r, :])
            project_v(1)
            pe.wait_ge(kq_normed, 2 * H)
            pe.wait_ge(rows_kept, 6)

            def queries(s, half):
                for h in range(4):
                    last = mm(PB[6 + half][:, h * P:(h + 1) * P],
                              bc(kq[:, H + 4 * half + h, NP_TOK + s:NP_TOK + s + 1], [P, P]), ident, start=True, stop=True)
                last.then_inc(qb_out, 1)

            def turn_v_head(h):
                pe.wait_ge(vp_kept, 2 * h + 1)
                if h:
                    pe.wait_ge(v_rows_kept, 2 * h)
                for t, (t0, n) in enumerate(TILES):
                    last = tr(PB[2][0:n, t * P:(t + 1) * P], vTh[:, h % 2, t0:t0 + n], ident)
                last.then_inc(v_rows_out, 1)

            def prompt_logits(h):
                if h == 0:
                    pe.wait_ge(vp_kept, 2 * H)
                else:
                    pe.wait_ge(ps_max, h)
                mm(PB[0][:, 0:P], kq[:, H + h, 0:P], kq[:, h, 0:P], start=True, stop=True)
                mm(PB[0][:, P:3 * P], kq[:, H + h, P:2 * P], kq[:, h, 0:2 * P], start=True, stop=True).then_inc(ps_out, 1)

            def prompt_turn(h):
                pe.wait_ge(ps_norm, h + 1)
                if h:
                    pe.wait_ge(pT_made, h)
                for b in range(3):
                    last = tr(PB[1][:, b * P:(b + 1) * P], p3[:, b * P:(b + 1) * P], ident)
                last.then_inc(pT_out, 1)

            def prompt_values(h):
                pe.wait_ge(pT_made, h + 1)
                if h:
                    pe.wait_ge(po_kept, h)
                else:
                    pe.wait_ge(v_rows_kept, 2 * H)
                mm(PB[2][:, 0:2 * P], vrows[:, 0, h * HD:(h + 1) * HD], pT3[:, 0:2 * P], start=True, stop=False)
                mm(PB[2][:, P:2 * P], vrows[:, 1, h * HD:(h + 1) * HD], pT3[:, 2 * P:3 * P], start=False, stop=True)\
                    .then_inc(po_out, 1)

            def open_step(s):
                if s >= 1:
                    pe.wait_ge(s_made, 2 * s)
                    if s >= 2:
                        pe.wait_ge(att_made, s - 1)
                    else:
                        pe.wait_ge(own_made, 1)
                    mm(PB[3][:, 64:128], ones, sc[:, (s - 1) % 2, 0:NPAGE, :].rearrange("p g h -> p (g h)"),
                       start=True, stop=True).then_inc(gs_out, 1)
                if s < NS:
                    queries(s, 1)

            def next_queries(s):
                if s + 1 < NS:
                    pe.wait_ge(s_made, 2 * s + 1)
                    queries(s + 1, 0)

            pe.wait_ge(kq_made, 2 * H)
            queries(0, 0)
            open_step(0)
            pe.wait_ge(own_in, 1)
            mm(PB[3][:, 0:H * NS], ones, ownp.rearrange("p h s -> p (h s)"), start=True, stop=True).then_inc(own_out, 1)

            for s in range(NS + 1):
                c = (s - 1) % 2
                prompt = PROMPT_HEADS[s]
                if prompt:
                    prompt_logits(prompt[0])
                if s >= 1:
                    pe.wait_ge(pm_made, s)
                    tr(PB[5][0:H, 128:256], pmx, ident).then_inc(pm_turned, 1)
                    pe.wait_ge(dg_made, s)
                    mm(PB[3][:, 256:264], ones[0:H, :], dg[0:H, :], start=True, stop=True).then_inc(mb_out, 1)
                if prompt:
                    prompt_turn(prompt[0])
                for h in prompt[1:]:
                    prompt_logits(h)
                if s >= 1:
                    pe.wait_ge(rs_made, s)
                    mm(PB[5][:, 264:272], ones, rsum, start=True, stop=True).then_inc(den_out, 1)
                    v_slot = V_SLOT[s - 1]
                    if s >= 2:
                        pe.wait_ge(ov_made, s - 1)
                    for g in range(NPAGE):
                        if g % 4 == 0:
                            arrived(pe, f"V{s - 1}", v_slot + g // 4, each=64)
                        for half in range(2):
                            q = 2 * (g % 2) + half
                            last = mm(PB[4][32 * q:32 * q + 32, :], pe4[:, c, g, :],
                                      W[:, v_slot + g // 4, (g % 4) * D + 512 * half:(g % 4) * D + 512 * (half + 1)],
                                      start=(g < 2), stop=(g >= NPAGE - 2), tile_position=(0, 32 * q))
                    last.then_inc(pv_out, 1)
                if prompt:
                    prompt_values(prompt[0])
                if s >= 1:
                    pe.wait_ge(ov_made, s)
                    for b in range(4):
                        last = mm(PB[3][:, 272 + b:272 + b + 5:4], ov[:, b * P:(b + 1) * P],
                                  const("pick").rearrange("p (b n) -> p b n", n=2)[:, b, :], start=True, stop=True)
                    last.then_inc(o_out, 1)
                for h in V_HEADS[s]:
                    if h >= 2:
                        project_v(h)
                    if h:
                        turn_v_head(h - 1)
                    if h == 3:
                        next_queries(s)
                    elif h == 5:
                        open_step(s + 1)
                    elif h == H - 1:
                        turn_v_head(h)
                if not V_HEADS[s]:
                    next_queries(s)
                for h in prompt[1:]:
                    prompt_turn(h)
                    prompt_values(h)
                if not V_HEADS[s] and s < NS:
                    open_step(s + 1)
            pe.wait_ge(att_made, NS + 1)
            pe.wait_ge(po_kept, H)
            for j in range(KT):
                if j >= 2:
                    pe.wait_ge(wo_added, j - 1)
                for h in range(H):
                    if j == 0 and h % 4 == 0:
                        arrived(pe, "w_o", W_O + h // 4)
                    last = mm(PB[j % 2][:, 0:T], slot(W_O + h // 4, 4)[:, h % 4, j:D:KT], aT[:, h, :],
                              start=(h == 0), stop=(h == H - 1))
                last.then_inc(wo_out, 1)
                if j >= 2:
                    sum_and_route(1, sqM, j - 2)
            sum_and_route(1, sqM, KT - 2)
            sum_and_route(1, sqM, KT - 1)
            moe(1, 4 * KT)

        @block.vector
        def _(dve):
            v = nc.vector
            steps = Chain(dve, vec)
            link, ran, settle = steps.link, steps.ran, steps.wait

            v.memset(eps[:, :], EPS).then_inc(eps_set, 1)
            link(v.memset(mv, 1.0))
            for k in range(KT):
                dve.wait_ge(x_turned, k + 1)
                v.tensor_copy(xT[:, k, :], PB[k % 2][:, 0:T]).then_inc(x_kept, 1)
            dve.wait_ge(ga_load, 16)

            def normed(n, targets):
                dve.wait_ge(rms_made, n + 1)
                v.reciprocal(rstd[:, :], rms[:, :]).then_inc(rstd_made, 1)
                dve.wait_ge(rstd_made, n + 1)
                for dst, g in targets:
                    for k in range(KT):
                        v.scalar_tensor_tensor(out=dst[:, k, :], in0=xT[:, k, :], scalar=gains[:, g, k:k + 1],
                                               in1=rstd[:, :], op0=ALU.mult, op1=ALU.mult).then_inc(h_made, 1)
            dve.wait_ge(x_kept, KT)
            normed(0, [(hT, G_A)])

            def keep_mixing():
                for half, bank in ((0, PB[3]), (1, PB[7])):
                    dve.wait_ge(ws_turned, half + 1)
                    v.tensor_copy(wsT[:, 4 * half:4 * half + 4, :], bank[:, :].rearrange("p (g t) -> p g t", g=4))\
                        .then_inc(ws_kept, 1)
                dve.wait_ge(ws_turned, 3)
                link(v.tensor_copy(w00[0:NS], PB[2][0:NS, 0:NG]))
                v.tensor_tensor(d8[0:NS], bc(ident[0:NS, 0:NS].unsqueeze(1), [NS, NG, NS]),
                                bc(w00[0:NS].unsqueeze(2), [NS, NG, NS]), ALU.mult).then_inc(ws_kept, 1)
                dve.wait_ge(g_load, 16 * SMALL_LOADS)
            for b in range(4):
                dve.wait_ge(v_turned, b + 1)
                for t, (_, n) in enumerate(TILES):
                    v.tensor_copy(vr[0:n, t, 512 * b:512 * (b + 1)], PB[4 + t][0:n, :]).then_inc(v_kept, 1)
                    v.bn_stats(stats[0:n, t, 6 * b:6 * b + 6], PB[4 + t][0:n, :]).then_inc(v_kept, 1)
                if b == 1:
                    keep_mixing()
            dve.wait_ge(v_kept, 24)
            for t, (_, n) in enumerate(TILES):
                ran(v.bn_aggr(mv[0:n, t, :], stats[0:n, t, :]))
            settle()
            v.sem_inc(mv_made, 1)
            dve.wait_ge(vsd_made, 1)
            link(v.reciprocal(vrstd, vrstd))
            def norm_v(b):
                dve.wait_ge(ln_load, 32 * (b + 1))
                for t, (_, n) in enumerate(TILES):
                    part = vr[0:n, t, 512 * b:512 * (b + 1)]
                    ran(v.tensor_scalar(part, part, mv[0:n, t, 0:1], vrstd[0:n, t:t + 1], ALU.subtract, ALU.mult))
                settle()
                for i, op in ((0, ALU.mult), (1, ALU.add)):
                    for t, (_, n) in enumerate(TILES):
                        part = vr[0:n, t, 512 * b:512 * (b + 1)]
                        ran(v.tensor_tensor(part, part, lng[0:n, i, :], op))
                    settle()
                v.sem_inc(ln_used, 1)

            def gate_group(g):
                u = vT[:, 2 * g:2 * g + 2, :]
                dve.wait_ge(mix_out, g + 1)
                ran(v.tensor_tensor(mixed[:, :, 0:NP_TOK].rearrange("p i (t s) -> p i t s", t=2),
                                    PB[4 + g % 2][:, :].rearrange("p (i t s) -> p i t s", i=2, t=2),
                                    bc(bs[:, g:g + 1, :].unsqueeze(1), [P, 2, 2, P]), ALU.add))
                link(v.tensor_scalar(mixed[:, :, NP_TOK:T], PB[6 + g % 2][:, 0:2 * NS].rearrange("p (i s) -> p i s", i=2),
                                     bs[:, g, 0:1], None, ALU.add))
                dve.wait_ge(u_gelu, 2 * g + 2)
                v.tensor_tensor(u, u, mixed[:, :, :], ALU.mult).then_inc(um_made, 2)
                dve.wait_ge(um_made, 2 * g + 2)
            norm_v(0)
            for b in range(1, 4):
                norm_v(b)
                gate_group(2 * b - 2)
                gate_group(2 * b - 1)
            gate_group(6)
            gate_group(7)
            for j in range(KT):
                dve.wait_ge(a_out, j + 1)
                v.tensor_tensor(xT[:, j, :], xT[:, j, :], PB[j % 2][:, 0:T], ALU.add).then_inc(a_added, 1)
            dve.wait_ge(a_added, KT)

            def moe(l):
                dve.wait_ge(lgT_out, l + 1)
                v.tensor_tensor(lgT[0:NGRP + NE, :], PB[3][0:NGRP + NE, 0:T], rstd[0:NGRP + NE, :], ALU.mult)\
                    .then_inc(lgT_made, 1)
                link(v.memset(lg, 0.0))
                dve.wait_ge(lg_out, l + 1)
                bias = rbias[:, l, :]
                ran(v.tensor_tensor(lg[:, 0:2, :], PB[2][:, 0:40].rearrange("p (t n) -> p t n", t=2),
                                    bc(bias.unsqueeze(1), [P, 2, NGRP + NE]), ALU.add))
                link(v.tensor_tensor(lg[0:NS, 2, :], PB[2][0:NS, 40:60], bias[0:NS], ALU.add))
                lgg = lg[:, :, 0:NGRP]
                s34 = [P, 3, 4]
                firsts = bc(const("first").unsqueeze(1), s34)

                def wide(x):
                    return bc(x.unsqueeze(2), s34)

                def argmax(x, top, onehot):
                    link(v.tensor_reduce(top, x, AX.X, ALU.max))
                    link(v.tensor_tensor(cand, x, wide(top), ALU.is_equal))
                    link(v.tensor_tensor(cand, cand, firsts, ALU.mult))
                    link(v.tensor_reduce(mn, cand, AX.X, ALU.min))
                    link(v.tensor_tensor(onehot, cand, wide(mn), ALU.is_equal))
                argmax(lgg, gm, ohg)
                link(v.tensor_tensor(ex, lgg, wide(gm), ALU.subtract))
                v.sem_inc(soft_in, 1)
                link(v.tensor_tensor(prod.rearrange("p t (j g) -> p t j g", g=4),
                                     lg[:, :, NGRP:].rearrange("p t (g j) -> p t j g", g=4),
                                     bc(ohg.unsqueeze(2), [P, 3, 4, 4]), ALU.mult))
                link(v.tensor_reduce(leg, prod.rearrange("p t (j g) -> p t j g", g=4), AX.X, ALU.add))
                argmax(leg, m1, oh1)
                link(v.scalar_tensor_tensor(out=le2, in0=oh1, scalar=-3e38, in1=leg, op0=ALU.mult, op1=ALU.add))
                argmax(le2, m2, oh2)
                link(v.tensor_tensor(e2, m2, m1, ALU.subtract))
                v.sem_inc(soft_in, 1)
                link(v.tensor_tensor(cand, oh1, oh2, ALU.add))
                g44 = [P, 3, 4, 4]
                link(v.tensor_tensor(chose.rearrange("p t (g j) -> p t g j", g=4), bc(ohg.unsqueeze(3), g44),
                                     bc(cand.unsqueeze(2), g44), ALU.mult))
                v.tensor_tensor(chose, chose, bc(const("valid").unsqueeze(2), [P, 3, 16]), ALU.mult)\
                    .then_inc(chose_made, 1)
                dve.wait_ge(chose_made, l + 1)
                dve.wait_ge(rank_out, l + 1)
                counted = PB[3][:, 0:3 * NE].rearrange("p (t e) -> p t e", t=3)
                v.tensor_reduce(many[:, :], counted[:, 2, :], AX.X, ALU.max).then_inc(many_set, 1)
                link(v.scalar_tensor_tensor(out=rank, in0=counted, scalar=1.0, in1=chose, op0=ALU.add, op1=ALU.mult))
                link(v.tensor_scalar(rank, rank, -1.0, None, ALU.add))

                def onehot(i):
                    v.tensor_tensor(hot, bc(const("iota").unsqueeze(1).unsqueeze(1), [P, 3, 2, CAP]),
                                    bc(rank[:, :, bass.ds(2 * i, 2)].unsqueeze(3), [P, 3, 2, CAP]), ALU.is_equal)\
                        .then_inc(hot_made[l], 1)

                def copy_hg(i):
                    dve.wait_ge(gather_out[l], i + 1)
                    v.tensor_copy(hg[:, 4:8, :], PB[1][:, :].rearrange("p (k s) -> p k s", k=4)).then_inc(hg_hi[l], 1)
                onehot(0)
                dve.wait_ge(soft_out, 2 * l + 2)
                link(v.tensor_reduce(pg, ex, AX.X, ALU.add))
                link(v.reciprocal(pg, pg))
                link(v.tensor_scalar(w1, e2, 1.0, None, ALU.add))
                link(v.reciprocal(w1, w1))
                link(v.tensor_tensor(w1, w1, pg, ALU.mult))
                link(v.tensor_tensor(w2, e2, w1, ALU.mult))
                link(v.tensor_tensor(oh1, oh1, wide(w1), ALU.mult))
                link(v.tensor_tensor(oh2, oh2, wide(w2), ALU.mult))
                link(v.tensor_tensor(oh1, oh1, oh2, ALU.add))
                link(v.tensor_tensor(gates.rearrange("p t (g j) -> p t g j", g=4), bc(ohg.unsqueeze(3), g44),
                                     bc(oh1.unsqueeze(2), g44), ALU.mult))
                v.sem_inc(gates_made, 1)
                copy_hg(0)
                dve.wait_ge(many_set, l + 1)
                flag = dve.value_load(many[P - 1:P, 0:1], min_val=0, max_val=T)
                with dve.If(flag > LIMIT):
                    own_steps = Chain(dve, vecD[l])
                    def all_tokens(i):
                        own_steps.base, own_steps.n = i * (2 * FT), 0
                        for e in range(2):
                            wait_for(dve, gcol_out[l], i * 2 + e)
                            v.tensor_copy(gb, bc(gates[:, :, bass.ds(2 * i + e, 1)], [P, 3, P])).then_inc(gb_made[l], 1)
                            dve.wait_ge(gcol_out[l], i * 2 + e + 1)
                            wait_for(dve, hD_made[l], i * (2 * FT) + e * FT)
                            v.tensor_copy(gcol, PB[7][:, 0:T]).then_inc(gcol_made[l], 1)
                            dve.wait_ge(gcol_made[l], i * 2 + e + 1)
                            wait_for(dve, yD_out[l], i * (2 * KT) + e * KT)
                            for f in range(FT):
                                dve.wait_ge(sD_made[l], i * (2 * FT) + e * FT + f + 1)
                                own_steps.link(v.tensor_tensor(heD[:, f, :], sgD, PB[2 + f % 2][:, 0:T], ALU.mult))
                                v.tensor_tensor(heD[:, f, :], heD[:, f, :], gcol, ALU.mult).then_inc(hD_made[l], 1)
                            for j in range(KT):
                                dve.wait_ge(yD_out[l], i * (2 * KT) + e * KT + j + 1)
                                wait_for(dve, yD_added[l], i * (2 * KT) + e * KT + j)
                                v.tensor_tensor(xT[:, j, :], xT[:, j, :], PB[4 + j % 2][:, 0:T], ALU.add)\
                                    .then_inc(yD_added[l], 1)
                    all_tokens(0)
                    with dve.Fori(1, NPAIR) as i:
                        all_tokens(i)
                    dve.wait_ge(yD_added[l], NE * KT)
                    v.sem_inc(moe_done, KT)
                with dve.Else():
                    def add_y(i):
                        for j in range(KT):
                            dve.wait_ge(y_out[l], i * KT + j + 1)
                            v.tensor_tensor(xT[:, j, :], xT[:, j, :], y_bank(i, j)[:, 0:T], ALU.add).then_inc(
                                moe_done if isinstance(i, int) and i == NPAIR - 1 else y_added[l], 1)

                    def pair(i, first, last):
                        dve.wait_ge(silu_made[l], i + 1)
                        dve.wait_ge(up_out[l], i + 1)
                        v.tensor_tensor(he, sg, PB[3][:, :], ALU.mult).then_inc(he_made[l], 1)
                        if not first:
                            add_y(i - 1)
                        if not last:
                            copy_hg(i + 1)
                        dve.wait_ge(sT_out[l], i + 1)
                        v.tensor_copy(sT, PB[7][:, 0:T]).then_inc(sT_made[l], 1)
                        if not last:
                            if not isinstance(i, int) or i < NPAIR - 2:
                                dve.wait_ge(ghot_made[l], i + 2)
                                onehot(i + 2)
                        dve.wait_ge(down_out[l], i + 1)
                        v.tensor_copy(dr[:, 512:D], PB[5][:, :]).then_inc(dr_hi[l], 1)
                    dve.wait_ge(ghot_made[l], 1)
                    onehot(1)
                    pair(0, True, False)
                    with dve.Fori(1, NPAIR - 2) as i:
                        pair(i, False, False)
                    pair(NPAIR - 2, False, False)
                    pair(NPAIR - 1, False, True)
                    add_y(NPAIR - 1)
                dve.nop()

            normed(1, [])
            moe(0)
            dve.wait_ge(moe_done, KT)
            normed(2, [(hk, G_KV)])

            for g in range(2 * H + 2):
                if g < 2 * H:
                    dve.wait_ge(kq_rms, g + 1)
                    link(v.reciprocal(rsh, rmh))
                    v.scalar_tensor_tensor(out=kq[:, g, :], in0=acc(g)[:, 0:T], scalar=hgain[:, g // H:g // H + 1],
                                           in1=rsh, op0=ALU.mult, op1=ALU.mult).then_inc(kq_normed, 1)
                    dve.wait_ge(kq_normed, g + 1)
                if g < KT // 2:
                    for k in (2 * g, 2 * g + 1):
                        v.scalar_tensor_tensor(out=hq[:, k, :], in0=xT[:, k, :], scalar=gains[:, G_B, k:k + 1],
                                               in1=rstd[:, :], op0=ALU.mult, op1=ALU.mult).then_inc(h_made, 1)
                if g >= 1 and g <= 2 * H:
                    dve.wait_ge(kq_rot, g)
                    rot = kq[0:ROT, g - 1, :]
                    ran(v.tensor_tensor(turned[0:ROT, :], PB[3][0:ROT, 0:T], const("sin")[0:ROT, :], ALU.mult))
                    link(v.tensor_tensor(rot, rot, const("cos")[0:ROT, :], ALU.mult))
                    v.tensor_tensor(rot, rot, turned[0:ROT, :], ALU.add).then_inc(kq_made, 1)
                    dve.wait_ge(kq_made, g)
            v.tensor_tensor(ownp, kq[:, 0:H, NP_TOK:T], kq[:, H:2 * H, NP_TOK:T], ALU.mult).then_inc(own_in, 1)
            dve.wait_ge(own_out, 1)
            v.tensor_copy(own.rearrange("p h s -> p (h s)"), PB[3][:, 0:H * NS]).then_inc(own_made, 1)
            dve.wait_ge(own_made, 1)
            dve.wait_ge(pad_set, 1)

            def keys(s, half, g):
                c = s % 2
                k_slot = K_SLOT[s] + g // 4
                if g == 0:
                    dve.wait_ge(qb_out, 2 * s + half + 1)
                if g % 4 == 0 and half == 0:
                    arrived(dve, f"K{s}", k_slot, each=64)
                for i in range(4):
                    h = 4 * half + i
                    kb = W[:, k_slot, (g % 4) * D + h * HD:(g % 4) * D + (h + 1) * HD]
                    last = v.tensor_tensor_reduce(kb, kb, PB[6 + half][:, i * P:(i + 1) * P], 1.0, 0.0,
                                                  ALU.mult, ALU.add, sc[:, c, g, h:h + 1])
                if g == NPAGE - 1:
                    last.then_inc(s_made, 1)

            for s in range(NS + 1):
                c = (s - 1) % 2
                scp = sc[:, c, 0:NPAGE, :]

                def prompt_max(h):
                    dve.wait_ge(ps_out, h + 1)
                    if h:
                        dve.wait_ge(ps_exp, 2 * h)
                    link(v.tensor_tensor(s3, PB[0][:, 0:3 * P], const("causal"), ALU.add))
                    ran(v.tensor_reduce(mx3[:, 0:1], s3[:, 0:P], AX.X, ALU.max))
                    link(v.tensor_reduce(mx3[:, 1:2], s3[:, P:3 * P], AX.X, ALU.max))
                    if h:
                        dve.wait_ge(pT_out, h)
                    v.tensor_scalar(mx3, mx3, -SCALE, None, ALU.mult).then_inc(ps_max, 1)

                def blocks():
                    dve.wait_ge(gs_out, s)
                    link(v.tensor_reduce(gsum, PB[3][:, 64:128].rearrange("p (b g h) -> p b h g", b=NBLK, g=2),
                                         AX.X, ALU.add))
                    link(v.tensor_reduce(mnb, gsum.rearrange("p b h -> p h b"), AX.X, ALU.min))
                    link(v.tensor_tensor(eqb, gsum, bc(mnb.unsqueeze(1), [P, NBLK, H]), ALU.is_equal))
                    link(v.tensor_tensor(eqb, eqb, bc(const("blk").unsqueeze(2), [P, NBLK, H]), ALU.mult))
                    link(v.tensor_reduce(vmb, eqb.rearrange("p b h -> p h b"), AX.X, ALU.max))
                    link(v.tensor_tensor(drop, eqb, bc(vmb.unsqueeze(1), [P, NBLK, H]), ALU.is_equal))
                    for g in range(2):
                        half = scp.rearrange("p (b g) h -> p b g h", g=2)[:, :, g, :]
                        ran(v.scalar_tensor_tensor(out=half, in0=drop, scalar=NEG, in1=half, op0=ALU.mult, op1=ALU.add))
                    settle()
                    v.tensor_reduce(pmx, scp.rearrange("p g h -> p h g"), AX.X, ALU.max).then_inc(pm_made, 1)

                def maxima():
                    dve.wait_ge(pm_turned, s)
                    link(v.tensor_reduce(hm[0:H, :], PB[5][0:H, 128:256], AX.X, ALU.max))
                    v.tensor_scalar(dg[0:H, :], ident[0:H, 0:H], hm[0:H, 0:1], None, ALU.mult).then_inc(dg_made, 1)

                def shift():
                    dve.wait_ge(mb_out, s)
                    mine = own[:, :, s - 1]
                    link(v.tensor_tensor(mall, PB[3][:, 256:264], mine, ALU.max))
                    ran(v.tensor_tensor(sc[:, c, NPAGE, :], mine, mall, ALU.subtract))
                    ran(v.tensor_tensor(scp, scp, bc(mall.unsqueeze(1), [P, NPAGE, H]), ALU.subtract))
                    settle()
                    v.sem_inc(sc_made, 1)

                def prompt_norm(h):
                    dve.wait_ge(ps_exp, 2 * (h + 1))
                    link(v.reciprocal(ri3, rs3))
                    ran(v.tensor_scalar(p3[:, 0:P], p3[:, 0:P], ri3[:, 0:1], None, ALU.mult))
                    ran(v.tensor_scalar(p3[:, P:3 * P], p3[:, P:3 * P], ri3[:, 1:2], None, ALU.mult))
                    settle()
                    v.sem_inc(ps_norm, 1)

                def row_sums():
                    dve.wait_ge(se_made, s)
                    v.tensor_reduce(rsum, pe4[:, c, 0:NPAGE, 0:H].rearrange("p g h -> p h g"), AX.X, ALU.add)\
                        .then_inc(rs_made, 1)

                def denominators():
                    dve.wait_ge(den_out, s)
                    link(v.tensor_tensor(den, PB[5][:, 264:272], pe4[:, c, NPAGE, 0:H], ALU.add))
                    link(v.reciprocal(rden, den))
                    v.tensor_tensor(own_w[:, :, s - 1], rden, pe4[:, c, NPAGE, 0:H], ALU.mult).then_inc(vec_own, 1)

                def result():
                    dve.wait_ge(o_out, s)
                    v.tensor_tensor(aT[:, :, NP_TOK + s - 1], rden, PB[3][:, 272:280], ALU.mult).then_inc(att_made, 1)

                after = {(0, 0): blocks, (0, 2): maxima, (0, 4): shift, (0, 6): row_sums, (1, 0): denominators,
                         (1, 6): result}
                prompt_after = {(0, 1): (prompt_max, 0), (0, 5): (prompt_norm, 0),
                                (1, 2): (prompt_max, 1), (1, 5): (prompt_norm, 1)}
                for half in range(2):
                    for g in range(NPAGE):
                        if s < NS:
                            keys(s, half, g)
                        if s >= 1 and (half, g) in after:
                            after[half, g]()
                        if (half, g) in prompt_after:
                            part, nth = prompt_after[half, g]
                            for h in PROMPT_HEADS[s][nth:nth + 1]:
                                part(h)
            dve.wait_ge(att_made, NS)
            dve.wait_ge(vec_own, NS)
            dve.wait_ge(vp_kept, 2 * H)
            link(v.tensor_tensor(own_w, own_w, vTs, ALU.mult))
            v.tensor_tensor(aT[:, :, NP_TOK:T], aT[:, :, NP_TOK:T], own_w, ALU.add).then_inc(att_made, 1)
            for j in range(KT):
                dve.wait_ge(wo_out, j + 1)
                v.tensor_tensor(xT[:, j, :], xT[:, j, :], PB[j % 2][:, 0:T], ALU.add).then_inc(wo_added, 1)
            dve.wait_ge(wo_added, KT)
            normed(3, [])
            moe(1)
            dve.wait_ge(y_turned, 1)
            for t, (_, n) in enumerate(TILES):
                v.tensor_copy(y_half(t, n, 0), PB[t][0:n, :].rearrange("q (k p) -> q k p", k=4)).then_inc(yr_made, 1)


_OUTS = [("y_prompt", (1, 256, 1024)), ("y_sample", (8, 1, 1024)), ("v_rows_prompt", (1, 1, 128, 2048)),
         ("v_rows_sample", (1, 8, 1, 2048)), ("k_prompt", (1, 256, 8, 128)), ("v_prompt", (1, 256, 8, 128)),
         ("k_sample", (8, 1, 8, 128)), ("v_sample", (8, 1, 8, 128))]


def kernel(**inputs):
    import numpy as np
    import concourse.bacc as bacc
    from concourse.bass_utils import run_bass_kernel_spmd

    nc = bacc.Bacc("TRN2", target_bir_lowering=False, num_devices=1)
    arrays, a, o = {}, {}, {}
    for name, value in {**inputs, "consts": constants()}.items():
        value = np.ascontiguousarray(value)
        arrays["in_" + name] = value
        a[name] = nc.dram_tensor("in_" + name, value.shape, mybir.dt.from_np(value.dtype), kind="ExternalInput").ap()
    for name, shape in _OUTS:
        o[name] = nc.dram_tensor("out_" + name, shape, F32, kind="ExternalOutput").ap()
    program(nc, a, o)
    r = run_bass_kernel_spmd(nc, [arrays], core_ids=[0])
    return tuple(r.results[0]["out_" + name] for name, _ in _OUTS)
```
